# Optimizing a Trainium2 kernel written in Bass

```python
import jax, jax.numpy as jnp
from jax import lax
import numpy as np

D_MODEL = 1024
BATCH = 1
SEQ = 256
DEPTH = 2

HEAD_DIM = 64
N_BRANCHES = 4
BRANCH_WIDTH = D_MODEL // 4
ROPE_THETA = 500000.0
ROPE_DIM = HEAD_DIM // 4
NORM_EPS = 1e-6
NEG_INF = -1e30
QBLK = 128

NSA_HEADS = BRANCH_WIDTH // HEAD_DIM
NSA_GROUPS = 2
NSA_REP = NSA_HEADS // NSA_GROUPS
NSA_KV = NSA_GROUPS * HEAD_DIM
CMP_LEN = 32
CMP_STRIDE = 16
CMP_HIDDEN = 128
SEL_BLOCK = 64
SEL_TOPN = 8
SEL_QBLK = 32
SEL_FORCE = 1e30
WINDOW = 512

POOL_WINDOWS = (2, 4, 8, 16)
POOL_GROUPS = len(POOL_WINDOWS)
POOL_GROUP_DIM = BRANCH_WIDTH // POOL_GROUPS

RWKV_HEADS = BRANCH_WIDTH // HEAD_DIM
RWKV_DECAY_RANK = 32
RWKV_A_RANK = 32
RWKV_V_RANK = 32
RWKV_G_RANK = 64
RWKV_GN_EPS = 64e-5

GLA_HEADS = 4
GLA_DV = BRANCH_WIDTH // GLA_HEADS
GLA_DK = GLA_DV // 2
GLA_GATE_RANK = 16
GLA_TAU = 16.0
GLA_CHUNK = 16

NSA_IN = NSA_HEADS * HEAD_DIM + 6 * NSA_KV + 3 * NSA_HEADS
POOL_IN = BRANCH_WIDTH
RWKV_IN = 3 * BRANCH_WIDTH + RWKV_DECAY_RANK + RWKV_A_RANK + RWKV_G_RANK
GLA_IN = 2 * GLA_HEADS * GLA_DK + 2 * BRANCH_WIDTH + GLA_GATE_RANK
IN_WIDTH = NSA_IN + POOL_IN + RWKV_IN + GLA_IN

MEM_LEN = 256
CA_HEADS = 4
CA_WIDTH = CA_HEADS * HEAD_DIM

D_FF = 2816
N_EXPERTS = 8
TOP_K = 2
N_DENSE = (DEPTH + 1) // 2
N_MOE = DEPTH // 2

kernel_name = 'hybrid_nsa_pool_rwkv7_gla_moe_block'

def _split(t, sizes):
    return jnp.split(t, np.cumsum(sizes)[:-1].tolist(), axis=-1)

def rms_norm(x, g, eps=NORM_EPS):
    xf = x.astype(jnp.float32)
    y = xf * lax.rsqrt(jnp.mean(xf * xf, axis=-1, keepdims=True) + eps)
    return (y * g.astype(jnp.float32)).astype(x.dtype)

def rope_tables(positions):
    inv_freq = ROPE_THETA ** (-jnp.arange(0, ROPE_DIM, 2, dtype=jnp.float32) / ROPE_DIM)
    ang = positions.astype(jnp.float32)[..., None] * inv_freq
    return jnp.cos(ang), jnp.sin(ang)

def apply_partial_rope(t, cos, sin):
    half = ROPE_DIM // 2
    c = cos[:, :, None, :].astype(t.dtype)
    s = sin[:, :, None, :].astype(t.dtype)
    t1, t2, rest = t[..., :half], t[..., half:ROPE_DIM], t[..., ROPE_DIM:]
    return jnp.concatenate([t1 * c - t2 * s, t2 * c + t1 * s, rest], axis=-1)

def masked_softmax(scores, mask):
    s = jnp.where(mask, scores.astype(jnp.float32), NEG_INF)
    return jnp.where(mask, jax.nn.softmax(s, axis=-1), 0.0)

def nsa_mixer(p, cos, sin, cmp_pe, cmp_w1, cmp_w2):
    B, S, _ = p.shape
    G, R, hd = NSA_GROUPS, NSA_REP, HEAD_DIM
    q, kc, vc, ks, vs, kw, vw, gates = _split(p, (NSA_HEADS * hd,) + (NSA_KV,) * 6 + (3 * NSA_HEADS,))
    q = apply_partial_rope(q.reshape(B, S, NSA_HEADS, hd), cos, sin) * (hd ** -0.5)
    q = q.reshape(B, S, G, R, hd)
    kvs = lambda t: t.reshape(B, S, G, hd)
    t_idx = np.arange(S)

    n_cmp = (S - CMP_LEN) // CMP_STRIDE + 1
    cmp_start = np.arange(n_cmp) * CMP_STRIDE
    cmp_idx = cmp_start[:, None] + np.arange(CMP_LEN)[None, :]
    cmp_end = cmp_start + CMP_LEN - 1

    def compress(t, j):
        blocks = t[:, cmp_idx] + cmp_pe[j][:, None, :]
        hid = jax.nn.gelu(jnp.einsum('bnlgd,ldf->bngf', blocks, cmp_w1[j]))
        return jnp.einsum('bngf,fd->bngd', hid, cmp_w2[j])

    k_cmp = apply_partial_rope(compress(kvs(kc), 0), cos[:, cmp_end], sin[:, cmp_end])
    v_cmp = compress(kvs(vc), 1)
    cmp_mask = cmp_end[None, :] <= t_idx[:, None]
    p_cmp = masked_softmax(jnp.einsum('bsgrd,bngd->bgrsn', q, k_cmp), cmp_mask)
    o_cmp = jnp.einsum('bgrsn,bngd->bsgrd', p_cmp.astype(v_cmp.dtype), v_cmp)

    n_slc = S // SEL_BLOCK
    slc_start = np.arange(n_slc) * SEL_BLOCK
    cover = np.clip(np.minimum(cmp_start[:, None] + CMP_LEN, slc_start[None, :] + SEL_BLOCK)
                    - np.maximum(cmp_start[:, None], slc_start[None, :]), 0, None) / CMP_LEN
    imp = jnp.einsum('bgrsn,nj->bgsj', p_cmp, jnp.asarray(cover, jnp.float32))
    cur = t_idx[:, None] // SEL_BLOCK
    blk = np.arange(n_slc)[None, :]
    forced = (blk == 0) | (blk == cur) | (blk == cur - 1)
    causal_blk = slc_start[None, :] <= t_idx[:, None]
    imp = jnp.where(forced, SEL_FORCE, jnp.where(causal_blk, imp, -SEL_FORCE))
    n_top = min(SEL_TOPN, n_slc)
    _, sel = lax.top_k(imp, n_top)

    k_sel = apply_partial_rope(kvs(ks), cos, sin).transpose(0, 2, 1, 3)
    v_sel = kvs(vs).transpose(0, 2, 1, 3)
    n_sq = S // SEL_QBLK
    n_keys = n_top * SEL_BLOCK
    gather_rows = jax.vmap(jax.vmap(lambda src, idx: src[idx]))

    def sel_block(args):
        i, qb, sb = args
        tok = (sb[..., None] * SEL_BLOCK + np.arange(SEL_BLOCK)).reshape(B, G, SEL_QBLK * n_keys)
        kg = gather_rows(k_sel, tok).reshape(B, G, SEL_QBLK, n_keys, hd)
        vg = gather_rows(v_sel, tok).reshape(B, G, SEL_QBLK, n_keys, hd)
        qpos = i * SEL_QBLK + jnp.arange(SEL_QBLK)
        mask = tok.reshape(B, G, 1, SEL_QBLK, n_keys) <= qpos[:, None]
        pr = masked_softmax(jnp.einsum('bqgrd,bgqkd->bgrqk', qb, kg), mask)
        return jnp.einsum('bgrqk,bgqkd->bqgrd', pr.astype(vg.dtype), vg)

    q_sb = jnp.moveaxis(q.reshape(B, n_sq, SEL_QBLK, G, R, hd), 1, 0)
    sel_b = jnp.moveaxis(sel.reshape(B, G, n_sq, SEL_QBLK, n_top), 2, 0)
    o_sel = lax.map(sel_block, (jnp.arange(n_sq), q_sb, sel_b))
    o_sel = jnp.moveaxis(o_sel, 0, 1).reshape(B, S, G, R, hd)

    pad = ((0, 0), (WINDOW, 0), (0, 0), (0, 0))
    k_win = jnp.pad(apply_partial_rope(kvs(kw), cos, sin), pad)
    v_win = jnp.pad(kvs(vw), pad)
    span = WINDOW + QBLK
    rel = jnp.arange(span) - WINDOW

    def win_block(args):
        i, qb = args
        start = i * QBLK
        kb = lax.dynamic_slice_in_dim(k_win, start, span, axis=1)
        vb = lax.dynamic_slice_in_dim(v_win, start, span, axis=1)
        qpos = start + jnp.arange(QBLK)
        kpos = start + rel
        dist = qpos[:, None] - kpos[None, :]
        mask = (dist >= 0) & (dist < WINDOW) & (kpos[None, :] >= 0)
        pr = masked_softmax(jnp.einsum('bqgrd,bkgd->bgrqk', qb, kb), mask)
        return jnp.einsum('bgrqk,bkgd->bqgrd', pr.astype(vb.dtype), vb)

    n_wb = S // QBLK
    q_wb = jnp.moveaxis(q.reshape(B, n_wb, QBLK, G, R, hd), 1, 0)
    o_win = jnp.moveaxis(lax.map(win_block, (jnp.arange(n_wb), q_wb)), 0, 1).reshape(B, S, G, R, hd)

    g = jax.nn.sigmoid(gates.reshape(B, S, G, R, 3))
    o = g[..., 0:1] * o_cmp + g[..., 1:2] * o_sel + g[..., 2:3] * o_win
    return o.reshape(B, S, NSA_HEADS * hd)

def pool_mixer(u, w, scale):
    B, S, _ = u.shape
    uf = u.astype(jnp.float32)
    c = jnp.cumsum(uf, axis=1)
    count = jnp.arange(1, S + 1, dtype=jnp.float32)[None, :, None]
    outs = []
    for gi, win in enumerate(POOL_WINDOWS):
        sl = slice(gi * POOL_GROUP_DIM, (gi + 1) * POOL_GROUP_DIM)
        cg = c[..., sl]
        prev = jnp.pad(cg, ((0, 0), (win, 0), (0, 0)))[:, :S]
        outs.append((cg - prev) / jnp.minimum(count, win) - uf[..., sl])
    d = jnp.stack(outs, axis=2).astype(u.dtype)
    y = jnp.einsum('bsgc,gcd->bsgd', d, w).reshape(B, S, BRANCH_WIDTH)
    return y * scale

def token_shift(t):
    return jnp.pad(t, ((0, 0), (1, 0), (0, 0)))[:, :-1]

def rwkv7_mixer(p, mu, w0, w2, a0, a2, g2, k_k, k_a, r_k, ln_g, v_first, v_res_logit):
    B, S, _ = p.shape
    H, hd, W = RWKV_HEADS, HEAD_DIM, BRANCH_WIDTH
    f32 = jnp.float32
    dtype = p.dtype
    p = p.astype(f32)
    p = p + (token_shift(p) - p) * mu
    r, k, v, wd, ad, gd = _split(p, (W, W, W, RWKV_DECAY_RANK, RWKV_A_RANK, RWKV_G_RANK))
    w_log = -jax.nn.softplus(-(w0 + jnp.tanh(wd) @ w2)) - 0.5
    decay = jnp.exp(-jnp.exp(w_log))
    a = jax.nn.sigmoid(a0 + ad @ a2)
    g = jax.nn.sigmoid(gd) @ g2
    if v_first is not None:
        v = v + (v_first - v) * jax.nn.sigmoid(v_res_logit)
    heads = lambda t: t.reshape(B, S, H, hd)
    kk = heads(k * k_k)
    kk = kk / jnp.maximum(jnp.linalg.norm(kk, axis=-1, keepdims=True), 1e-12)
    k = k * (1.0 + (a - 1.0) * k_a)
    b = kk * heads(a)
    xs = tuple(jnp.moveaxis(t, 1, 0) for t in (heads(r), heads(decay), heads(k), heads(v), kk, b))

    def step(state, inp):
        r_t, w_t, k_t, v_t, kk_t, b_t = inp
        s_kk = jnp.einsum('bhvk,bhk->bhv', state, kk_t)
        state = (state * w_t[:, :, None, :] - s_kk[..., None] * b_t[:, :, None, :]
                 + v_t[..., None] * k_t[:, :, None, :])
        return state, jnp.einsum('bhvk,bhk->bhv', state, r_t)

    _, y = lax.scan(step, jnp.zeros((B, H, hd, hd), f32), xs)
    y = jnp.moveaxis(y, 0, 1)
    mean = jnp.mean(y, axis=-1, keepdims=True)
    var = jnp.mean(jnp.square(y - mean), axis=-1, keepdims=True)
    y = (y - mean) * lax.rsqrt(var + RWKV_GN_EPS) * ln_g.reshape(H, hd)
    y = y + jnp.sum(heads(r) * heads(k) * r_k, axis=-1, keepdims=True) * heads(v)
    return (y.reshape(B, S, W) * g).astype(dtype), v

def gla_mixer(p, a2, ab, norm_g):
    B, S, _ = p.shape
    H, dk, dv, C = GLA_HEADS, GLA_DK, GLA_DV, GLA_CHUNK
    f32 = jnp.float32
    dtype = p.dtype
    q, k, v, ad, og = _split(p, (H * dk, H * dk, BRANCH_WIDTH, GLA_GATE_RANK, BRANCH_WIDTH))
    log_a = jax.nn.log_sigmoid((ad @ a2 + ab).astype(f32)) / GLA_TAU
    nc = S // C
    chunks = lambda t, d: t.astype(f32).reshape(B, nc, C, H, d)
    q = chunks(q, dk) * (dk ** -0.5)
    k = chunks(k, dk)
    v = chunks(v, dv)
    bcum = jnp.cumsum(chunks(log_a, dk), axis=2)
    blast = bcum[:, :, -1]
    q_t = q * jnp.exp(bcum)
    k_t = k * jnp.exp(-bcum)
    k_end = k * jnp.exp(blast[:, :, None] - bcum)
    causal = np.tril(np.ones((C, C), dtype=bool))
    att = jnp.where(causal, jnp.einsum('bnthk,bnshk->bnhts', q_t, k_t), 0.0)
    o_intra = jnp.einsum('bnhts,bnshv->bnthv', att, v)

    def step(state, inp):
        kc, vc, dl = inp
        new = state * dl[..., None] + jnp.einsum('bchk,bchv->bhkv', kc, vc)
        return new, state

    xs = (jnp.moveaxis(k_end, 1, 0), jnp.moveaxis(v, 1, 0), jnp.moveaxis(jnp.exp(blast), 1, 0))
    _, s_prev = lax.scan(step, jnp.zeros((B, H, dk, dv), f32), xs)
    o_inter = jnp.einsum('bnthk,nbhkv->bnthv', q_t, s_prev)
    o = (o_intra + o_inter).reshape(B, S, H, dv)
    o = o * lax.rsqrt(jnp.mean(o * o, axis=-1, keepdims=True) + NORM_EPS) * norm_g
    return (o.reshape(B, S, BRANCH_WIDTH) * jax.nn.silu(og.astype(f32))).astype(dtype)

def cross_attention(hc, mem_n, wq, wkv, wo):
    B, S, _ = hc.shape
    M = mem_n.shape[1]
    q = (hc @ wq).reshape(B, S, CA_HEADS, HEAD_DIM) * (HEAD_DIM ** -0.5)
    k, v = _split(mem_n @ wkv, (CA_WIDTH, CA_WIDTH))
    k = k.reshape(B, M, CA_HEADS, HEAD_DIM)
    v = v.reshape(B, M, CA_HEADS, HEAD_DIM)
    pr = jax.nn.softmax(jnp.einsum('bshd,bmhd->bhsm', q, k).astype(jnp.float32), axis=-1)
    o = jnp.einsum('bhsm,bmhd->bshd', pr.astype(v.dtype), v).reshape(B, S, CA_WIDTH)
    return o @ wo

def swiglu(x, wg, wu, wd):
    return (jax.nn.silu(x @ wg) * (x @ wu)) @ wd

def moe_swiglu(x, router, wg, wu, wd):
    logits = (x @ router).astype(jnp.float32)
    top_val, top_idx = lax.top_k(logits, TOP_K)
    weights = jax.nn.softmax(top_val, axis=-1)
    combine = jnp.sum(jax.nn.one_hot(top_idx, N_EXPERTS, dtype=jnp.float32) * weights[..., None], axis=-2)
    out = jnp.zeros_like(x)
    for e in range(N_EXPERTS):
        out = out + combine[..., e:e + 1].astype(x.dtype) * swiglu(x, wg[e], wu[e], wd[e])
    return out

def setup_inputs(seed: int = 0) -> dict:
    key = jax.random.key(seed)
    keys = iter(jax.random.split(key, 64))
    f32 = jnp.float32

    def normal(shape, scale):
        return jax.random.normal(next(keys), shape, f32) * scale

    def gain(shape):
        return 1.0 + normal(shape, 0.05)

    def uniform(shape, lo, hi):
        return jax.random.uniform(next(keys), shape, f32, lo, hi)

    L, D, W = DEPTH, D_MODEL, BRANCH_WIDTH
    x = normal((BATCH, SEQ, D), 1.0)
    mem = normal((BATCH, MEM_LEN, D), 1.0)
    start = jax.random.randint(next(keys), (BATCH, 1), 0, 4096, dtype=jnp.int32)
    positions = start + jnp.arange(SEQ, dtype=jnp.int32)[None, :]
    return {
        'x': x,
        'mem': mem,
        'positions': positions,
        'norm_mix': gain((L, D)),
        'w_in': normal((L, D, IN_WIDTH), D ** -0.5),
        'nsa_cmp_pe': normal((L, 2, CMP_LEN, HEAD_DIM), 0.1),
        'nsa_cmp_w1': normal((L, 2, CMP_LEN, HEAD_DIM, CMP_HIDDEN), (CMP_LEN * HEAD_DIM) ** -0.5),
        'nsa_cmp_w2': normal((L, 2, CMP_HIDDEN, HEAD_DIM), CMP_HIDDEN ** -0.5),
        'pool_w': normal((L, POOL_GROUPS, POOL_GROUP_DIM, POOL_GROUP_DIM), POOL_GROUP_DIM ** -0.5),
        'pool_scale': gain((L, W)),
        'rwkv_mu': uniform((L, RWKV_IN), 0.0, 1.0),
        'rwkv_w0': uniform((L, W), -6.0, 1.0),
        'rwkv_w2': normal((L, RWKV_DECAY_RANK, W), 0.5 * RWKV_DECAY_RANK ** -0.5),
        'rwkv_a0': normal((L, W), 0.1),
        'rwkv_a2': normal((L, RWKV_A_RANK, W), RWKV_A_RANK ** -0.5),
        'rwkv_g2': normal((L, RWKV_G_RANK, W), RWKV_G_RANK ** -0.5),
        'rwkv_v0': normal((L - 1, W), 0.1),
        'rwkv_v1': normal((L - 1, D, RWKV_V_RANK), D ** -0.5),
        'rwkv_v2': normal((L - 1, RWKV_V_RANK, W), RWKV_V_RANK ** -0.5),
        'rwkv_k_k': 0.85 + normal((L, W), 0.05),
        'rwkv_k_a': gain((L, W)),
        'rwkv_r_k': normal((L, RWKV_HEADS, HEAD_DIM), 0.1),
        'rwkv_ln': gain((L, W)),
        'gla_a2': normal((L, GLA_GATE_RANK, GLA_HEADS * GLA_DK), GLA_GATE_RANK ** -0.5),
        'gla_ab': uniform((L, GLA_HEADS * GLA_DK), 0.0, 4.0),
        'gla_norm': gain((L, GLA_DV)),
        'w_gate': normal((L, N_BRANCHES, D, D), D ** -0.5),
        'b_gate': normal((L, N_BRANCHES, D), 0.1),
        'w_branch': normal((L, N_BRANCHES, W, D), W ** -0.5),
        'w_out': normal((L, D, D), D ** -0.5),
        'norm_ca': gain((L, D)),
        'mem_norm': gain((D,)),
        'w_ca_q': normal((L, D, CA_WIDTH), D ** -0.5),
        'w_ca_kv': normal((L, D, 2 * CA_WIDTH), D ** -0.5),
        'w_ca_o': normal((L, CA_WIDTH, D), CA_WIDTH ** -0.5),
        'norm_ffn': gain((L, D)),
        'ffn_w_gate': normal((N_DENSE, D, D_FF), D ** -0.5),
        'ffn_w_up': normal((N_DENSE, D, D_FF), D ** -0.5),
        'ffn_w_down': normal((N_DENSE, D_FF, D), D_FF ** -0.5),
        'moe_router': normal((N_MOE, D, N_EXPERTS), D ** -0.5),
        'moe_w_gate': normal((N_MOE, N_EXPERTS, D, D_FF), D ** -0.5),
        'moe_w_up': normal((N_MOE, N_EXPERTS, D, D_FF), D ** -0.5),
        'moe_w_down': normal((N_MOE, N_EXPERTS, D_FF, D), D_FF ** -0.5),
        'norm_final': gain((D,)),
    }

def reference(x, mem, positions, norm_mix, w_in, nsa_cmp_pe, nsa_cmp_w1, nsa_cmp_w2, pool_w, pool_scale,
              rwkv_mu, rwkv_w0, rwkv_w2, rwkv_a0, rwkv_a2, rwkv_g2, rwkv_v0, rwkv_v1, rwkv_v2,
              rwkv_k_k, rwkv_k_a, rwkv_r_k, rwkv_ln, gla_a2, gla_ab, gla_norm,
              w_gate, b_gate, w_branch, w_out, norm_ca, mem_norm, w_ca_q, w_ca_kv, w_ca_o,
              norm_ffn, ffn_w_gate, ffn_w_up, ffn_w_down,
              moe_router, moe_w_gate, moe_w_up, moe_w_down, norm_final):
    cos, sin = rope_tables(positions)
    mem_n = rms_norm(mem, mem_norm)
    v_first = None
    for l in range(DEPTH):
        h = rms_norm(x, norm_mix[l])
        p_nsa, p_pool, p_rwkv, p_gla = _split(h @ w_in[l], (NSA_IN, POOL_IN, RWKV_IN, GLA_IN))
        o_nsa = nsa_mixer(p_nsa, cos, sin, nsa_cmp_pe[l], nsa_cmp_w1[l], nsa_cmp_w2[l])
        o_pool = pool_mixer(p_pool, pool_w[l], pool_scale[l])
        v_res_logit = None if l == 0 else rwkv_v0[l - 1] + (h @ rwkv_v1[l - 1]) @ rwkv_v2[l - 1]
        o_rwkv, v_l = rwkv7_mixer(p_rwkv, rwkv_mu[l], rwkv_w0[l], rwkv_w2[l], rwkv_a0[l], rwkv_a2[l],
                                  rwkv_g2[l], rwkv_k_k[l], rwkv_k_a[l], rwkv_r_k[l], rwkv_ln[l],
                                  v_first, v_res_logit)
        if l == 0:
            v_first = v_l
        o_gla = gla_mixer(p_gla, gla_a2[l], gla_ab[l], gla_norm[l])
        merged = jnp.zeros_like(x)
        for i, o in enumerate((o_nsa, o_pool, o_rwkv, o_gla)):
            gate = jax.nn.sigmoid(h @ w_gate[l, i] + b_gate[l, i])
            merged = merged + gate * (o @ w_branch[l, i])
        x = x + merged @ w_out[l]
        x = x + cross_attention(rms_norm(x, norm_ca[l]), mem_n, w_ca_q[l], w_ca_kv[l], w_ca_o[l])
        hf = rms_norm(x, norm_ffn[l])
        j = l // 2
        if l % 2 == 0:
            x = x + swiglu(hf, ffn_w_gate[j], ffn_w_up[j], ffn_w_down[j])
        else:
            x = x + moe_swiglu(hf, moe_router[j], moe_w_gate[j], moe_w_up[j], moe_w_down[j])
    return rms_norm(x, norm_final)


_drawn_inputs = setup_inputs


def setup_inputs(seed=0):
    import zlib

    import numpy as np

    out = dict(_drawn_inputs(seed))
    spreads = {}
    factors = {'rwkv_v0': 2.864, 'norm_ca': 3.625, 'mem_norm': 2.906}
    for name, (base, spread) in spreads.items():
        noise = np.random.default_rng([zlib.crc32(name.encode()), seed]).standard_normal(out[name].shape)
        drawn = base * np.exp(spread * noise) if base else spread * noise
        out[name] = __import__('jax').numpy.asarray(drawn.astype(out[name].dtype))
    for name, factor in factors.items():
        out[name] = (out[name] * factor).astype(out[name].dtype)
    return out
```

```python
from contextlib import ExitStack

import numpy as np

import concourse.bass as bass
from concourse import mybir

F32 = mybir.dt.float32
I32 = mybir.dt.int32
U32 = mybir.dt.uint32
ALU = mybir.AluOpType
ACT = mybir.ActivationFunctionType
AX = mybir.AxisListType.X

P = 128
DEPTH, D, SEQ, MEM = 2, 1024, 256, 256
KC = D // P
TT = SEQ // P
HD = 64
W_BR = 256
N_BR = 4
DFF, N_EXP = 2816, 8
FC = DFF // P
EPS, GN_EPS = 1e-6, 64e-5
NEG = -1e30
CMP_LEN, CMP_STRIDE = 32, 16
N_CMP = (SEQ - CMP_LEN) // CMP_STRIDE + 1
ROPE_HALF = 8
C_RW = 64
C_GL = 16
N_GL = SEQ // C_GL

OCT = 8 * P
SLAB = 3 * OCT
RING = 4
N_TM = 4
N_FM = 4
O_CMP, O_MERGE, O_OUT, O_KV, O_CQ, O_CO = 0, 4, 44, 52, 56, 58
N_OCT = 60
LAYER_SLABS = N_TM + N_FM + N_OCT // 3
FIRST_SLAB = [0, LAYER_SLABS + FC]
N_SLABS = 2 * LAYER_SLABS + FC * (1 + N_EXP)

TM_Q, TM_KS, TM_KW, TM_KC, TM_VC, TM_VS, TM_VW, TM_POOL, TM_GV, TM_END = (
    0, 256, 384, 512, 640, 768, 896, 1024, 1280, 1536)
FM_R, FM_K, FM_V, FM_LR, FM_GQ, FM_GK, FM_OG, FM_MISC = 0, 2, 4, 6, 7, 8, 9, 11
MISC_V1, MISC_GATES = 32, 64

PAR_COLS = dict(norm_mix=8, norm_ca=8, norm_ffn=8, mem_norm=8, b_gate=32, pool_scale=2, mu=7, w0=2, a0=2,
                k_k=2, k_a=2, r_k=2, ln=2, v0=2, ab=1, gnorm=1, pe=32, router=64)
PAR = {}
for _n, _c in PAR_COLS.items():
    PAR[_n] = sum(PAR_COLS[m] for m in list(PAR_COLS)[:len(PAR)])
N_PAR = sum(PAR_COLS.values())
MIX_COLS = dict(w2=256, a2=256, g2=256, v2=256, gla_a2=128, pool=256, cmp=128)
MIX = {}
for _n, _c in MIX_COLS.items():
    MIX[_n] = sum(MIX_COLS[m] for m in list(MIX_COLS)[:len(MIX)])
N_MIX = sum(MIX_COLS.values())
CON_COLS = dict(ident=128, causal=512, cmp_add=2 * N_CMP, cmp_keep=2 * N_CMP, level=6 * 128, rw_b=256, rw_k=256,
                gl_causal=128, pool=4 * 384, reset64=512, reset16=256, ones=128, chunk16=8, freq=8, iota=128, before=128, every=128)
CON = {}
for _n, _c in CON_COLS.items():
    CON[_n] = sum(CON_COLS[m] for m in list(CON_COLS)[:len(CON)])
N_CON = sum(CON_COLS.values())

PLAN = [("norm", 0)]
for _l in range(DEPTH):
    PLAN += [("norm", 1 + 3 * _l), ("project", _l), ("nsa", _l), ("pool", _l), ("gla", _l), ("rwkv", _l),
             ("merge", _l), ("memory", _l), ("norm", 2 + 3 * _l), ("cross", _l), ("norm", 3 + 3 * _l),
             ("ffn", _l) if _l == 0 else ("moe", _l)]
PLAN += [("final", 0)]


def slabs_of(plan):
    n = 0
    for step, l in plan:
        n = {"project": FIRST_SLAB[min(l, 1)] + N_TM + N_FM, "nsa": FIRST_SLAB[min(l, 1)] + 10,
             "merge": FIRST_SLAB[min(l, 1)] + 8 + 18,
             "memory": FIRST_SLAB[min(l, 1)] + 8 + 19, "cross": FIRST_SLAB[min(l, 1)] + 8 + 20,
             "ffn": FIRST_SLAB[1], "moe": N_SLABS}.get(step, n)
    return n


def trunk(nc, stream, params, mixw, consts, x_in, mem_in, pos_in, gain_in, out):
    n_slabs = slabs_of(PLAN)
    with ExitStack() as ctx:
        def sb(name, shape, dt=F32):
            return ctx.enter_context(nc.sbuf_tensor(name, shape, dt))

        def sem(name):
            return ctx.enter_context(nc.semaphore(name))

        ring = sb("ring", [P, RING, SLAB])
        x = sb("x", [P, TT, D])
        hT = sb("hT", [P, KC, SEQ])
        oT = sb("oT", [P, 2 * N_BR, SEQ])
        n_ptm, n_pfm = TT * (TM_END + 12), 12 * SEQ
        big = sb("big", [P, n_ptm + n_pfm + KC * MEM])
        ptm = big[:, 0:n_ptm].rearrange("p (t c) -> p t c", t=TT)
        pfm = big[:, n_ptm:n_ptm + n_pfm].rearrange("p (c t) -> p c t", c=12)
        memT = big[:, n_ptm + n_pfm:].rearrange("p (k t) -> p k t", k=KC)
        y_exp = big[:, 0:N_EXP * D].rearrange("p (e d) -> p e d", e=N_EXP)
        v_first = sb("v_first", [P, 2, SEQ])
        par = sb("par", [P, DEPTH, N_PAR])
        mw = sb("mw", [P, N_MIX])
        con = sb("con", [P, N_CON])
        pos = sb("pos", [P, 3], I32)
        trig = sb("trig", [P, 2, 3, ROPE_HALF])
        stat = sb("stat", [P, 64])
        idx = sb("idx", [P, 8], U32)
        load_of = sb("load_of", [P, N_EXP], I32)
        arena = sb("arena", [P, 17000])
        ps = ctx.enter_context(nc.psum_tensor("ps", [P, 8 * 512], F32))

        def bank(b, n=1):
            return ps[:, b * 512:(b + n) * 512]

        class Carve:

            def __init__(self, at=0):
                self.at = at

            def __call__(self, *shape):
                n = int(np.prod(shape))
                v = arena[:, self.at:self.at + n]
                self.at += n
                assert self.at <= 17000, self.at
                names = "abcde"[:len(shape)]
                if len(shape) == 1:
                    return v
                return v.rearrange("p (" + " ".join(names) + ") -> p " + " ".join(names),
                                   **dict(zip(names, shape)))

        def parc(l, name, i=0, n=1):
            c = PAR[name] + i
            return par[:, l, c:c + n]

        def conc(name, a=0, n=None):
            c = CON[name] + a
            return con[:, c:c + (CON_COLS[name] - a if n is None else n)]

        def mixc(name, a=0, n=128):
            return mw[:, MIX[name] + a:MIX[name] + a + n]

        def spread(ap, axis, n):
            v = ap.unsqueeze(axis)
            shape = list(v.shape)
            shape[axis] = n
            return v.broadcast_to(shape)

        ident = conc("ident")

        c = Carve()
        xn = c(TT, D)
        mem_sb = c(TT, D)

        c = Carve()
        qpad = c(2, 2, SEQ)
        kT = c(2, SEQ)
        prob = c(2, 4, SEQ)
        probT = c(8, P)
        att_tmp = c(4, HD)
        o_tm = c(TT, 4, HD)
        kc2 = c(2, 2, SEQ)
        hid_c = c(2, 2 * N_CMP)
        hid_pe = c(2)
        k_cmp = c(2, HD)
        v_cmp = c(2, HD)
        kcT = c(N_CMP)
        cprob = c(2, 4, N_CMP)
        cprobT = c(8, P)
        rope_a, rope_b, rope_c, rope_d = (c(2, 8, 8) for _ in range(4))
        gates = c(TT, 12)
        kc_dup = c(TT, 4, 2, HD)
        ca_oT = c(2, SEQ)

        c = Carve(12000)
        ca_k = c(2, SEQ)
        ca_v = c(2, W_BR)

        c = Carve()
        poolT = c(2, SEQ)

        c = Carve()
        gl_z, gl_e, gl_b, gl_eq, gl_ek, gl_ke = (c(SEQ) for _ in range(6))
        gl_dl = c(N_GL)
        gl_q = c(4, SEQ)
        gl_att = c(TT, 4, P)
        gl_k8 = c(TT, 8, P)
        gl_s = c(N_GL, HD)
        gl_o = c(2, SEQ)
        gl_sq = c(2, SEQ)
        gl_r = c(2, SEQ)
        gl_og = c(2, SEQ)

        c = Carve()
        rw_kr = c(2, 2, 2, SEQ)
        rw_ab = c(TT, 2, 2, 2, P)
        rw_ak = c(TT, 2, 2, 2, P)
        rw_km = c(TT, 2, 2, P)
        rw_bm = c(TT, 2, 2, P)
        rw_ep, rw_g, rw_bt, rw_kt, rw_rk, rw_bonus = (c(2, SEQ) for _ in range(6))
        rw_s = c(2, 2, HD)
        rw_lrx = c(SEQ)
        work = c.at
        rw_lw, rw_cl, rw_clm, rw_em, rw_kk, rw_sq, rw_a, rw_k2 = (c(2, SEQ) for _ in range(8))
        c = Carve(work)
        rw_x = c(8, P)
        rw_xt = c(8, P)
        rw_t1 = c(8, P)
        rw_v = c(TT, W_BR)
        rw_z = c(W_BR)
        rw_u = c(W_BR)
        c = Carve(work)
        rw_y, rw_yc, rw_y2, rw_r = (c(2, SEQ) for _ in range(4))
        rw_top = work + 8 * 512
        c = Carve(rw_top)
        rw_vg = c(2, SEQ)

        c = Carve()
        merged = c(KC, SEQ)
        sig = c(4, SEQ)
        mtmp = c(4, SEQ)
        c = Carve(TT * D)
        silu = c(2, SEQ)
        hidden = c(2, SEQ)
        combine = c(TT, N_EXP)
        comb_few = c(TT, N_EXP)
        comb_many = c(TT, N_EXP)
        few = c(N_EXP)
        picked = c(TT, N_EXP)
        place = c(TT, N_EXP)
        logit = c(TT, N_EXP)
        top = c(TT, 8)
        topi = c(TT, 8)
        pick = c(TT, N_EXP)
        sel = c(2, TT, P)
        sel_w = c(2, TT, P)
        sel_wT = c(N_EXP, TT, P)
        h_exp = c(N_EXP, KC, P)
        c = Carve()
        fin_gain = c(D)
        fin_x = c(TT, D)

        landed = [sem(f"slab_landed_{i}") for i in range(RING)]
        slab_read = sem("slab_read")
        loads = sem("loads")
        mix_loaded = sem("mix_loaded")
        gain_loaded = sem("gain_loaded")
        stored = sem("stored")
        dve_step = sem("dve_step")
        act_step = sem("act_step")
        root_ready = sem("root_ready")
        root_done = sem("root_done")
        trig_arg = sem("trig_arg")
        trig_done = sem("trig_done")
        squares = sem("squares")
        x_scaled = sem("x_scaled")
        x_turned = sem("x_turned")
        h_ready = sem("h_ready")
        proj_done = sem("proj_done")
        proj_dve = sem("proj_copied_dve")
        proj_act = sem("proj_copied_act")
        roped = sem("roped")
        nsa_turned = sem("nsa_turned")
        q_padded = sem("q_padded")
        kT_copied = sem("kT_copied")
        kc_copied = sem("kc_copied")
        cmp_hidden = sem("cmp_hidden")
        cmp_gelu = sem("cmp_gelu")
        cmp_kv = sem("cmp_kv")
        cmp_kv_copied = sem("cmp_kv_copied")
        cmp_kturned = sem("cmp_kturned")
        cmp_kcopied = sem("cmp_kcopied")
        cmp_scored = sem("cmp_scored")
        cmp_shifted = sem("cmp_shifted")
        cmp_exp = sem("cmp_exp")
        cmp_prob = sem("cmp_prob")
        cmp_pturned = sem("cmp_pturned")
        cmp_pcopied = sem("cmp_pcopied")
        cmp_out = sem("cmp_out")
        cmp_added = sem("cmp_added")
        gates_on = sem("gates_on")
        scored = sem("scored")
        score_max = sem("score_max")
        exped = sem("exped")
        p_turned = sem("p_turned")
        p_copied = sem("p_copied")
        att_out = sem("att_out")
        o_added = sem("o_added")
        o_turned = sem("o_turned")
        o_copied = sem("o_copied")
        pool_d = sem("pool_d")
        pool_dc = sem("pool_dcopied")
        pool_y = sem("pool_y")
        pool_o = sem("pool_o")
        gl_pe = sem("gla_products")
        gl_dve = sem("gla_dve")
        gl_act = sem("gla_act")
        rw_pe = sem("rwkv_products")
        rw_dve = sem("rwkv_dve")
        rw_act = sem("rwkv_act")
        rw_out = sem("rwkv_out")
        inv_pe = sem("inverse_products")
        inv_dve = sem("inverse_dve")
        seq_pe = sem("chunk_products")
        seq_dve = sem("chunk_dve")
        gate_done = sem("gate_products")
        gate_sig = sem("gate_sigmoids")
        gate_used = sem("gate_used")
        merged_out = sem("merged_out")
        x_merged = sem("x_merged")
        mem_done = sem("mem_products")
        mem_copied = sem("mem_copied")
        caq_done = sem("caq_done")
        caq_padded = sem("caq_padded")
        cao_done = sem("cao_done")
        x_crossed = sem("x_crossed")
        routed = sem("router_logits")
        top_diff = sem("top_differences")
        top_exp = sem("top_exp")
        placed = sem("places_counted")
        sel_ready = sem("selections_ready")
        gathered = sem("tokens_gathered")
        gathered_c = sem("tokens_copied")
        load_ready = sem("expert_loads_ready")
        scattered = sem("outputs_scattered")
        x_moe = sem("x_moe")
        gu_done = sem("gate_up_done")
        silu_done = sem("silu_done")
        hid_ready = sem("hidden_ready")
        down_done = sem("down_done")
        x_added = sem("x_added")
        fin_ready = sem("fin_ready")
        fin_sq = sem("fin_squares")

        block = ctx.enter_context(nc.Block())

        @block.sync
        def _(sp):
            sp.dma_start(mem_sb, mem_in).then_inc(loads, 16)
            sp.dma_start(con[:, :], consts).then_inc(loads, 16)
            sp.dma_start(par[:, :, :], params.rearrange("l p c -> p l c")).then_inc(loads, 16)
            sp.dma_start(x[:, :, :], x_in).then_inc(loads, 16)
            sp.dma_start(pos[:, :], pos_in).then_inc(loads, 16)
            sp.dma_start(mw[:, :], mixw[0]).then_inc(mix_loaded, 16)
            for n in range(min(RING, n_slabs)):
                sp.dma_start(ring[:, n, :], stream[n]).then_inc(landed[n], 16)
            rounds = (n_slabs - RING) // RING
            if rounds > 0:
                with sp.Fori(0, rounds) as i:
                    for k in range(RING):
                        sp.wait_ge(slab_read, i * RING + (k + 1))
                        sp.dma_start(ring[:, k, :], stream[i * RING + (RING + k)]).then_inc(landed[k], 16)
            for n in range(RING + rounds * RING, n_slabs):
                sp.wait_ge(slab_read, n - RING + 1)
                sp.dma_start(ring[:, n % RING, :], stream[n]).then_inc(landed[n % RING], 16)
            if PLAN[-1][0] == "final":
                sp.wait_ge(fin_ready, 1)
                sp.dma_start(out, fin_x).then_inc(stored, 16)
                sp.wait_ge(stored, 16)

        @block.tensor
        def _(pe):
            reading = {"slab": -1}

            def mm(o, a, b, start=True, stop=True):
                return pe.matmul(o, a, b, start=start, stop=stop, skip_group_check=True)

            def slab(n):
                if reading["slab"] != n:
                    pe.wait_ge(landed[n % RING], 16 * (n // RING + 1))
                    reading["slab"] = n
                    reading["release"] = n > 0
                return ring[:, n % RING, :]

            def octet(l, o):
                s = slab(FIRST_SLAB[l] + N_TM + N_FM + o // 3)
                return s[:, (o % 3) * OCT:(o % 3 + 1) * OCT]

            def first(ins):
                if reading.get("release"):
                    ins.then_inc(slab_read, 1)
                    reading["release"] = False

            def turn(o, i, n=P):
                return pe.transpose(o, i, conc("ident")[0:n, 0:n])

            def norm(k):
                for kc in range(KC):
                    for tt in range(TT):
                        if kc == 0:
                            pe.wait_ge(x_scaled, TT * k + tt + 1)
                        t = turn(bank(kc // 2)[:, (kc % 2) * 256 + tt * P:(kc % 2) * 256 + (tt + 1) * P],
                                 xn[:, tt, kc * P:(kc + 1) * P])
                    if kc % 2:
                        t.then_inc(x_turned, 1)

            def project(l):
                pe.wait_ge(h_ready, KC * (2 + 3 * l))
                g = 15 * l
                groups = []
                for s in range(N_TM):
                    w = slab(FIRST_SLAB[l] + s).rearrange("p (k c) -> p k c", k=KC)
                    for tt in range(TT):
                        b = (2 * s + tt) % 8
                        for kc in range(KC):
                            m = mm(bank(b)[:, 0:384], hT[:, kc, tt * P:(tt + 1) * P], w[:, kc, :],
                                   kc == 0, kc == KC - 1)
                            if kc == 0:
                                first(m)
                        m.then_inc(proj_done, 1)
                for pair in range(6):
                    if pair % 2 == 0:
                        pe.wait_ge(proj_dve, 8 * l + pair // 2 + 1)
                    else:
                        pe.wait_ge(proj_act, 7 * l + pair // 2 + 1)
                    for half in range(2):
                        ch = 2 * pair + half
                        w = slab(FIRST_SLAB[l] + N_TM + ch // 3)[:, (ch % 3) * OCT:(ch % 3 + 1) * OCT]
                        for kc in range(KC):
                            m = mm(bank(pair)[:, half * 256:half * 256 + 256], w[:, kc * P:(kc + 1) * P],
                                   hT[:, kc, :], kc == 0, kc == KC - 1)
                            if kc == 0:
                                first(m)
                    m.then_inc(proj_done, 1)
                pe.wait_ge(proj_dve, 8 * l + 4)
                w = slab(FIRST_SLAB[l] + N_TM + 3)[:, 2 * OCT:3 * OCT]
                for tt in range(TT):
                    for kc in range(KC):
                        m = mm(bank(6)[:, tt * 12:(tt + 1) * 12], hT[:, kc, tt * P:(tt + 1) * P],
                               w[:, kc * P + MISC_GATES:kc * P + MISC_GATES + 12], kc == 0, kc == KC - 1)
                m.then_inc(proj_done, 1)

            def scores(u, tt, keys):
                nk = keys.shape[2]
                for hp in range(2):
                    for h2 in range(2):
                        h = 2 * h2 + hp if u % 6 < 4 else 2 * hp + h2
                        m = mm(bank(2 * (u % 2) + h // 2)[:, (h % 2) * 256:(h % 2) * 256 + nk],
                               qpad[:, hp, h2, tt * P:(tt + 1) * P], keys[:, hp, :])
                m.then_inc(scored, 1)

            def turn_probs(u, nk):
                pe.wait_ge(exped, u + 1)
                for h in range(4):
                    for kb in range(nk // P):
                        m = turn(bank(4, 2)[:, (2 * h + kb) * P:(2 * h + kb + 1) * P],
                                 prob[:, u % 2, h, kb * P:(kb + 1) * P])
                m.then_inc(p_turned, 1)

            def weigh(u, values, nk):
                pe.wait_ge(p_copied, u + 1)
                for h in range(4):
                    for kb in range(nk // P):
                        m = mm(bank(6 + u % 2)[:, h * HD:(h + 1) * HD], probT[:, 2 * h + kb, :],
                               values(h, kb), kb == 0, kb == nk // P - 1)
                m.then_inc(att_out, 1)

            def turn_out(l, which):
                pe.wait_ge(o_added, 6 * l + (4 if which == 0 else 6))
                for cc in range(2):
                    for tt in range(TT):
                        m = turn(bank(0)[:, cc * 256 + tt * P:cc * 256 + (tt + 1) * P],
                                 o_tm[:, tt, 2 * cc:2 * cc + 2, :].rearrange("p a b -> p (a b)"))
                m.then_inc(o_turned, 1)

            def nsa(l):
                pe.wait_ge(roped, l + 1)
                pe.wait_ge(proj_act, 7 * (l + 1))
                for r in range(2):
                    for tt in range(TT):
                        turn(bank(0)[:, (2 * r + tt) * P:(2 * r + tt + 1) * P],
                             ptm[:, tt, TM_Q + r * P:TM_Q + (r + 1) * P])
                for a, at in enumerate((TM_KS, TM_KW)):
                    for tt in range(TT):
                        turn(bank(1)[:, (2 * a + tt) * P:(2 * a + tt + 1) * P], ptm[:, tt, at:at + P])
                for j in range(2):
                    for g in range(2):
                        for tt in range(TT):
                            m = turn(bank(2 + j)[:, (2 * g + tt) * P:(2 * g + tt + 1) * P],
                                     kc_dup[:, tt, 2 * j + g, :, :].rearrange("p a b -> p (a b)"))
                m.then_inc(nsa_turned, 1)
                pe.wait_ge(kc_copied, l + 1)
                for j in range(2):
                    for lp in range(16):
                        w = octet(l, O_CMP + 2 * j + lp // 8)[:, (lp % 8) * P:(lp % 8 + 1) * P]
                        t = kc2[:, j, :, :].rearrange("p g (m a b) -> p g m a b", a=8, b=2)
                        t = t[:, :, lp // 8:lp // 8 + N_CMP, lp % 8, 0]
                        o = bank(4)[:, j * 32:j * 32 + 2 * N_CMP].rearrange("p (g n) -> p g n", g=2)
                        first(mm(o, w, t, lp == 0, lp == 15))
                        m = mm(bank(5)[:, j:j + 1], w, parc(l, "pe", j * 16 + lp), lp == 0, lp == 15)
                m.then_inc(cmp_hidden, 1)
                pe.wait_ge(cmp_gelu, 2 * (l + 1))
                if l == 0:
                    pe.wait_ge(mix_loaded, 16)
                else:
                    pe.wait_ge(mix_loaded, 32)
                for j in range(2):
                    for g in range(2):
                        m = mm(bank(6)[0:N_CMP, (2 * j + g) * HD:(2 * j + g + 1) * HD],
                               hid_c[:, j, g * N_CMP:(g + 1) * N_CMP], mixc("cmp", j * HD, HD))
                m.then_inc(cmp_kv, 1)
                pe.wait_ge(cmp_kv_copied, l + 1)
                turn(bank(7)[:, 0:N_CMP], k_cmp[0:N_CMP, :, :].rearrange("p a b -> p (a b)"),
                     N_CMP).then_inc(cmp_kturned, 1)
                pe.wait_ge(cmp_kcopied, l + 1)
                pe.wait_ge(q_padded, l + 1)
                for tt in range(TT):
                    for h in range(4):
                        m = mm(bank(5)[:, (4 * tt + h) * N_CMP:(4 * tt + h + 1) * N_CMP],
                               qpad[:, h % 2, h // 2, tt * P:(tt + 1) * P], kcT)
                m.then_inc(cmp_scored, 1)
                pe.wait_ge(kT_copied, l + 1)
                units = [(6 * l, 0, 0), (6 * l + 1, 0, 1), (6 * l + 2, 1, 0), (6 * l + 3, 1, 1)]

                def keys(a, tt):
                    return spread(kT[:, a, 0:P * (tt + 1)], 1, 2)

                def values(a):
                    at = TM_VS if a == 0 else TM_VW
                    return lambda h, kb: ptm[:, kb, at + (h // 2) * HD:at + (h // 2 + 1) * HD]

                scores(units[0][0], units[0][2], keys(units[0][1], units[0][2]))
                pe.wait_ge(cmp_prob, l + 1)
                for h in range(8):
                    m = turn(bank(4, 2)[0:N_CMP, h * P:(h + 1) * P], cprob[:, h // 4, h % 4, :])
                m.then_inc(cmp_pturned, 1)
                pe.wait_ge(cmp_pcopied, l + 1)
                for h in range(8):
                    m = mm(bank(7)[:, h * HD:(h + 1) * HD], cprobT[0:N_CMP, h, :],
                           v_cmp[0:N_CMP, (h % 4) // 2, :])
                m.then_inc(cmp_out, 1)
                for n, (u, a, tt) in enumerate(units):
                    if n < 3:
                        u2, a2, t2 = units[n + 1]
                        if n >= 1:
                            pe.wait_ge(score_max, u)
                        scores(u2, t2, keys(a2, t2))
                    turn_probs(u, P * (tt + 1))
                    if n == 1:
                        pe.wait_ge(cmp_added, l + 1)
                    if n >= 2:
                        pe.wait_ge(o_added, u - 1)
                    weigh(u, values(a), P * (tt + 1))
                turn_out(l, 0)

            def pool(l):
                pe.wait_ge(o_copied, 2 * l + 1)
                for pr in range(2):
                    for g2 in range(2):
                        g = 2 * pr + g2
                        o = bank(7)[g2 * HD:(g2 + 1) * HD, pr * 256:(pr + 1) * 256]
                        for tt in range(TT):
                            u = ptm[:, tt, TM_POOL + g * HD:TM_POOL + (g + 1) * HD]
                            if tt == 0:
                                m = mm(o, u, conc("pool", 384 * g, 256), True, False)
                            else:
                                m = mm(o[:, P:2 * P], u, conc("pool", 384 * g + 256, P), False, True)
                m.then_inc(pool_d, 1)
                pe.wait_ge(pool_dc, l + 1)
                for pr in range(2):
                    m = mm(bank(6)[:, pr * 256:(pr + 1) * 256], mixc("pool", pr * P), poolT[:, pr, :])
                m.then_inc(pool_y, 1)

            def gla(l):
                pe.wait_ge(pool_o, l + 1)
                mm(bank(0)[:, 0:256], mixc("gla_a2"), pfm[:, FM_MISC, :]).then_inc(gl_pe, 1)
                pe.wait_ge(gl_dve, 7 * l + 3)
                for tt in range(TT):
                    m = mm(bank(1 + tt), gl_ek[:, tt * P:(tt + 1) * P], gl_q[:, :, tt * P:(tt + 1) * P])
                m.then_inc(gl_pe, 1)
                for tt in range(TT):
                    m = turn(bank(3)[:, tt * P:(tt + 1) * P], gl_ke[:, tt * P:(tt + 1) * P])
                m.then_inc(gl_pe, 1)
                pe.wait_ge(gl_dve, 7 * l + 4)
                for tt in range(TT):
                    for h in range(4):
                        for n in range(8):
                            m = mm(bank(4 + tt)[32 * h:32 * h + 32, n * HD:(n + 1) * HD],
                                   gl_k8[:, tt, n, 32 * h:32 * h + 32],
                                   ptm[:, tt, TM_GV + h * HD:TM_GV + (h + 1) * HD])
                m.then_inc(gl_pe, 1)
                pe.wait_ge(gl_dve, 7 * l + 5)
                for hp in range(2):
                    for tt in range(TT):
                        for h2 in range(2):
                            h = 2 * hp + h2
                            o = bank(6)[h2 * HD:(h2 + 1) * HD, hp * 256 + tt * P:hp * 256 + (tt + 1) * P]
                            mm(o, ptm[:, tt, TM_GV + h * HD:TM_GV + (h + 1) * HD], gl_att[:, tt, h, :],
                               True, False)
                            for n in range(8):
                                m = mm(o[:, n * C_GL:(n + 1) * C_GL], gl_s[:, 8 * tt + n, :],
                                       gl_q[:, h, tt * P + n * C_GL:tt * P + (n + 1) * C_GL], False, n == 7)
                m.then_inc(gl_pe, 1)
                pe.wait_ge(gl_dve, 7 * l + 6)
                mm(bank(7), conc("ones"), gl_sq.rearrange("p a b -> p (a b)")).then_inc(gl_pe, 1)

            def rwkv(l):
                n_pe = 7 * l
                pe.wait_ge(rw_act, 8 * l + 1)
                for hp in range(2):
                    mm(bank(0)[:, hp * 256:hp * 256 + 256], mixc("w2", hp * P), rw_lrx)
                    mm(bank(1)[:, hp * 256:hp * 256 + 256], mixc("a2", hp * P), rw_lrx)
                    if l:
                        mm(bank(3)[:, hp * 256:hp * 256 + 256], mixc("v2", hp * P), pfm[:, FM_MISC, :])
                    m = mm(bank(2)[:, hp * 256:hp * 256 + 256], mixc("g2", hp * P), rw_lrx)
                m.then_inc(rw_pe, 1)
                pe.wait_ge(rw_dve, 7 * l + 3)
                mm(bank(4), conc("ones"), rw_sq.rearrange("p a b -> p (a b)")).then_inc(rw_pe, 1)
                pe.wait_ge(rw_dve, 7 * l + 4)
                mm(bank(5), conc("ones"), rw_rk.rearrange("p a b -> p (a b)"))
                for tt in range(TT):
                    for hp in range(2):
                        i = 2 * tt + hp
                        turn(bank(6)[:, i * P:(i + 1) * P], rw_kt[:, hp, tt * P:(tt + 1) * P])
                        turn(bank(7)[:, i * P:(i + 1) * P], rw_bt[:, hp, tt * P:(tt + 1) * P])
                for tt in range(TT):
                    for hp in range(2):
                        kr = rw_kr[:, hp, :, :, tt * P:(tt + 1) * P].rearrange("p a b t -> p (a b) t")
                        m = mm(bank(2 * tt + hp), rw_bt[:, hp, tt * P:(tt + 1) * P], kr)
                m.then_inc(rw_pe, 1)
                pe.wait_ge(rw_dve, 7 * l + 5)
                for tt in range(TT):
                    for hp in range(2):
                        kr = rw_kr[:, hp, :, :, tt * P:(tt + 1) * P].rearrange("p a b t -> p (a b) t")
                        m = mm(bank(2 * tt + hp), rw_kt[:, hp, tt * P:(tt + 1) * P], kr)
                m.then_inc(rw_pe, 1)
                pe.wait_ge(rw_dve, 7 * l + 6)
                for tt in range(TT):
                    for hp in range(2):
                        m = turn(bank(5)[:, (2 * tt + hp) * P:(2 * tt + hp + 1) * P],
                                 pfm[:, FM_V + hp, tt * P:(tt + 1) * P])
                m.then_inc(rw_pe, 1)

                for j in range(6):
                    pe.wait_ge(inv_dve, 13 * l + 2 * j + 1)
                    for q in range(8):
                        m = mm(bank(q // 4)[:, (q % 4) * P:(q % 4 + 1) * P],
                               rw_ab[:, q // 4, (q // 2) % 2, q % 2, 0, :], rw_x[:, q, :])
                    m.then_inc(inv_pe, 1)
                    pe.wait_ge(inv_dve, 13 * l + 2 * j + 2)
                    for q in range(8):
                        at = slice((q % 4) * P, (q % 4 + 1) * P)
                        mm(bank(2 + q // 4)[:, at], rw_xt[:, q, :], rw_t1[:, q, :])
                        m = mm(bank(6 + q // 4)[:, at], rw_t1[:, q, :], rw_xt[:, q, :])
                    m.then_inc(inv_pe, 1)
                pe.wait_ge(inv_dve, 13 * l + 13)

                for ch in range(4):
                    tt, par2 = ch // 2, ch % 2
                    rows = slice(64 * par2, 64 * par2 + 64)
                    tok = slice(ch * C_RW, (ch + 1) * C_RW)
                    if ch == 0:
                        pe.wait_ge(rw_act, 8 * l + 6)
                    else:
                        pe.wait_ge(seq_dve, 12 * l + 3 * ch)
                    for h in range(4):
                        o = bank(0)[rows, h * HD:(h + 1) * HD]
                        mm(o, rw_kr[:, h // 2, h % 2, 0, tok], rw_s[:, ch % 2, h // 2, :], True, False)
                        m = mm(o, rw_ak[:, tt, h // 2, h % 2, 0, rows], rw_v[:, tt, h * HD:(h + 1) * HD],
                               False, True)
                    m.then_inc(seq_pe, 1)
                    pe.wait_ge(seq_dve, 12 * l + 3 * ch + 1)
                    for h in range(4):
                        m = mm(bank(1)[rows, h * HD:(h + 1) * HD], rw_xt[:, 4 * tt + h, rows],
                               rw_z[:, h * HD:(h + 1) * HD])
                    m.then_inc(seq_pe, 1)
                    pe.wait_ge(seq_dve, 12 * l + 3 * ch + 2)
                    for hp in range(2):
                        o = bank(3)[:, hp * P:(hp + 1) * P]
                        mm(o, rw_km[:, tt, par2, hp, :], rw_v[:, tt, hp * P:(hp + 1) * P], True, False)
                        m = mm(o, rw_bm[:, tt, par2, hp, :], rw_u[:, hp * P:(hp + 1) * P], False, True)
                    m.then_inc(seq_pe, 1)
                    for h in range(4):
                        o = bank(2)[(h % 2) * HD:(h % 2 + 1) * HD, (h // 2) * 256 + ch * C_RW:
                                    (h // 2) * 256 + (ch + 1) * C_RW]
                        mm(o, rw_s[:, ch % 2, h // 2, :], rw_kr[:, h // 2, h % 2, 1, tok], True, False)
                        mm(o, rw_v[:, tt, h * HD:(h + 1) * HD], rw_ak[:, tt, h // 2, h % 2, 1, rows],
                           False, False)
                        m = mm(o, rw_u[:, h * HD:(h + 1) * HD], rw_ab[:, tt, h // 2, h % 2, 1, rows],
                               False, True)
                    m.then_inc(seq_pe, 1)
                pe.wait_ge(rw_act, 8 * l + 7)
                mm(bank(4), conc("ones"), rw_y.rearrange("p a b -> p (a b)")).then_inc(rw_pe, 1)
                pe.wait_ge(rw_dve, 7 * l + 7)
                mm(bank(5), conc("ones"), rw_y2.rearrange("p a b -> p (a b)")).then_inc(rw_pe, 1)

            def merge(l):
                pe.wait_ge(o_copied, 2 * l + 1)
                pe.wait_ge(pool_o, l + 1)
                pe.wait_ge(gl_dve, 7 * (l + 1))
                pe.wait_ge(rw_out, l + 1)
                for j in range(KC):
                    for i in range(N_BR):
                        n = 32 * l + 4 * j + i
                        b = bank(n % 4)
                        if 4 * j + i >= 4:
                            pe.wait_ge(gate_used, n - 3)
                        wb = octet(l, O_MERGE + 5 * j)
                        for kc in range(2):
                            m = mm(b[:, 256:512], wb[:, (2 * i + kc) * P:(2 * i + kc + 1) * P],
                                   oT[:, 2 * i + kc, :], kc == 0, kc == 1)
                            if kc == 0:
                                first(m)
                    for i in range(N_BR):
                        n = 32 * l + 4 * j + i
                        b = bank(n % 4)
                        wg = octet(l, O_MERGE + 5 * j + 1 + i)
                        for kc in range(KC):
                            m = mm(b[:, 0:256], wg[:, kc * P:(kc + 1) * P], hT[:, kc, :], kc == 0, kc == KC - 1)
                            if kc == 0:
                                first(m)
                        m.then_inc(gate_done, 1)
                pe.wait_ge(gate_used, 32 * (l + 1))
                for kc in range(KC):
                    w = octet(l, O_OUT + kc)
                    for tt in range(TT):
                        for nb in range(2):
                            m = mm(bank(4 + 2 * tt + nb), merged[:, kc, tt * P:(tt + 1) * P],
                                   w[:, nb * 512:(nb + 1) * 512], kc == 0, kc == KC - 1)
                            if tt == 0 and nb == 0:
                                first(m)
                m.then_inc(merged_out, 1)

            def memory(l):
                for cc in range(2):
                    w = octet(l, O_KV + cc)
                    for kc in range(KC):
                        m = mm(bank(0)[:, cc * 256:cc * 256 + 256], w[:, kc * P:(kc + 1) * P],
                               memT[:, kc, :], kc == 0, kc == KC - 1)
                        if kc == 0:
                            first(m)
                for mt in range(2):
                    for kc in range(KC):
                        w = octet(l, O_KV + 2 + kc // 4)[:, (kc % 4) * 256:(kc % 4 + 1) * 256]
                        m = mm(bank(1 + mt)[:, 0:256], memT[:, kc, mt * P:(mt + 1) * P], w,
                               kc == 0, kc == KC - 1)
                        if kc % 4 == 0 and mt == 0:
                            first(m)
                m.then_inc(mem_done, 1)
                pe.wait_ge(mem_copied, 2 * (l + 1))

            def cross(l):
                pe.wait_ge(h_ready, KC * (3 + 3 * l))
                for cc in range(2):
                    w = octet(l, O_CQ + cc)
                    for kc in range(KC):
                        m = mm(bank(4)[:, cc * 256:cc * 256 + 256], w[:, kc * P:(kc + 1) * P], hT[:, kc, :],
                               kc == 0, kc == KC - 1)
                        if kc == 0:
                            first(m)
                m.then_inc(caq_done, 1)
                pe.wait_ge(caq_padded, l + 1)
                for tt in range(TT):
                    scores(6 * l + 4 + tt, tt, ca_k)
                for tt in range(TT):
                    turn_probs(6 * l + 4 + tt, MEM)
                    weigh(6 * l + 4 + tt, lambda h, kb: ca_v[:, kb, h * HD:(h + 1) * HD], MEM)
                turn_out(l, 1)
                pe.wait_ge(o_copied, 2 * l + 2)
                for kc in range(2):
                    w = octet(l, O_CO + kc)
                    for tt in range(TT):
                        for nb in range(2):
                            m = mm(bank(2 * tt + nb), ca_oT[:, kc, tt * P:(tt + 1) * P],
                                   w[:, nb * 512:(nb + 1) * 512], kc == 0, kc == 1)
                            if tt == 0 and nb == 0:
                                first(m)
                m.then_inc(cao_done, 1)

            def gate_up(at, release, h, width):
                b = bank(4 + at % 2)
                w = ring[:, at % RING, :]
                for half in range(2):
                    for kc in range(KC):
                        m = mm(b[:, half * 256:half * 256 + width],
                               w[:, half * OCT + kc * P:half * OCT + (kc + 1) * P], h[:, kc, :],
                               kc == 0, kc == KC - 1)
                        if release and half == 0 and kc == 0:
                            m.then_inc(slab_read, 1)
                m.then_inc(gu_done, 1)

            def down(f, at, width):
                w = ring[:, at % RING, :]
                for tt in range(width // P):
                    for nb in range(2):
                        m = mm(bank(2 * tt + nb), hidden[:, at % 2, tt * P:(tt + 1) * P],
                               w[:, 2 * OCT + nb * 512:2 * OCT + (nb + 1) * 512], f == 0, f == FC - 1)
                return m

            def expert(c0, e0, slab0, h, width, up=0, ups=0, upe=0):
                for f in range(FC + 1):
                    if f < FC:
                        pe.wait_ge(landed[(slab0 + f) % RING], ups * 16 + 16 * ((slab0 + f) // RING + 1))
                        if c0 + f >= 2:
                            pe.wait_ge(hid_ready, up + (c0 + f - 1))
                        gate_up(slab0 + f, e0 > 0 or f != 1, h, width)
                    if f >= 1:
                        if f == 1 and e0 >= 1:
                            pe.wait_ge(x_added, upe + e0)
                        pe.wait_ge(hid_ready, up + (c0 + f))
                        m = down(f - 1, slab0 + f - 1, width)
                m.then_inc(down_done, 1)

            def ffn(l):
                pe.wait_ge(h_ready, KC * (4 + 3 * l))
                expert(0, 0, LAYER_SLABS, hT, SEQ)

            def moe(l):
                pe.wait_ge(h_ready, KC * (4 + 3 * l))
                for tt in range(TT):
                    for kc in range(KC):
                        m = mm(bank(6)[:, tt * 8:tt * 8 + 8], hT[:, kc, tt * P:(tt + 1) * P],
                               parc(l, "router", 8 * kc, 8), kc == 0, kc == KC - 1)
                m.then_inc(routed, 1)
                pe.wait_ge(top_diff, 1)
                mm(bank(7)[:, 0:8], conc("before"), picked[:, 0, :])
                mm(bank(7)[:, 8:16], conc("every"), picked[:, 0, :], True, False)
                mm(bank(7)[:, 8:16], conc("before"), picked[:, 1, :], False, True)
                mm(bank(7)[:, 16:24], conc("every"), picked[:, 0, :], True, False)
                mm(bank(7)[:, 16:24], conc("every"), picked[:, 1, :], False, True).then_inc(placed, 1)
                for e in range(N_EXP):
                    pe.wait_ge(sel_ready, e + 1)
                    if e >= 2:
                        pe.wait_ge(gathered_c, e - 1)
                    for kc in range(KC):
                        for tt in range(TT):
                            mm(bank(2 * (e % 2), 2)[:, kc * P:(kc + 1) * P], xn[:, tt, kc * P:(kc + 1) * P],
                               sel[:, e % 2, tt, :], tt == 0, tt == 1)
                    for tt in range(TT):
                        m = turn(bank(6 + e % 2)[:, tt * P:(tt + 1) * P], sel_w[:, e % 2, tt, :])
                    m.then_inc(gathered, 1)
                pe.wait_ge(gathered_c, N_EXP)
                pe.wait_ge(load_ready, 1)
                s0 = FIRST_SLAB[1] + LAYER_SLABS
                with pe.Fori(0, N_EXP // 2) as i:
                    for half in range(2):
                        ups = (i * (2 * FC), i * (2 * FC // RING), i * 2)
                        tokens = pe.value_load(load_of[0:1, bass.ds(i * 2 + half, 1)], min_val=0, max_val=SEQ)
                        with pe.If(tokens < P + 1):
                            own = h_exp[:, bass.ds(i * 2 + half, 1), :, :].rearrange("p e k t -> p (e k) t")
                            expert(FC * (1 + half), 1 + half, s0 + FC * half, own, P, *ups)
                        with pe.Else():
                            expert(FC * (1 + half), 1 + half, s0 + FC * half, hT, SEQ, *ups)
                pe.wait_ge(x_added, 1 + N_EXP)
                for e in range(N_EXP):
                    for tt in range(TT):
                        for nb in range(2):
                            m = mm(bank(2 * tt + nb), sel_wT[:, e, tt, :], y_exp[:, e, nb * 512:(nb + 1) * 512],
                                   e == 0, e == N_EXP - 1)
                m.then_inc(scattered, 1)

            def final(l):
                pass

            steps = dict(norm=norm, project=project, nsa=nsa, pool=pool, gla=gla, rwkv=rwkv, merge=merge,
                         memory=memory, cross=cross, ffn=ffn, moe=moe, final=final)
            pe.wait_ge(loads, 80)
            for step, l in PLAN:
                steps[step](l)

        @block.scalar
        def _(act):
            n_step = [0]

            def link(ins):
                n_step[0] += 1
                ins.then_inc(act_step, 1)
                act.wait_ge(act_step, n_step[0])

            n_root = [0]

            def root(a):
                n_root[0] += 1
                act.wait_ge(root_ready, n_root[0])
                act.activation(a, a, ACT.Sqrt).then_inc(root_done, 1)

            def norm(k):
                if k > 0:
                    l = (k - 1) // 3
                    if (k - 1) % 3 == 1:
                        act.wait_ge(x_merged, l + 1)
                    elif (k - 1) % 3 == 2:
                        act.wait_ge(x_crossed, l + 1)
                    elif l > 0:
                        act.wait_ge(x_added, 1)
                src = mem_sb if k == 0 else x
                for tt in range(TT):
                    act.activation(xn[:, tt, :], src[:, tt, :], ACT.Square,
                                   accum_out=stat[:, tt:tt + 1]).then_inc(squares, 1)
                root(stat[:, 0:2])
                gain = ("mem_norm", 0) if k == 0 else (("norm_mix", "norm_ca", "norm_ffn")[(k - 1) % 3],
                                                        (k - 1) // 3)
                dst = memT if k == 0 else hT
                for kc in range(KC):
                    act.wait_ge(x_turned, KC // 2 * k + kc // 2 + 1)
                    act.activation(dst[:, kc, :], bank(kc // 2)[:, (kc % 2) * 256:(kc % 2) * 256 + 256],
                                   ACT.Copy, scale=parc(gain[1], gain[0], kc)).then_inc(h_ready, 1)

            def project(l):
                for n in range(7):
                    act.wait_ge(proj_done, 15 * l + 2 * n + 2)
                    if n < 4:
                        act.copy(ptm[:, 1, n * 384:(n + 1) * 384], bank(2 * n + 1)[:, 0:384])\
                           .then_inc(proj_act, 1)
                    else:
                        ch = 2 * (2 * (n - 4) + 1)
                        act.copy(pfm[:, ch:ch + 2, :].rearrange("p a b -> p (a b)"), bank(2 * (n - 4) + 1))\
                           .then_inc(proj_act, 1)

            def probs(u, nk):
                act.wait_ge(score_max, u + 1)
                for h in range(4):
                    m = act.activation(prob[:, u % 2, h, 0:nk], prob[:, u % 2, h, 0:nk], ACT.Exp,
                                       bias=stat[:, 8 + 8 * (u % 2) + h:9 + 8 * (u % 2) + h],
                                       accum_out=stat[:, 12 + 8 * (u % 2) + h:13 + 8 * (u % 2) + h])
                m.then_inc(exped, 1)

            def copy_probs(u, nk):
                act.wait_ge(p_turned, u + 1)
                v = bank(4, 2).rearrange("p (h k t) -> p h k t", h=4, k=2)[:, :, 0:nk // P, :]
                o = probT.rearrange("p (h k) t -> p h k t", h=4)[:, :, 0:nk // P, :]
                act.copy(o, v).then_inc(p_copied, 1)

            def nsa(l):
                act.wait_ge(nsa_turned, l + 1)
                act.copy(kT[:, :, :].rearrange("p a b -> p (a b)"), bank(1)).then_inc(kT_copied, 1)
                act.wait_ge(cmp_hidden, l + 1)
                link(act.copy(hid_pe, bank(5)[:, 0:2]))
                for j in range(2):
                    act.activation(hid_c[:, j, :], bank(4)[:, j * 32:j * 32 + 2 * N_CMP], ACT.Gelu_apprx_tanh,
                                   bias=hid_pe[:, j:j + 1]).then_inc(cmp_gelu, 1)
                act.wait_ge(proj_dve, 8 * (l + 1))
                act.activation(gates, ptm[:, :, TM_END:TM_END + 12], ACT.Sigmoid).then_inc(gates_on, 1)
                act.wait_ge(cmp_shifted, l + 1)
                cp = cprob.rearrange("p a b c -> p (a b c)")
                act.activation(cp, cp, ACT.Exp).then_inc(cmp_exp, 1)
                probs(6 * l, P)
                for n in range(4):
                    if n == 0:
                        act.wait_ge(cmp_pturned, l + 1)
                        act.copy(cprobT[0:N_CMP, :, :].rearrange("p a b -> p (a b)"),
                                 bank(4, 2)[0:N_CMP, :]).then_inc(cmp_pcopied, 1)
                    copy_probs(6 * l + n, P * (n % 2 + 1))
                    if n < 3:
                        probs(6 * l + n + 1, P * ((n + 1) % 2 + 1))
                act.wait_ge(o_turned, 2 * l + 1)
                act.copy(oT[:, 0:2, :].rearrange("p a b -> p (a b)"), bank(0)).then_inc(o_copied, 1)

            def pool(l):
                act.wait_ge(pool_y, l + 1)
                for pr in range(2):
                    m = act.activation(oT[:, 2 + pr, :], bank(6)[:, pr * 256:(pr + 1) * 256], ACT.Copy,
                                       scale=parc(l, "pool_scale", pr))
                m.then_inc(pool_o, 1)

            def gla(l):
                act.wait_ge(gl_dve, 7 * l + 1)
                link(act.activation(gl_e, gl_e, ACT.Exp, scale=-1.0))
                act.activation(gl_e, gl_e, ACT.Ln, bias=1.0).then_inc(gl_act, 1)
                act.wait_ge(gl_dve, 7 * l + 2)
                act.activation(gl_eq, gl_b, ACT.Exp, scale=1.0 / 16)
                act.activation(gl_dl, gl_b[:, C_GL - 1:SEQ:C_GL], ACT.Exp, scale=1.0 / 16)
                act.activation(gl_ek, gl_b, ACT.Exp, scale=-1.0 / 16)
                act.activation(gl_ke, gl_ke, ACT.Exp, scale=1.0 / 16).then_inc(gl_act, 1)
                act.activation(gl_og, pfm[:, FM_OG:FM_OG + 2, :], ACT.Silu).then_inc(gl_act, 1)
                root(gl_r)

            def rwkv(l):
                act.wait_ge(rw_dve, 7 * l + 1)
                act.activation(rw_lrx[0:32, :], pfm[0:32, FM_LR, :], ACT.Tanh)
                act.copy(rw_lrx[32:64, :], pfm[32:64, FM_LR, :])
                act.activation(rw_lrx[64:128, :], pfm[64:128, FM_LR, :], ACT.Sigmoid).then_inc(rw_act, 1)
                act.wait_ge(rw_pe, 7 * l + 1)
                for hp in range(2):
                    at = slice(hp * 256, hp * 256 + 256)
                    act.activation(rw_lw[:, hp, :], bank(0)[:, at], ACT.Sigmoid, bias=parc(l, "w0", hp))
                    act.activation(rw_a[:, hp, :], bank(1)[:, at], ACT.Sigmoid, bias=parc(l, "a0", hp))
                    if l:
                        act.activation(rw_vg[:, hp, :], bank(3)[:, at], ACT.Sigmoid, bias=parc(l, "v0", hp))
                act.copy(rw_g.rearrange("p a b -> p (a b)"), bank(2)).then_inc(rw_act, 1)
                act.wait_ge(rw_dve, 7 * l + 2)
                act.activation(rw_ep, rw_cl, ACT.Exp)
                act.activation(rw_em, rw_cl, ACT.Exp, scale=-1.0)
                act.activation(rw_clm, rw_clm, ACT.Exp).then_inc(rw_act, 1)
                root(rw_bt)
                act.wait_ge(rw_pe, 7 * l + 3)
                act.copy(rw_bonus.rearrange("p a b -> p (a b)"), bank(5)).then_inc(rw_act, 1)
                for par2 in range(2):
                    r = slice(64 * par2, 64 * par2 + 64)
                    act.mul(rw_bm[r, :, par2, :, :], bank(7)[r, :].rearrange("p (a b c) -> p a b c", a=2, b=2),
                            -1.0)
                    m = act.copy(rw_km[r, :, par2, :, :],
                                 bank(6)[r, :].rearrange("p (a b c) -> p a b c", a=2, b=2))
                m.then_inc(rw_act, 1)
                act.wait_ge(rw_pe, 7 * l + 5)
                act.wait_ge(inv_dve, 13 * l + 1)
                act.copy(rw_v.rearrange("p a b -> p (a b)"), bank(5)).then_inc(rw_act, 1)
                act.wait_ge(seq_pe, 16 * (l + 1))
                act.copy(rw_y.rearrange("p a b -> p (a b)"), bank(2)).then_inc(rw_act, 1)
                act.wait_ge(rw_pe, 7 * l + 6)
                act.copy(rw_r.rearrange("p a b -> p (a b)"), bank(4)).then_inc(rw_act, 1)
                root(rw_r)
                if l == 0:
                    act.dma_start(mw[:, :], mixw[1]).then_inc(mix_loaded, 16)

            def merge(l):
                for n in range(32 * l, 32 * l + 32):
                    j, i = (n % 32) // 4, n % 4
                    act.wait_ge(gate_done, n + 1)
                    if n % 32 >= 4:
                        act.wait_ge(gate_used, n - 3)
                    act.activation(sig[:, i, :], bank(n % 4)[:, 0:256], ACT.Sigmoid,
                                   bias=parc(l, "b_gate", 8 * i + j)).then_inc(gate_sig, 1)

            def memory(l):
                act.wait_ge(mem_done, l + 1)
                act.copy(ca_k.rearrange("p a b -> p (a b)"), bank(0)).then_inc(mem_copied, 1)
                act.copy(ca_v, bank(1, 2).rearrange("p (a b) -> p a b", a=2)[:, :, 0:256]).then_inc(mem_copied, 1)

            def cross(l):
                for tt in range(TT):
                    probs(6 * l + 4 + tt, MEM)
                for tt in range(TT):
                    copy_probs(6 * l + 4 + tt, MEM)
                act.wait_ge(o_turned, 2 * l + 2)
                act.copy(ca_oT.rearrange("p a b -> p (a b)"), bank(0)).then_inc(o_copied, 1)

            def silus(at, c, up):
                act.wait_ge(gu_done, up + (c + 1))
                act.activation(silu[:, at % 2, :], bank(4 + at % 2)[:, 0:256], ACT.Silu).then_inc(silu_done, 1)

            def ffn(l):
                for f in range(FC):
                    silus(LAYER_SLABS + f, f, 0)

            def moe(l):
                act.wait_ge(top_diff, 1)
                act.activation(pick, logit, ACT.Exp).then_inc(top_exp, 1)
                s0 = FIRST_SLAB[1] + LAYER_SLABS
                with act.Fori(0, N_EXP // 2) as i:
                    for f in range(2 * FC):
                        silus(s0 + f, FC + f, i * (2 * FC))

            def final(l):
                act.wait_ge(x_moe, 1)
                act.dma_start(fin_gain, gain_in).then_inc(gain_loaded, 16)
                for tt in range(TT):
                    act.activation(fin_x[:, tt, :], x[:, tt, :], ACT.Square,
                                   accum_out=stat[:, tt:tt + 1]).then_inc(fin_sq, 1)
                root(stat[:, 0:2])

            steps = dict(norm=norm, project=project, nsa=nsa, pool=pool, gla=gla, rwkv=rwkv, merge=merge,
                         memory=memory, cross=cross, ffn=ffn, moe=moe, final=final)
            act.wait_ge(loads, 80)
            act.wait_ge(trig_arg, 1)
            act.activation(trig[:, :, :, :], trig[:, :, :, :], ACT.Sin).then_inc(trig_done, 1)
            for step, l in PLAN:
                steps[step](l)

        @block.vector
        def _(dve):
            n_step = [0]

            def link(ins):
                n_step[0] += 1
                ins.then_inc(dve_step, 1)
                dve.wait_ge(dve_step, n_step[0])

            n_root = [0]

            def rooted(a, ins):
                n_root[0] += 1
                ins.then_inc(root_ready, 1)
                dve.wait_ge(root_done, n_root[0])
                link(dve.reciprocal(a, a))

            def tt_(o, a, b, op):
                return dve.tensor_tensor(o, a, b, op)

            def rope_tables():
                two_pi = 2 * np.pi
                c1 = 6.28125
                c2 = float(np.float32(np.floor((two_pi - c1) * 2.0 ** 20) / 2.0 ** 20))
                c3 = float(np.float32(two_pi - c1 - c2))
                magic = 1.5 * 2.0 ** 23
                ang = gl_z[:, 0:24]
                turns = gl_e[:, 0:48].rearrange("p (a b) -> p a b", a=2)
                posf = stat[:, 40:43]
                link(dve.tensor_copy(posf, pos[:, :]))
                link(tt_(ang.rearrange("p (a b) -> p a b", b=8), spread(posf, 2, 8), spread(conc("freq"), 1, 3),
                         ALU.mult))
                arg = trig[:, :, :, :].rearrange("p a b c -> p a (b c)")
                for s, quarter in ((0, 0.25), (1, 0.0)):
                    link(dve.tensor_scalar(turns[:, s, :], ang, 1.0 / two_pi, quarter, ALU.mult, ALU.add))
                    link(dve.tensor_scalar(turns[:, s, :], turns[:, s, :], magic, magic, ALU.add, ALU.subtract))
                    link(dve.scalar_tensor_tensor(out=arg[:, s, :], in0=turns[:, s, :], scalar=-c1, in1=ang,
                                                  op0=ALU.mult, op1=ALU.add))
                    for cc in (c2, c3):
                        link(dve.scalar_tensor_tensor(out=arg[:, s, :], in0=turns[:, s, :], scalar=-cc,
                                                      in1=arg[:, s, :], op0=ALU.mult, op1=ALU.add))
                link(dve.tensor_scalar(arg[:, 0, :], arg[:, 0, :], float(np.pi / 2), None, ALU.add))
                lim = float(np.nextafter(np.float32(np.pi), np.float32(0)))
                dve.tensor_scalar(arg, arg, lim, -lim, ALU.min, ALU.max).then_inc(trig_arg, 1)

            def rstd_of(s, scale, eps):
                rooted(s, dve.tensor_scalar(s, s, scale, eps, ALU.mult, ALU.add))

            def norm(k):
                dve.wait_ge(squares, TT * (k + 1))
                rstd_of(stat[:, 0:2], 1.0 / D, EPS)
                src = mem_sb if k == 0 else x
                for tt in range(TT):
                    dve.tensor_scalar(xn[:, tt, :], src[:, tt, :], stat[:, tt:tt + 1], None, ALU.mult)\
                       .then_inc(x_scaled, 1)

            def project(l):
                for n in range(8):
                    dve.wait_ge(proj_done, 15 * l + 2 * n + 1)
                    if n < 4:
                        m = dve.tensor_copy(ptm[:, 0, n * 384:(n + 1) * 384], bank(2 * n)[:, 0:384])
                    elif n < 7:
                        ch = 2 * (2 * (n - 4))
                        m = dve.tensor_copy(pfm[:, ch:ch + 2, :].rearrange("p a b -> p (a b)"), bank(2 * (n - 4)))
                    else:
                        m = dve.tensor_copy(ptm[:, :, TM_END:TM_END + 12],
                                            bank(6)[:, 0:24].rearrange("p (a b) -> p a b", a=2))
                    m.then_inc(proj_dve, 1)

            def rope(t1, t2, cos, sin, ta, tb, tc, td):
                tt_(ta, t1, cos, ALU.mult)
                tt_(tb, t2, sin, ALU.mult)
                tt_(tc, t2, cos, ALU.mult)
                link(tt_(td, t1, sin, ALU.mult))
                tt_(t1, ta, tb, ALU.subtract)
                return tt_(t2, tc, td, ALU.add)

            def shifted(u, tt, nk, mask, scale=0.125):
                dve.wait_ge(scored, u + 1)
                src = bank(2 * (u % 2), 2).rearrange("p (h k) -> p h k", h=4)[:, :, 0:nk]
                dst = prob[:, u % 2, :, 0:nk]
                if mask is None:
                    link(dve.tensor_scalar(dst, src, scale, None, ALU.mult))
                else:
                    link(dve.scalar_tensor_tensor(out=dst, in0=src, scalar=scale, in1=spread(mask, 1, 4),
                                                  op0=ALU.mult, op1=ALU.add))
                nm = stat[:, 8 + 8 * (u % 2):12 + 8 * (u % 2)]
                link(dve.tensor_reduce(nm, dst, AX, ALU.max))
                dve.tensor_scalar(nm, nm, -1.0, None, ALU.mult).then_inc(score_max, 1)

            def output(u, tt, gate):
                dve.wait_ge(att_out, u + 1)
                rs = stat[:, 32 + 4 * (u % 2):36 + 4 * (u % 2)]
                link(dve.reciprocal(rs, stat[:, 12 + 8 * (u % 2):16 + 8 * (u % 2)]))
                src = bank(6 + u % 2)[:, 0:256].rearrange("p (h d) -> p h d", h=4)
                if gate is None:
                    tt_(o_tm[:, tt, :, :], src, spread(rs, 2, HD), ALU.mult).then_inc(o_added, 1)
                    return
                link(tt_(rs, rs, gate, ALU.mult))
                link(tt_(att_tmp, src, spread(rs, 2, HD), ALU.mult))
                tt_(o_tm[:, tt, :, :], o_tm[:, tt, :, :], att_tmp, ALU.add).then_inc(o_added, 1)

            def pad_queries(b, sem_):
                src = bank(b).rearrange("p (a t) -> p a t", a=2)
                dve.tensor_copy(qpad[0:64, :, 0, :], src[0:64])
                dve.tensor_copy(qpad[64:128, :, 1, :], src[64:128]).then_inc(sem_, 1)

            def nsa(l):
                dve.wait_ge(proj_act, 7 * (l + 1))
                if l == 0:
                    dve.wait_ge(trig_done, 1)
                dve.memset(qpad[64:128, :, 0, :], 0.0)
                dve.memset(qpad[0:64, :, 1, :], 0.0)
                dve.memset(kc2[64:128, :, :, SEQ - 1:SEQ], 0.0)
                for tt in range(TT):
                    dve.tensor_copy(kc_dup[:, tt, :, :, :], spread(
                        ptm[:, tt, TM_KC:TM_KC + 256].rearrange("p (a b) -> p a b", a=4), 2, 2))
                heads = ptm[:, :, 0:512].rearrange("p t (h d) -> p t h d", d=HD)

                def table(s):
                    return spread(trig[:, s, 0:2, :], 2, 8)

                rope(heads[:, :, :, 0:8], heads[:, :, :, 8:16], table(0), table(1),
                     rope_a, rope_b, rope_c, rope_d).then_inc(roped, 1)
                dve.wait_ge(nsa_turned, l + 1)
                for j in range(2):
                    src = bank(2 + j).rearrange("p (g t) -> p g t", g=2)
                    dve.tensor_copy(kc2[0:64, j, :, :], src[0:64])
                    m = dve.tensor_copy(kc2[64:128, j, :, 0:SEQ - 1], src[64:128, :, 1:SEQ])
                m.then_inc(kc_copied, 1)
                pad_queries(0, q_padded)
                dve.wait_ge(cmp_kv, l + 1)
                dve.tensor_copy(v_cmp[0:N_CMP, :, :], bank(6)[0:N_CMP, 128:256].rearrange("p (a b) -> p a b", a=2))
                link(dve.tensor_copy(k_cmp[0:N_CMP, :, :],
                                     bank(6)[0:N_CMP, 0:128].rearrange("p (a b) -> p a b", a=2)))

                def ctable(s):
                    return spread(trig[0:N_CMP, s, 2, :], 1, 2)

                rope(k_cmp[0:N_CMP, :, 0:8], k_cmp[0:N_CMP, :, 8:16], ctable(0), ctable(1),
                     rope_a[0:N_CMP, 0, 0:2, :], rope_b[0:N_CMP, 0, 0:2, :], rope_c[0:N_CMP, 0, 0:2, :],
                     rope_d[0:N_CMP, 0, 0:2, :]).then_inc(cmp_kv_copied, 1)
                dve.wait_ge(cmp_kturned, l + 1)
                dve.tensor_copy(kcT, bank(7)[:, 0:N_CMP]).then_inc(cmp_kcopied, 1)
                dve.wait_ge(cmp_scored, l + 1)
                src = bank(5)[:, 0:8 * N_CMP].rearrange("p (t h n) -> p t h n", t=2, h=4)
                add = spread(conc("cmp_add").rearrange("p (t n) -> p t n", t=2), 2, 4)
                keep = spread(conc("cmp_keep").rearrange("p (t n) -> p t n", t=2), 2, 4)
                for tt in range(TT):
                    m = dve.scalar_tensor_tensor(out=cprob[:, tt], in0=src[:, tt], scalar=0.125, in1=add[:, tt],
                                                 op0=ALU.mult, op1=ALU.add)
                link(m)
                mx = stat[:, 24:32].rearrange("p (t h) -> p t h", t=2)
                link(dve.tensor_reduce(mx, cprob, AX, ALU.max))
                tt_(cprob, cprob, spread(mx, 3, N_CMP), ALU.subtract).then_inc(cmp_shifted, 1)
                shifted(6 * l, 0, P, conc("causal", 0, P))
                dve.wait_ge(cmp_exp, l + 1)
                link(dve.tensor_reduce(mx, cprob, AX, ALU.add))
                tt_(cprob, cprob, keep, ALU.mult).then_inc(cmp_prob, 1)
                dve.wait_ge(gates_on, l + 1)
                gt = gates.rearrange("p t (h a) -> p t h a", a=3)
                link(dve.reciprocal(mx, mx))
                link(tt_(mx, mx, gt[:, :, :, 0], ALU.mult))
                dve.wait_ge(cmp_out, l + 1)
                src = bank(7).rearrange("p (t h d) -> p t h d", t=2, h=4)
                tt_(o_tm, src, spread(mx, 3, HD), ALU.mult).then_inc(cmp_added, 1)
                dve.wait_ge(cmp_added, l + 1)
                for n in range(4):
                    if n < 3:
                        t2 = (n + 1) % 2
                        shifted(6 * l + n + 1, t2, P * (t2 + 1), conc("causal", 256 * t2, P * (t2 + 1)))
                    output(6 * l + n, n % 2, gt[:, n % 2, :, 1 + n // 2])

            def pool(l):
                dve.wait_ge(pool_d, l + 1)
                dve.tensor_copy(poolT.rearrange("p a b -> p (a b)"), bank(7)).then_inc(pool_dc, 1)

            def gla(l):
                dve.wait_ge(gl_pe, 6 * l + 1)
                link(dve.tensor_scalar(gl_z, bank(0)[:, 0:256], parc(l, "ab"), None, ALU.add))
                dve.scalar_tensor_tensor(out=gl_e, in0=gl_z, scalar=-1.0, in1=gl_z,
                                         op0=ALU.mult, op1=ALU.max).then_inc(gl_dve, 1)
                link(dve.tensor_scalar(gl_z, gl_z, 0.0, None, ALU.min))
                dve.wait_ge(gl_act, 3 * l + 1)
                link(tt_(gl_z, gl_z, gl_e, ALU.subtract))
                link(dve.tensor_tensor_scan(gl_b, conc("reset16"), gl_z, 0.0, ALU.mult, ALU.add))
                b = gl_b.rearrange("p (n t) -> p n t", t=C_GL)
                last = b[:, :, C_GL - 1:C_GL].broadcast_to([P, N_GL, C_GL])
                tt_(gl_ke.rearrange("p (n t) -> p n t", t=C_GL), last, b, ALU.subtract).then_inc(gl_dve, 1)
                dve.memset(gl_q, 0.0)
                link(dve.memset(gl_s[:, 0, :], 0.0))
                dve.wait_ge(gl_act, 3 * l + 2)
                for h in range(4):
                    r = slice(32 * h, 32 * h + 32)
                    dve.scalar_tensor_tensor(out=gl_q[r, h, :], in0=pfm[r, FM_GQ, :], scalar=32.0 ** -0.5,
                                             in1=gl_eq[r, :], op0=ALU.mult, op1=ALU.mult)
                tt_(gl_ek, gl_ek, pfm[:, FM_GK, :], ALU.mult)
                tt_(gl_ke, gl_ke, pfm[:, FM_GK, :], ALU.mult).then_inc(gl_dve, 1)
                dve.wait_ge(gl_pe, 6 * l + 3)
                for tt in range(TT):
                    m = tt_(gl_k8[:, tt, :, :], spread(bank(3)[:, tt * P:(tt + 1) * P], 1, 8),
                            spread(conc("chunk16"), 2, P), ALU.mult)
                m.then_inc(gl_dve, 1)
                for tt in range(TT):
                    tt_(gl_att[:, tt, :, :], bank(1 + tt).rearrange("p (h t) -> p h t", h=4),
                        spread(conc("gl_causal"), 1, 4), ALU.mult)
                dve.wait_ge(gl_pe, 6 * l + 4)
                for n in range(N_GL - 1):
                    m = dve.scalar_tensor_tensor(out=gl_s[:, n + 1, :], in0=gl_s[:, n, :], scalar=gl_dl[:, n:n + 1],
                                                 in1=bank(4 + n // 8)[:, (n % 8) * HD:(n % 8 + 1) * HD],
                                                 op0=ALU.mult, op1=ALU.add)
                    if n < N_GL - 2:
                        link(m)
                m.then_inc(gl_dve, 1)
                dve.wait_ge(gl_pe, 6 * l + 5)
                link(dve.tensor_copy(gl_o.rearrange("p a b -> p (a b)"), bank(6)))
                tt_(gl_sq, gl_o, gl_o, ALU.mult).then_inc(gl_dve, 1)
                dve.wait_ge(gl_pe, 6 * l + 6)
                rooted(gl_r, dve.tensor_scalar(gl_r.rearrange("p a b -> p (a b)"), bank(7), EPS, None, ALU.add))
                link(tt_(gl_o, gl_o, gl_r, ALU.mult))
                dve.wait_ge(gl_act, 3 * l + 3)
                dve.scalar_tensor_tensor(out=oT[:, 6:8, :], in0=gl_o, scalar=parc(l, "gnorm"), in1=gl_og,
                                         op0=ALU.mult, op1=ALU.mult).then_inc(gl_dve, 1)

            def rwkv(l):
                d = rw_kr.rearrange("p a b c t -> p (a b c) t")
                tt_(d[:, 0:7, 1:SEQ], pfm[:, 0:7, 0:SEQ - 1], pfm[:, 0:7, 1:SEQ], ALU.subtract)
                link(dve.tensor_scalar(d[:, 0:7, 0:1], pfm[:, 0:7, 0:1], -1.0, None, ALU.mult))
                for cc in range(7):
                    m = dve.scalar_tensor_tensor(out=pfm[:, cc, :], in0=d[:, cc, :], scalar=parc(l, "mu", cc),
                                                 in1=pfm[:, cc, :], op0=ALU.mult, op1=ALU.add)
                m.then_inc(rw_dve, 1)
                dve.wait_ge(rw_dve, 7 * l + 1)
                r, k, v = (pfm[:, a:a + 2, :] for a in (FM_R, FM_K, FM_V))
                for s, t in ((rw_kr[64:128, :, 0, :, :], 0), (rw_kr[0:64, :, 1, :, :], 0)):
                    dve.memset(s, 0.0)
                for t in (rw_km, rw_bm):
                    dve.memset(t[64:128, :, 0, :, :], 0.0)
                    dve.memset(t[0:64, :, 1, :, :], 0.0)
                link(dve.memset(rw_s[:, 0, :, :], 0.0))
                for hp in range(2):
                    link(dve.tensor_scalar(rw_kk[:, hp, :], k[:, hp, :], parc(l, "k_k", hp), None, ALU.mult))
                dve.wait_ge(rw_act, 8 * l + 2)
                link(dve.tensor_scalar(rw_lw, rw_lw, -float(np.exp(-0.5)), None, ALU.mult))
                link(dve.tensor_tensor_scan(rw_cl.rearrange("p a b -> p (a b)"), conc("reset64"),
                                            rw_lw.rearrange("p a b -> p (a b)"), 0.0, ALU.mult, ALU.add))
                tt_(rw_clm, rw_cl, rw_lw, ALU.subtract).then_inc(rw_dve, 1)
                tt_(rw_sq, rw_kk, rw_kk, ALU.mult).then_inc(rw_dve, 1)
                if l == 0:
                    dve.tensor_copy(v_first[:, :, :], v)
                else:
                    link(tt_(rw_bonus, v_first[:, :, :], v, ALU.subtract))
                    link(tt_(rw_bonus, rw_bonus, rw_vg, ALU.mult))
                    link(tt_(v, v, rw_bonus, ALU.add))
                for hp in range(2):
                    link(dve.tensor_scalar(rw_k2[:, hp, :], rw_a[:, hp, :], -1.0, parc(l, "k_a", hp),
                                           ALU.add, ALU.mult))
                link(dve.scalar_tensor_tensor(out=rw_k2, in0=rw_k2, scalar=1.0, in1=k, op0=ALU.add, op1=ALU.mult))
                dve.wait_ge(rw_pe, 7 * l + 2)
                nrm = rw_bt
                rooted(nrm, dve.tensor_scalar(nrm.rearrange("p a b -> p (a b)"), bank(4), 64.0, 1e-24,
                                          ALU.mult, ALU.max))
                link(tt_(rw_kk, rw_kk, nrm, ALU.mult))
                link(tt_(rw_a, rw_kk, rw_a, ALU.mult))
                dve.wait_ge(rw_act, 8 * l + 3)
                for h2 in range(2):
                    rr = slice(64 * h2, 64 * h2 + 64)
                    tt_(rw_kr[rr, :, h2, 0, :], rw_kk[rr], rw_clm[rr], ALU.mult)
                    tt_(rw_kr[rr, :, h2, 1, :], r[rr], rw_ep[rr], ALU.mult)
                tt_(rw_bt, rw_a, rw_em, ALU.mult)
                tt_(rw_kt, rw_k2, rw_em, ALU.mult)
                for hp in range(2):
                    m = dve.scalar_tensor_tensor(out=rw_rk[:, hp, :], in0=r[:, hp, :], scalar=parc(l, "r_k", hp),
                                                 in1=rw_k2[:, hp, :], op0=ALU.mult, op1=ALU.mult)
                m.then_inc(rw_dve, 1)
                for which, dst in ((0, rw_ab), (1, rw_ak)):
                    dve.wait_ge(rw_pe, 7 * l + 3 + which)
                    if which == 1:
                        dve.wait_ge(rw_act, 8 * l + 5)
                    mask = conc("rw_k" if which else "rw_b").rearrange("p (a t) -> p a t", a=2)
                    for tt in range(TT):
                        for hp in range(2):
                            m = tt_(dst[:, tt, hp], bank(2 * tt + hp).rearrange("p (a b t) -> p a b t", a=2, b=2),
                                    spread(mask, 1, 2), ALU.mult)
                    m.then_inc(rw_dve, 1)
                dve.tensor_copy(rw_x, spread(ident, 1, 8))
                dve.memset(rw_z, 0.0)
                dve.memset(rw_u, 0.0)
                dve.tensor_copy(rw_xt, spread(ident, 1, 8)).then_inc(inv_dve, 1)
                for j in range(6):
                    dve.wait_ge(inv_pe, 12 * l + 2 * j + 1)
                    mask = spread(conc("level", j * P, P), 1, 8)
                    tt_(rw_t1, bank(0, 2).rearrange("p (q t) -> p q t", q=8), mask, ALU.mult).then_inc(inv_dve, 1)
                    dve.wait_ge(inv_pe, 12 * l + 2 * j + 2)
                    tt_(rw_x, rw_x, bank(2, 2).rearrange("p (q t) -> p q t", q=8), ALU.add)
                    tt_(rw_xt, rw_xt, bank(6, 2).rearrange("p (q t) -> p q t", q=8), ALU.add).then_inc(inv_dve, 1)
                for ch in range(4):
                    rows = slice(64 * (ch % 2), 64 * (ch % 2) + 64)
                    dve.wait_ge(seq_pe, 16 * l + 4 * ch + 1)
                    dve.tensor_copy(rw_z[rows, :], bank(0)[rows, 0:256]).then_inc(seq_dve, 1)
                    dve.wait_ge(seq_pe, 16 * l + 4 * ch + 2)
                    dve.tensor_copy(rw_u[rows, :], bank(1)[rows, 0:256]).then_inc(seq_dve, 1)
                    dve.wait_ge(seq_pe, 16 * l + 4 * ch + 3)
                    new = rw_s[:, (ch + 1) % 2, :, :]
                    for h2 in range(2):
                        rr = slice(64 * h2, 64 * h2 + 64)
                        src = bank(3)[rr, 0:256].rearrange("p (a b) -> p a b", a=2)[:, :, h2 * HD:(h2 + 1) * HD]
                        m = tt_(new[rr], rw_s[rr, ch % 2, :, :], src, ALU.add)
                    link(m)
                    dec = rw_ep[:, :, ch * C_RW + C_RW - 1:ch * C_RW + C_RW].broadcast_to([P, 2, HD])
                    tt_(new, new, dec, ALU.mult).then_inc(seq_dve, 1)
                dve.wait_ge(rw_act, 8 * l + 8)
                link(tt_(rw_yc, rw_y, rw_r, ALU.subtract))
                tt_(rw_y2, rw_yc, rw_yc, ALU.mult).then_inc(rw_dve, 1)
                dve.wait_ge(rw_pe, 7 * l + 7)
                rooted(rw_r, dve.tensor_scalar(rw_r.rearrange("p a b -> p (a b)"), bank(5), GN_EPS, None, ALU.add))
                link(tt_(rw_yc, rw_yc, rw_r, ALU.mult))
                link(dve.scalar_tensor_tensor(out=rw_bonus, in0=rw_bonus, scalar=64.0, in1=v,
                                              op0=ALU.mult, op1=ALU.mult))
                for hp in range(2):
                    m = dve.scalar_tensor_tensor(out=rw_yc[:, hp, :], in0=rw_yc[:, hp, :],
                                                 scalar=parc(l, "ln", hp), in1=rw_bonus[:, hp, :],
                                                 op0=ALU.mult, op1=ALU.add)
                link(m)
                tt_(oT[:, 4:6, :], rw_yc, rw_g, ALU.mult).then_inc(rw_out, 1)

            def merge(l):
                for n in range(32 * l, 32 * l + 32):
                    j, i = (n % 32) // 4, n % 4
                    dve.wait_ge(gate_sig, n + 1)
                    if i == 0:
                        tt_(merged[:, j, :], sig[:, i, :], bank(n % 4)[:, 256:512], ALU.mult).then_inc(gate_used, 1)
                        continue
                    link(tt_(mtmp[:, i, :], sig[:, i, :], bank(n % 4)[:, 256:512], ALU.mult))
                    tt_(merged[:, j, :], merged[:, j, :], mtmp[:, i, :], ALU.add).then_inc(gate_used, 1)
                add_to_x(4, merged_out, l + 1, x_merged)

            def add_to_x(b, sem_, n, done):
                dve.wait_ge(sem_, n)
                for tt in range(TT):
                    m = tt_(x[:, tt, :], x[:, tt, :], bank(b + 2 * tt, 2), ALU.add)
                m.then_inc(done, 1)

            def memory(l):
                pass

            def cross(l):
                dve.wait_ge(caq_done, l + 1)
                dve.memset(qpad[64:128, :, 0, :], 0.0)
                dve.memset(qpad[0:64, :, 1, :], 0.0)
                pad_queries(4, caq_padded)
                for tt in range(TT):
                    shifted(6 * l + 4 + tt, tt, MEM, None)
                for tt in range(TT):
                    output(6 * l + 4 + tt, tt, None)
                add_to_x(0, cao_done, l + 1, x_crossed)

            def hiddens(at, c, up):
                dve.wait_ge(silu_done, up + (c + 1))
                tt_(hidden[:, at % 2, :], silu[:, at % 2, :], bank(4 + at % 2)[:, 256:512], ALU.mult)\
                    .then_inc(hid_ready, 1)

            def ffn(l):
                for f in range(FC):
                    hiddens(LAYER_SLABS + f, f, 0)
                add_to_x(0, down_done, 1, x_added)

            def moe(l):
                dve.wait_ge(routed, 1)
                link(dve.tensor_copy(logit, bank(6)[:, 0:16].rearrange("p (t e) -> p t e", t=2)))
                for tt in range(TT):
                    link(dve.max(top[:, tt, :], logit[:, tt, :]))
                    link(dve.max_index(idx[:, :], top[:, tt, :], logit[:, tt, :]))
                    link(dve.tensor_copy(topi[:, tt, :], idx[:, :]))
                    one, two = (topi[:, tt, s:s + 1].broadcast_to([P, 8]) for s in (0, 1))
                    tt_(picked[:, tt, :], conc("iota", 0, 8), one, ALU.is_equal)
                    link(tt_(pick[:, tt, :], conc("iota", 0, 8), two, ALU.is_equal))
                    link(tt_(picked[:, tt, :], picked[:, tt, :], pick[:, tt, :], ALU.add))
                big_ = top[:, :, 0:1].broadcast_to([P, TT, 8])
                tt_(logit, logit, big_, ALU.subtract).then_inc(top_diff, 1)
                dve.wait_ge(top_exp, 1)
                link(tt_(combine, picked, pick, ALU.mult))
                link(dve.tensor_reduce(stat[:, 44:46], combine, AX, ALU.add))
                link(dve.reciprocal(stat[:, 44:46], stat[:, 44:46]))
                link(tt_(combine, combine, stat[:, 44:46].unsqueeze(2).broadcast_to([P, TT, 8]), ALU.mult))
                dve.wait_ge(placed, 1)
                dve.tensor_copy(load_of[:, :], bank(7)[:, 16:24]).then_inc(load_ready, 1)
                dve.tensor_copy(place, bank(7)[:, 0:16].rearrange("p (t e) -> p t e", t=2))
                link(dve.tensor_scalar(few, bank(7)[:, 16:24], float(P), None, ALU.is_le))
                link(tt_(comb_few, combine, spread(few, 1, TT), ALU.mult))
                link(tt_(comb_many, combine, comb_few, ALU.subtract))
                for e in range(N_EXP + 1):
                    if e < N_EXP:
                        for tt in range(TT):
                            pl = place[:, tt, e:e + 1]
                            if e >= 2:
                                dve.wait_ge(gathered, e - 1)
                            dve.tensor_scalar(sel[:, e % 2, tt, :], conc("iota"), pl, picked[:, tt, e:e + 1],
                                              ALU.is_equal, ALU.mult)
                            m = dve.tensor_scalar(sel_w[:, e % 2, tt, :], conc("iota"), pl,
                                                  comb_few[:, tt, e:e + 1], ALU.is_equal, ALU.mult)
                        m.then_inc(sel_ready, 1)
                    if e >= 1:
                        dve.wait_ge(gathered, e)
                        tt_(h_exp[:, e - 1], bank(2 * ((e - 1) % 2), 2).rearrange("p (k t) -> p k t", k=KC),
                            spread(parc(l, "norm_ffn", 0, 8), 2, P), ALU.mult)
                        dve.tensor_copy(sel_wT[:, e - 1], bank(6 + (e - 1) % 2)[:, 0:256]
                                        .rearrange("p (t s) -> p t s", t=2)).then_inc(gathered_c, 1)
                s0 = FIRST_SLAB[1] + LAYER_SLABS
                with dve.Fori(0, N_EXP // 2) as i:
                    for half in range(2):
                        for f in range(FC):
                            hiddens(s0 + FC * half + f, FC * (1 + half) + f, i * (2 * FC))
                        dve.wait_ge(down_done, i * 2 + (2 + half))
                        dve.wait_ge(x_added, i * 2 + (1 + half))
                        dve.tensor_copy(y_exp[:, bass.ds(i * 2 + half, 1), :].rearrange("p e d -> p (e d)"),
                                        bank(0, 2))
                        for tt in range(TT):
                            w = comb_many[:, tt, bass.ds(i * 2 + half, 1)]
                            m = dve.scalar_tensor_tensor(out=x[:, tt, :], in0=bank(2 * tt, 2), scalar=w,
                                                         in1=x[:, tt, :], op0=ALU.mult, op1=ALU.add)
                        m.then_inc(x_added, 1)
                add_to_x(0, scattered, 1, x_moe)

            def final(l):
                dve.wait_ge(fin_sq, TT)
                rstd_of(stat[:, 0:2], 1.0 / D, EPS)
                dve.wait_ge(gain_loaded, 16)
                for tt in range(TT):
                    m = dve.scalar_tensor_tensor(out=fin_x[:, tt, :], in0=x[:, tt, :], scalar=stat[:, tt:tt + 1],
                                                 in1=fin_gain, op0=ALU.mult, op1=ALU.mult)
                m.then_inc(fin_ready, 1)

            steps = dict(norm=norm, project=project, nsa=nsa, pool=pool, gla=gla, rwkv=rwkv, merge=merge,
                         memory=memory, cross=cross, ffn=ffn, moe=moe, final=final)
            dve.wait_ge(loads, 80)
            rope_tables()
            for step, l in PLAN:
                steps[step](l)


def constants():
    con = np.zeros((P, N_CON), np.float32)

    def put(name, a):
        a = np.asarray(a, np.float64).reshape(P, -1)
        assert a.shape[1] == CON_COLS[name], (name, a.shape)
        con[:, CON[name]:CON[name] + a.shape[1]] = a

    p = np.arange(P)
    t = np.arange(P)
    s256 = np.arange(256)
    put("ident", np.eye(P))
    q = p[:, None] + P * np.arange(2)[None, :]
    put("causal", np.where(s256[None, None, :] <= q[:, :, None], 0.0, NEG))
    end = np.arange(N_CMP) * CMP_STRIDE + CMP_LEN - 1
    ok = end[None, None, :] <= q[:, :, None]
    put("cmp_add", np.where(ok, 0.0, NEG))
    put("cmp_keep", ok)
    levels = []
    for j in range(6):
        b = 1 << j
        row, col = p[:, None], t[None, :]
        levels.append((row // (2 * b) == col // (2 * b)) & (row % (2 * b) >= b) & (col % (2 * b) < b))
    put("level", np.stack(levels, 1))
    s, tc = p[:, None], t[None, :]
    same = s // C_RW == tc // C_RW
    both = np.stack([same & (s < tc), same & (s <= tc)], 1).astype(float)
    put("rw_b", -both)
    put("rw_k", both)
    put("gl_causal", (s // C_GL == tc // C_GL) & (s <= tc))
    tab = []
    for w in (2, 4, 8, 16):
        tq, sq = np.arange(256)[None, :], np.arange(256)[:, None]
        m = ((sq <= tq) & (sq > tq - w)) / np.minimum(tq + 1, w) - (sq == tq)
        tab += [m[0:P, :], m[P:, P:]]
    put("pool", np.concatenate(tab, 1))
    put("reset64", np.tile((np.arange(512) % C_RW != 0)[None], (P, 1)))
    put("reset16", np.tile((np.arange(256) % C_GL != 0)[None], (P, 1)))
    put("ones", (p[:, None] // 64 == t[None, :] // 64) / 64.0)
    put("chunk16", p[:, None] // C_GL == np.arange(8)[None, :])
    inv = (np.float32(500000.0) ** (-np.arange(0, 16, 2, dtype=np.float32) / np.float32(16))).astype(np.float32)
    put("freq", np.tile(inv[None], (P, 1)))
    put("iota", np.tile(np.arange(P)[None], (P, 1)))
    put("before", p[:, None] < t[None, :])
    put("every", np.ones((P, P)))
    return con


def lay_out(a):
    f = np.float32

    def blocks(w):
        return w.reshape(-1, P, w.shape[1]).transpose(1, 0, 2).reshape(P, -1)

    stream = np.zeros((N_SLABS, P, SLAB), f)
    params = np.zeros((DEPTH, P, N_PAR), f)
    mixw = np.zeros((DEPTH, P, N_MIX), f)
    nsa, rw, gl = 0, 1292, 2188
    for l in range(DEPTH):
        w = a["w_in"][l]
        q = w[:, 0:256].reshape(D, 2, 2, HD).transpose(0, 2, 1, 3).reshape(D, 256)
        tm = np.concatenate([q, w[:, 512:640], w[:, 768:896], w[:, 256:512], w[:, 640:768],
                             w[:, 896:1024], w[:, 1036:1292], w[:, gl + 256:gl + 512]], 1)
        s0 = FIRST_SLAB[l]
        for s in range(N_TM):
            stream[s0 + s] = blocks(tm[:, s * 384:(s + 1) * 384])
        misc = np.zeros((D, P), f)
        misc[:, 0:16] = w[:, gl + 512:gl + 528]
        if l:
            misc[:, MISC_V1:MISC_V1 + 32] = a["rwkv_v1"][l - 1]
        misc[:, MISC_GATES:MISC_GATES + 12] = w[:, 1024:1036]
        fm = np.concatenate([w[:, rw:rw + 896], w[:, gl:gl + 256], w[:, gl + 528:gl + 784], misc], 1)
        for ch in range(12):
            stream[s0 + N_TM + ch // 3][:, (ch % 3) * OCT:(ch % 3 + 1) * OCT] = blocks(fm[:, ch * P:(ch + 1) * P])

        def put(o, block):
            stream[s0 + N_TM + N_FM + o // 3][:, (o % 3) * OCT:(o % 3 + 1) * OCT] = block

        for j in range(2):
            w1 = a["nsa_cmp_w1"][l, j].reshape(2 * D, P)
            for half in range(2):
                put(O_CMP + 2 * j + half, blocks(w1[half * D:(half + 1) * D]))
        for j in range(KC):
            put(O_MERGE + 5 * j, blocks(a["w_branch"][l, :, :, j * P:(j + 1) * P].reshape(D, P)))
            for i in range(N_BR):
                put(O_MERGE + 5 * j + 1 + i, blocks(a["w_gate"][l, i][:, j * P:(j + 1) * P]))
            put(O_OUT + j, a["w_out"][l, j * P:(j + 1) * P])
        kv = a["w_ca_kv"][l]
        for cc in range(2):
            put(O_KV + cc, blocks(kv[:, cc * P:(cc + 1) * P]))
            put(O_KV + 2 + cc, blocks(kv[cc * 512:(cc + 1) * 512, 256:512]))
            put(O_CQ + cc, blocks(a["w_ca_q"][l][:, cc * P:(cc + 1) * P]))
            put(O_CO + cc, a["w_ca_o"][l, cc * P:(cc + 1) * P])

        def small(name, v):
            v = v.reshape(-1, P).T
            params[l][:, PAR[name]:PAR[name] + v.shape[1]] = v

        small("norm_mix", a["norm_mix"][l])
        small("norm_ca", a["norm_ca"][l])
        small("norm_ffn", a["norm_ffn"][l])
        small("mem_norm", a["mem_norm"])
        small("b_gate", a["b_gate"][l])
        small("pool_scale", a["pool_scale"][l])
        small("mu", a["rwkv_mu"][l])
        for name, key in (("w0", "rwkv_w0"), ("a0", "rwkv_a0"), ("k_k", "rwkv_k_k"), ("k_a", "rwkv_k_a"),
                          ("r_k", "rwkv_r_k"), ("ln", "rwkv_ln"), ("ab", "gla_ab")):
            small(name, a[key][l])
        if l:
            small("v0", a["rwkv_v0"][l - 1])
            params[l][:, PAR["router"]:PAR["router"] + 64] = blocks(a["moe_router"][0])
        small("gnorm", np.concatenate([a["gla_norm"][l]] * 2))
        small("pe", a["nsa_cmp_pe"][l])

        def mix(name, rows, v, at=0):
            mixw[l][rows, MIX[name] + at:MIX[name] + at + v.shape[1]] = v

        mix("w2", slice(0, 32), a["rwkv_w2"][l])
        mix("a2", slice(32, 64), a["rwkv_a2"][l])
        mix("g2", slice(64, 128), a["rwkv_g2"][l])
        if l:
            mix("v2", slice(MISC_V1, MISC_V1 + 32), a["rwkv_v2"][l - 1])
        mix("gla_a2", slice(0, 16), a["gla_a2"][l])
        for g in range(4):
            mix("pool", slice(64 * (g % 2), 64 * (g % 2) + 64), a["pool_w"][l, g], P * (g // 2) + 64 * (g % 2))
        for j in range(2):
            mix("cmp", slice(0, P), a["nsa_cmp_w2"][l, j], j * HD)

    def feed(s0, wg, wu, wd):
        dst = stream[s0:s0 + FC].reshape(FC, P, 3, KC, P)
        dst[:, :, 0] = wg.reshape(KC, P, FC, P).transpose(2, 1, 0, 3)
        dst[:, :, 1] = wu.reshape(KC, P, FC, P).transpose(2, 1, 0, 3)
        dst[:, :, 2] = wd.reshape(FC, P, KC, P)

    feed(LAYER_SLABS, a["ffn_w_gate"][0], a["ffn_w_up"][0], a["ffn_w_down"][0])
    for e in range(N_EXP):
        feed(FIRST_SLAB[1] + LAYER_SLABS + FC * e, a["moe_w_gate"][0, e], a["moe_w_up"][0, e],
             a["moe_w_down"][0, e])
    pos = a["positions"].reshape(SEQ)
    positions = np.zeros((P, 3), pos.dtype)
    positions[:, 0:2] = pos.reshape(TT, P).T
    positions[0:N_CMP, 2] = pos[CMP_LEN - 1::CMP_STRIDE]
    return {
        "stream": stream, "params": params, "mixw": mixw, "consts": constants(),
        "x_in": np.ascontiguousarray(a["x"].reshape(TT, P, D).transpose(1, 0, 2)),
        "mem_in": np.ascontiguousarray(a["mem"].reshape(TT, P, D).transpose(1, 0, 2)),
        "pos_in": positions,
        "gain_in": np.ascontiguousarray(np.broadcast_to(a["norm_final"][None], (P, D))),
    }


def kernel(**inputs):
    import concourse.bacc as bacc
    from concourse.bass_utils import run_bass_kernel_spmd as run

    arrays = lay_out({k: np.asarray(v) for k, v in inputs.items()})
    nc = bacc.Bacc("TRN2", target_bir_lowering=False, num_devices=1)
    args = [nc.dram_tensor(n, list(v.shape), mybir.dt.from_np(v.dtype), kind="ExternalInput").ap()
            for n, v in arrays.items()]
    out = nc.dram_tensor("out", [P, TT, D], F32, kind="ExternalOutput").ap()
    trunk(nc, *args, out)
    r = run(nc, [arrays], core_ids=[0])
    return r.results[0]["out"].transpose(1, 0, 2).reshape(1, SEQ, D)
```

```python
from contextlib import ExitStack

import numpy as np

import concourse.bass as bass
from concourse import mybir

F32 = mybir.dt.float32
F32R = mybir.dt.float32r
I32 = mybir.dt.int32
U32 = mybir.dt.uint32
ALU = mybir.AluOpType
ACT = mybir.ActivationFunctionType
AX = mybir.AxisListType.X

P = 128
DEPTH, D, SEQ, MEM = 2, 1024, 256, 256
KC = D // P
TT = SEQ // P
HD = 64
W_BR = 256
N_BR = 4
DFF, N_EXP = 2816, 8
FC = DFF // P
EPS, GN_EPS = 1e-6, 64e-5
NEG = -1e30
CMP_LEN, CMP_STRIDE = 32, 16
N_CMP = (SEQ - CMP_LEN) // CMP_STRIDE + 1
ROPE_HALF = 8
C_RW = 64
C_GL = 16
N_GL = SEQ // C_GL

OCT = 8 * P
SLAB = 3 * OCT
RING = 4
ARENA = 17000
FFN_ARENA = 14976
N_TM, N_FM = 4, 4
FM_FIRST = 3
N_EARLY = 6
O_CMP = 0
O_GATE = 4
O_MERGE = O_GATE + N_BR * N_EARLY
O_OUT = O_MERGE + N_EARLY + (N_BR + 1) * (KC - N_EARLY)
O_KV, O_CQ, O_CO = O_OUT + 8, O_OUT + 12, O_OUT + 14
N_OCT = O_CO + 2
LAYER_SLABS = N_TM + N_FM + N_OCT // 3
FIRST_SLAB = [0, LAYER_SLABS + FC]
N_SLABS = 2 * LAYER_SLABS + FC * (1 + N_EXP)

TM_Q, TM_KS, TM_KW, TM_KC, TM_VC, TM_VS, TM_VW, TM_POOL, TM_GV, TM_END = (
    0, 256, 384, 512, 640, 768, 896, 1024, 1280, 1536)
FM_R, FM_K, FM_V, FM_LR, FM_MISC, FM_GQ, FM_GK, FM_OG = 0, 2, 4, 6, 7, 8, 9, 10
MISC_V1, MISC_GATES = 32, 64

PAR_COLS = dict(norm_mix=8, norm_ca=8, norm_ffn=8, mem_norm=8, b_gate=32, pool_scale=2, mu=7, w0=2, a0=2,
                k_k=2, k_a=2, r_k=2, ln=2, v0=2, ab=1, gnorm=1, pe=32, router=64)
PAR = {}
for _n, _c in PAR_COLS.items():
    PAR[_n] = sum(PAR_COLS[m] for m in list(PAR_COLS)[:len(PAR)])
N_PAR = sum(PAR_COLS.values())
MIX_COLS = dict(w2=256, a2=256, g2=256, v2=256, gla_a2=128, pool=256, cmp=128)
MIX = {}
for _n, _c in MIX_COLS.items():
    MIX[_n] = sum(MIX_COLS[m] for m in list(MIX_COLS)[:len(MIX)])
N_MIX = sum(MIX_COLS.values())
CON_COLS = dict(ident=128, causal=512, cmp_add=2 * N_CMP, cmp_keep=2 * N_CMP, level=6 * 128, rw_b=256, rw_k=256,
                gl_causal=128, pool=4 * 384, reset64=512, reset16=256, ones=128, chunk16=8, freq=8, iota=128, before=128, every=128)
CON = {}
for _n, _c in CON_COLS.items():
    CON[_n] = sum(CON_COLS[m] for m in list(CON_COLS)[:len(CON)])
N_CON = sum(CON_COLS.values())

PLAN = [("norm", 0)]
for _l in range(DEPTH):
    PLAN += [("norm", 1 + 3 * _l), ("project", _l), ("rwkv", _l), ("nsa", _l), ("pool", _l), ("gla", _l),
             ("merge", _l), ("memory", _l), ("norm", 2 + 3 * _l), ("cross", _l), ("norm", 3 + 3 * _l),
             ("ffn", _l) if _l == 0 else ("moe", _l)]
PLAN += [("final", 0)]


def slabs_of(plan):
    n = 0
    for step, l in plan:
        f = FIRST_SLAB[min(l, 1)]
        n = {"project": f + 3, "rwkv": f + 8, "nsa": f + 8 + O_GATE // 3 + 6, "gla": f + 8 + O_MERGE // 3 + 1,
             "merge": f + 8 + O_KV // 3 + 1, "memory": f + 8 + 19, "cross": f + 8 + 20,
             "ffn": FIRST_SLAB[1], "moe": N_SLABS}.get(step, n)
    return n


def trunk(nc, stream, params, mixw, consts, x_in, mem_in, pos_in, gain_in, out):
    n_slabs = slabs_of(PLAN)
    with ExitStack() as ctx:
        def sb(name, shape, dt=F32):
            return ctx.enter_context(nc.sbuf_tensor(name, shape, dt))

        def sem(name):
            return ctx.enter_context(nc.semaphore(name))

        ring = sb("ring", [P, RING, SLAB])
        x = sb("x", [P, TT, D])
        hT = sb("hT", [P, KC, SEQ])
        n_ptm, n_pfm = TT * (TM_END + 12), 12 * SEQ
        big = sb("big", [P, n_ptm + n_pfm + KC * MEM])
        ptm = big[:, 0:n_ptm].rearrange("p (t c) -> p t c", t=TT)
        pfm = big[:, n_ptm:n_ptm + n_pfm].rearrange("p (c t) -> p c t", c=12)
        memT = big[:, n_ptm + n_pfm:].rearrange("p (k t) -> p k t", k=KC)
        y_exp = big[:, 0:N_EXP * D].rearrange("p (e d) -> p e d", e=N_EXP)
        v_first = sb("v_first", [P, 2, SEQ])
        par = sb("par", [P, DEPTH, N_PAR])
        mw = sb("mw", [P, N_MIX])
        con = sb("con", [P, N_CON])
        pos = sb("pos", [P, 3], I32)
        trig = sb("trig", [P, 2, 3, ROPE_HALF])
        stat = sb("stat", [P, 64])
        idx = sb("idx", [P, 8], U32)
        load_of = sb("load_of", [P, N_EXP], I32)
        with ExitStack() as shared:
            arena = shared.enter_context(nc.sbuf_tensor("arena", [P, ARENA], F32))
            oT = shared.enter_context(nc.sbuf_tensor("oT", [P, 2 * N_BR, SEQ], F32))
        sb("arena_kept", [P, FFN_ARENA])
        down_w = sb("down_w", [P, 2, 2, D], F32R)
        hid = sb("hid", [P, 2, 2, SEQ], F32R)
        ps = ctx.enter_context(nc.psum_tensor("ps", [P, 8 * 512], F32))

        def bank(b, n=1):
            return ps[:, b * 512:(b + n) * 512]

        class Carve:

            def __init__(self, at=0):
                self.at = at

            def __call__(self, *shape):
                n = int(np.prod(shape))
                v = arena[:, self.at:self.at + n]
                self.at += n
                assert self.at <= ARENA, self.at
                names = "abcde"[:len(shape)]
                if len(shape) == 1:
                    return v
                return v.rearrange("p (" + " ".join(names) + ") -> p " + " ".join(names),
                                   **dict(zip(names, shape)))

        def parc(l, name, i=0, n=1):
            c = PAR[name] + i
            return par[:, l, c:c + n]

        def conc(name, a=0, n=None):
            c = CON[name] + a
            return con[:, c:c + (CON_COLS[name] - a if n is None else n)]

        def mixc(name, a=0, n=128):
            return mw[:, MIX[name] + a:MIX[name] + a + n]

        def spread(ap, axis, n):
            v = ap.unsqueeze(axis)
            shape = list(v.shape)
            shape[axis] = n
            return v.broadcast_to(shape)

        ident = conc("ident")

        c = Carve()
        xn = c(TT, D)
        mem_sb = c(TT, D)

        c = Carve()
        qpad = c(2, 2, SEQ)
        kT = c(2, SEQ)
        prob = c(2, 4, SEQ)
        probT = c(8, P)
        att_tmp = c(4, HD)
        o_tm = c(TT, 4, HD)
        kc2 = c(2, 2, SEQ)
        hid_c = c(2, 2 * N_CMP)
        hid_pe = c(2)
        k_cmp = c(2, HD)
        v_cmp = c(2, HD)
        kcT = c(N_CMP)
        cprob = c(2, 4, N_CMP)
        cprobT = c(8, P)
        rope_a, rope_b, rope_c, rope_d = (c(2, 8, 8) for _ in range(4))
        gates = c(TT, 12)
        kc_dup = c(TT, 4, 2, HD)
        ca_oT = c(2, SEQ)

        c = Carve(ARENA - N_BR * N_EARLY * SEQ)
        early = c(N_EARLY, N_BR, SEQ)

        c = Carve(12000)
        ca_k = c(2, SEQ)
        ca_v = c(2, W_BR)

        c = Carve()
        poolT = c(2, SEQ)

        c = Carve()
        gl_z, gl_e, gl_b, gl_eq, gl_ek, gl_ke = (c(SEQ) for _ in range(6))
        gl_dl = c(N_GL)
        gl_q = c(4, SEQ)
        gl_att = c(TT, 4, P)
        gl_k8 = c(TT, 8, P)
        gl_s = c(N_GL, HD)
        gl_o = c(2, SEQ)
        gl_sq = c(2, SEQ)
        gl_r = c(2, SEQ)
        gl_og = c(2, SEQ)

        c = Carve()
        rw_kr = c(2, 2, 2, SEQ)
        rw_ab = c(TT, 2, 2, 2, P)
        rw_ak = c(TT, 2, 2, 2, P)
        rw_km = c(TT, 2, 2, P)
        rw_bm = c(TT, 2, 2, P)
        rw_ep, rw_g, rw_bt, rw_kt, rw_rk, rw_bonus = (c(2, SEQ) for _ in range(6))
        rw_s = c(2, 2, HD)
        rw_lrx = c(SEQ)
        work = c.at
        rw_lw, rw_cl, rw_clm, rw_em, rw_kk, rw_sq, rw_a, rw_k2 = (c(2, SEQ) for _ in range(8))
        c = Carve(work)
        rw_x = c(8, P)
        rw_xt = c(8, P)
        rw_t1 = c(8, P)
        rw_v = c(TT, W_BR)
        rw_z = c(W_BR)
        rw_u = c(W_BR)
        c = Carve(work)
        rw_y, rw_yc, rw_y2, rw_r = (c(2, SEQ) for _ in range(4))
        rw_top = work + 8 * 512
        c = Carve(rw_top)
        rw_vg = c(2, SEQ)

        c = Carve()
        merged = c(KC, SEQ)
        sig = c(4, SEQ)
        mtmp = c(4, SEQ)
        mtmp2 = c(4, SEQ)
        c = Carve(TT * D)
        silu = c(2, SEQ)
        product = c(2, SEQ)
        combine = c(TT, N_EXP)
        comb_few = c(TT, N_EXP)
        comb_many = c(TT, N_EXP)
        few = c(N_EXP)
        picked = c(TT, N_EXP)
        place = c(TT, N_EXP)
        logit = c(TT, N_EXP)
        top = c(TT, 8)
        topi = c(TT, 8)
        pick = c(TT, N_EXP)
        sel = c(2, TT, P)
        sel_w = c(2, TT, P)
        sel_wT = c(N_EXP, TT, P)
        h_exp = c(N_EXP, KC, P)
        assert c.at <= FFN_ARENA, c.at
        c = Carve()
        fin_gain = c(D)
        fin_x = c(TT, D)

        landed = [sem(f"slab_landed_{i}") for i in range(RING)]
        slab_read = sem("slab_read")
        loads = sem("loads")
        mix_loaded = sem("mix_loaded")
        gain_loaded = sem("gain_loaded")
        stored = sem("stored")
        dve_step = sem("dve_step")
        act_step = sem("act_step")
        root_ready = sem("root_ready")
        root_done = sem("root_done")
        trig_arg = sem("trig_arg")
        trig_done = sem("trig_done")
        squares = sem("squares")
        x_scaled = sem("x_scaled")
        x_turned = sem("x_turned")
        h_ready = sem("h_ready")
        proj_done = sem("proj_done")
        proj_dve = sem("proj_copied_dve")
        proj_act = sem("proj_copied_act")
        roped = sem("roped")
        nsa_turned = sem("nsa_turned")
        q_padded = sem("q_padded")
        kT_copied = sem("kT_copied")
        kc_copied = sem("kc_copied")
        cmp_hidden = sem("cmp_hidden")
        cmp_gelu = sem("cmp_gelu")
        cmp_kv = sem("cmp_kv")
        cmp_kv_copied = sem("cmp_kv_copied")
        cmp_kturned = sem("cmp_kturned")
        cmp_kcopied = sem("cmp_kcopied")
        cmp_scored = sem("cmp_scored")
        cmp_shifted = sem("cmp_shifted")
        cmp_exp = sem("cmp_exp")
        cmp_prob = sem("cmp_prob")
        cmp_pturned = sem("cmp_pturned")
        cmp_pcopied = sem("cmp_pcopied")
        cmp_out = sem("cmp_out")
        cmp_added = sem("cmp_added")
        gates_on = sem("gates_on")
        scored = sem("scored")
        score_max = sem("score_max")
        exped = sem("exped")
        p_turned = sem("p_turned")
        p_copied = sem("p_copied")
        att_out = sem("att_out")
        o_added = sem("o_added")
        o_turned = sem("o_turned")
        o_copied = sem("o_copied")
        pool_d = sem("pool_d")
        pool_dc = sem("pool_dcopied")
        pool_y = sem("pool_y")
        pool_o = sem("pool_o")
        gl_pe = sem("gla_products")
        gl_dve = sem("gla_dve")
        gl_act = sem("gla_act")
        rw_pe = sem("rwkv_products")
        rw_dve = sem("rwkv_dve")
        rw_act = sem("rwkv_act")
        rw_out = sem("rwkv_out")
        inv_pe = sem("inverse_products")
        inv_dve = sem("inverse_dve")
        seq_pe = sem("chunk_products")
        seq_dve = sem("chunk_dve")
        fill_done = sem("late_projections")
        fill_copied = sem("late_projections_copied")
        early_done = sem("early_gate_products")
        early_copied = sem("early_gates_copied")
        early_sig = sem("early_sigmoids")
        branch_done = sem("branch_products")
        branch_used = sem("branches_added")
        gate_done = sem("gate_products")
        gate_sig = sem("gate_sigmoids")
        gate_used = sem("gate_used")
        merged_out = sem("merged_out")
        x_merged = sem("x_merged")
        mem_done = sem("mem_products")
        mem_copied = sem("mem_copied")
        caq_done = sem("caq_done")
        caq_padded = sem("caq_padded")
        cao_done = sem("cao_done")
        x_crossed = sem("x_crossed")
        routed = sem("router_logits")
        top_diff = sem("top_differences")
        top_exp = sem("top_exp")
        placed = sem("places_counted")
        sel_ready = sem("selections_ready")
        gathered = sem("tokens_gathered")
        gathered_c = sem("tokens_copied")
        load_ready = sem("expert_loads_ready")
        scattered = sem("outputs_scattered")
        x_moe = sem("x_moe")
        gu_done = sem("gate_up_done")
        silu_done = sem("silu_done")
        hid_ready = sem("hidden_ready")
        down_split = sem("down_weights_high")
        down_used = sem("down_products")
        x_added = sem("x_added")
        fin_ready = sem("fin_ready")
        fin_sq = sem("fin_squares")

        block = ctx.enter_context(nc.Block())

        @block.sync
        def _(sp):
            sp.dma_start(mem_sb, mem_in).then_inc(loads, 16)
            sp.dma_start(con[:, :], consts).then_inc(loads, 16)
            sp.dma_start(par[:, :, :], params.rearrange("l p c -> p l c")).then_inc(loads, 16)
            sp.dma_start(x[:, :, :], x_in).then_inc(loads, 16)
            sp.dma_start(pos[:, :], pos_in).then_inc(loads, 16)
            sp.dma_start(mw[:, :], mixw[0]).then_inc(mix_loaded, 16)
            for n in range(min(RING, n_slabs)):
                sp.dma_start(ring[:, n, :], stream[n]).then_inc(landed[n], 16)
            rounds = (n_slabs - RING) // RING
            if rounds > 0:
                with sp.Fori(0, rounds) as i:
                    for k in range(RING):
                        sp.wait_ge(slab_read, i * RING + (k + 1))
                        sp.dma_start(ring[:, k, :], stream[i * RING + (RING + k)]).then_inc(landed[k], 16)
            for n in range(RING + rounds * RING, n_slabs):
                sp.wait_ge(slab_read, n - RING + 1)
                sp.dma_start(ring[:, n % RING, :], stream[n]).then_inc(landed[n % RING], 16)
            if PLAN[-1][0] == "final":
                sp.wait_ge(fin_ready, 1)
                sp.dma_start(out, fin_x).then_inc(stored, 16)
                sp.wait_ge(stored, 16)

        @block.tensor
        def _(pe):
            reading = {"slab": -1}

            def mm(o, a, b, start=True, stop=True):
                return pe.matmul(o, a, b, start=start, stop=stop, skip_group_check=True)

            def slab(n):
                if reading["slab"] != n:
                    pe.wait_ge(landed[n % RING], 16 * (n // RING + 1))
                    reading["release"] = reading["slab"] >= 0
                    reading["slab"] = n
                return ring[:, n % RING, :]

            def octet(l, o):
                s = slab(FIRST_SLAB[l] + N_TM + N_FM + o // 3)
                return s[:, (o % 3) * OCT:(o % 3 + 1) * OCT]

            def first(ins):
                if reading.get("release"):
                    ins.then_inc(slab_read, 1)
                    reading["release"] = False

            def turn(o, i, n=P):
                return pe.transpose(o, i, conc("ident")[0:n, 0:n])

            def norm(k):
                for kc in range(KC):
                    for tt in range(TT):
                        if kc == 0:
                            pe.wait_ge(x_scaled, TT * k + tt + 1)
                        t = turn(bank(kc // 2)[:, (kc % 2) * 256 + tt * P:(kc % 2) * 256 + (tt + 1) * P],
                                 xn[:, tt, kc * P:(kc + 1) * P])
                    if kc % 2:
                        t.then_inc(x_turned, 1)

            def project(l):
                pe.wait_ge(h_ready, KC * (2 + 3 * l))
                for b in range(6):
                    if b == 4:
                        w = slab(FIRST_SLAB[l] + 2)[:, OCT:2 * OCT]
                        for tt in range(TT):
                            for kc in range(KC):
                                m = mm(bank(4)[:, tt * 12:(tt + 1) * 12], hT[:, kc, tt * P:(tt + 1) * P],
                                       w[:, kc * P + MISC_GATES:kc * P + MISC_GATES + 12],
                                       kc == 0, kc == KC - 1)
                        m.then_inc(proj_done, 1)
                        continue
                    for ch in ((2 * b, 2 * b + 1) if b < 4 else (8,)):
                        m = fm_chunk(l, ch, bank(b)[:, (ch % 2) * 256:(ch % 2) * 256 + 256])
                    m.then_inc(proj_done, 1)

            def fm_chunk(l, ch, o):
                w = slab(FIRST_SLAB[l] + (ch // 3 if ch < 9 else FM_FIRST + N_TM))
                w = w[:, (ch % 3) * OCT:(ch % 3 + 1) * OCT]
                for kc in range(KC):
                    m = mm(o, w[:, kc * P:(kc + 1) * P], hT[:, kc, :], kc == 0, kc == KC - 1)
                    if kc == 0:
                        first(m)
                return m

            def fill(l, k):
                if k == 0:
                    pe.wait_ge(proj_act, 4 * l + 3)
                else:
                    pe.wait_ge(fill_copied, 10 * l + k)
                if k < 8:
                    w = slab(FIRST_SLAB[l] + FM_FIRST + k // 2).rearrange("p (k c) -> p k c", k=KC)
                    for kc in range(KC):
                        m = mm(bank(4)[:, 0:384], hT[:, kc, (k % 2) * P:(k % 2 + 1) * P], w[:, kc, :],
                               kc == 0, kc == KC - 1)
                        if kc == 0:
                            first(m)
                elif k == 8:
                    fm_chunk(l, 9, bank(4)[:, 0:256])
                    m = fm_chunk(l, 10, bank(4)[:, 256:512])
                else:
                    m = fm_chunk(l, 11, bank(4)[:, 0:256])
                m.then_inc(fill_done, 1)

            def gate(l, g):
                if g:
                    pe.wait_ge(early_copied, N_BR * N_EARLY * l + g)
                w = octet(l, O_GATE + g)
                for kc in range(KC):
                    m = mm(bank(7)[:, 0:256], w[:, kc * P:(kc + 1) * P], hT[:, kc, :], kc == 0, kc == KC - 1)
                    if kc == 0:
                        first(m)
                m.then_inc(early_done, 1)

            def scores(u, tt, keys):
                nk = keys.shape[2]
                for hp in range(2):
                    for h2 in range(2):
                        h = 2 * h2 + hp if u % 6 < 4 else 2 * hp + h2
                        m = mm(bank(2 * (u % 2) + h // 2)[:, (h % 2) * 256:(h % 2) * 256 + nk],
                               qpad[:, hp, h2, tt * P:(tt + 1) * P], keys[:, hp, :])
                m.then_inc(scored, 1)

            def turn_probs(u, nk):
                pe.wait_ge(exped, u + 1)
                for h in range(4):
                    for kb in range(nk // P):
                        m = turn(bank(4, 2)[:, (2 * h + kb) * P:(2 * h + kb + 1) * P],
                                 prob[:, u % 2, h, kb * P:(kb + 1) * P])
                m.then_inc(p_turned, 1)

            def weigh(u, values, nk):
                pe.wait_ge(p_copied, u + 1)
                for h in range(4):
                    for kb in range(nk // P):
                        m = mm(bank(6)[:, h * HD:(h + 1) * HD], probT[:, 2 * h + kb, :],
                               values(h, kb), kb == 0, kb == nk // P - 1)
                m.then_inc(att_out, 1)

            def turn_out(l, which):
                pe.wait_ge(o_added, 6 * l + (4 if which == 0 else 6))
                for cc in range(2):
                    for tt in range(TT):
                        m = turn(bank(0)[:, cc * 256 + tt * P:cc * 256 + (tt + 1) * P],
                                 o_tm[:, tt, 2 * cc:2 * cc + 2, :].rearrange("p a b -> p (a b)"))
                m.then_inc(o_turned, 1)

            def nsa(l):
                pe.wait_ge(roped, l + 1)
                for r in range(2):
                    for tt in range(TT):
                        turn(bank(0)[:, (2 * r + tt) * P:(2 * r + tt + 1) * P],
                             ptm[:, tt, TM_Q + r * P:TM_Q + (r + 1) * P])
                for a, at in enumerate((TM_KS, TM_KW)):
                    for tt in range(TT):
                        turn(bank(1)[:, (2 * a + tt) * P:(2 * a + tt + 1) * P], ptm[:, tt, at:at + P])
                for j in range(2):
                    for g in range(2):
                        for tt in range(TT):
                            m = turn(bank(2 + j)[:, (2 * g + tt) * P:(2 * g + tt + 1) * P],
                                     kc_dup[:, tt, 2 * j + g, :, :].rearrange("p a b -> p (a b)"))
                m.then_inc(nsa_turned, 1)
                pe.wait_ge(kc_copied, l + 1)
                for j in range(2):
                    for lp in range(16):
                        w = octet(l, O_CMP + 2 * j + lp // 8)[:, (lp % 8) * P:(lp % 8 + 1) * P]
                        t = kc2[:, j, :, :].rearrange("p g (m a b) -> p g m a b", a=8, b=2)
                        t = t[:, :, lp // 8:lp // 8 + N_CMP, lp % 8, 0]
                        o = bank(4)[:, j * 32:j * 32 + 2 * N_CMP].rearrange("p (g n) -> p g n", g=2)
                        first(mm(o, w, t, lp == 0, lp == 15))
                        m = mm(bank(5)[:, j:j + 1], w, parc(l, "pe", j * 16 + lp), lp == 0, lp == 15)
                m.then_inc(cmp_hidden, 1)
                gate(l, 0)
                pe.wait_ge(cmp_gelu, 2 * (l + 1))
                for j in range(2):
                    for g in range(2):
                        m = mm(bank(6)[0:N_CMP, (2 * j + g) * HD:(2 * j + g + 1) * HD],
                               hid_c[:, j, g * N_CMP:(g + 1) * N_CMP], mixc("cmp", j * HD, HD))
                m.then_inc(cmp_kv, 1)
                gate(l, 1)
                pe.wait_ge(cmp_kv_copied, l + 1)
                turn(bank(6)[:, 0:N_CMP], k_cmp[0:N_CMP, :, :].rearrange("p a b -> p (a b)"),
                     N_CMP).then_inc(cmp_kturned, 1)
                pe.wait_ge(cmp_kcopied, l + 1)
                pe.wait_ge(q_padded, l + 1)
                for tt in range(TT):
                    for h in range(4):
                        m = mm(bank(5)[:, (4 * tt + h) * N_CMP:(4 * tt + h + 1) * N_CMP],
                               qpad[:, h % 2, h // 2, tt * P:(tt + 1) * P], kcT)
                m.then_inc(cmp_scored, 1)
                pe.wait_ge(kT_copied, l + 1)
                units = [(6 * l, 0, 0), (6 * l + 1, 0, 1), (6 * l + 2, 1, 0), (6 * l + 3, 1, 1)]

                def keys(a, tt):
                    return spread(kT[:, a, 0:P * (tt + 1)], 1, 2)

                def values(a):
                    at = TM_VS if a == 0 else TM_VW
                    return lambda h, kb: ptm[:, kb, at + (h // 2) * HD:at + (h // 2 + 1) * HD]

                scores(units[0][0], units[0][2], keys(units[0][1], units[0][2]))
                gate(l, 2)
                pe.wait_ge(cmp_prob, l + 1)
                for h in range(8):
                    m = turn(bank(4, 2)[0:N_CMP, h * P:(h + 1) * P], cprob[:, h // 4, h % 4, :])
                m.then_inc(cmp_pturned, 1)
                pe.wait_ge(cmp_pcopied, l + 1)
                for h in range(8):
                    m = mm(bank(6)[:, h * HD:(h + 1) * HD], cprobT[0:N_CMP, h, :],
                           v_cmp[0:N_CMP, (h % 4) // 2, :])
                m.then_inc(cmp_out, 1)
                for n, (u, a, tt) in enumerate(units):
                    if n < 3:
                        u2, a2, t2 = units[n + 1]
                        if n >= 1:
                            pe.wait_ge(score_max, u)
                        scores(u2, t2, keys(a2, t2))
                    gate(l, 3 + 3 * n)
                    gate(l, 4 + 3 * n)
                    turn_probs(u, P * (tt + 1))
                    gate(l, 5 + 3 * n)
                    if n == 0:
                        pe.wait_ge(cmp_added, l + 1)
                    else:
                        pe.wait_ge(o_added, u)
                    weigh(u, values(a), P * (tt + 1))
                gate(l, 15)
                turn_out(l, 0)

            def pool(l):
                pe.wait_ge(o_copied, 2 * l + 1)
                for pr in range(2):
                    for g2 in range(2):
                        g = 2 * pr + g2
                        o = bank(5)[g2 * HD:(g2 + 1) * HD, pr * 256:(pr + 1) * 256]
                        for tt in range(TT):
                            u = ptm[:, tt, TM_POOL + g * HD:TM_POOL + (g + 1) * HD]
                            if tt == 0:
                                m = mm(o, u, conc("pool", 384 * g, 256), True, False)
                            else:
                                m = mm(o[:, P:2 * P], u, conc("pool", 384 * g + 256, P), False, True)
                m.then_inc(pool_d, 1)
                gate(l, 16)
                pe.wait_ge(pool_dc, l + 1)
                for pr in range(2):
                    m = mm(bank(6)[:, pr * 256:(pr + 1) * 256], mixc("pool", pr * P), poolT[:, pr, :])
                m.then_inc(pool_y, 1)

            def gla(l):
                pe.wait_ge(pool_o, l + 1)
                mm(bank(0)[:, 0:256], mixc("gla_a2"), pfm[:, FM_MISC, :]).then_inc(gl_pe, 1)
                gate(l, 17)
                gate(l, 18)
                pe.wait_ge(gl_dve, 7 * l + 3)
                for tt in range(TT):
                    m = mm(bank(1 + tt), gl_ek[:, tt * P:(tt + 1) * P], gl_q[:, :, tt * P:(tt + 1) * P])
                m.then_inc(gl_pe, 1)
                for tt in range(TT):
                    m = turn(bank(3)[:, tt * P:(tt + 1) * P], gl_ke[:, tt * P:(tt + 1) * P])
                m.then_inc(gl_pe, 1)
                gate(l, 19)
                pe.wait_ge(gl_dve, 7 * l + 4)
                for tt in range(TT):
                    for h in range(4):
                        for n in range(8):
                            m = mm(bank(4 + tt)[32 * h:32 * h + 32, n * HD:(n + 1) * HD],
                                   gl_k8[:, tt, n, 32 * h:32 * h + 32],
                                   ptm[:, tt, TM_GV + h * HD:TM_GV + (h + 1) * HD])
                m.then_inc(gl_pe, 1)
                gate(l, 20)
                gate(l, 21)
                pe.wait_ge(gl_dve, 7 * l + 5)
                for hp in range(2):
                    for tt in range(TT):
                        for h2 in range(2):
                            h = 2 * hp + h2
                            o = bank(6)[h2 * HD:(h2 + 1) * HD, hp * 256 + tt * P:hp * 256 + (tt + 1) * P]
                            mm(o, ptm[:, tt, TM_GV + h * HD:TM_GV + (h + 1) * HD], gl_att[:, tt, h, :],
                               True, False)
                            for n in range(8):
                                m = mm(o[:, n * C_GL:(n + 1) * C_GL], gl_s[:, 8 * tt + n, :],
                                       gl_q[:, h, tt * P + n * C_GL:tt * P + (n + 1) * C_GL], False, n == 7)
                m.then_inc(gl_pe, 1)
                gate(l, 22)
                pe.wait_ge(gl_dve, 7 * l + 6)
                mm(bank(0), conc("ones"), gl_sq.rearrange("p a b -> p (a b)")).then_inc(gl_pe, 1)
                gate(l, 23)

            def rwkv(l):
                fill(l, 0)
                pe.wait_ge(mix_loaded, 16 * (l + 1))
                pe.wait_ge(rw_act, 8 * l + 1)
                for hp in range(2):
                    mm(bank(0)[:, hp * 256:hp * 256 + 256], mixc("w2", hp * P), rw_lrx)
                    mm(bank(1)[:, hp * 256:hp * 256 + 256], mixc("a2", hp * P), rw_lrx)
                    if l:
                        mm(bank(3)[:, hp * 256:hp * 256 + 256], mixc("v2", hp * P), pfm[:, FM_MISC, :])
                    m = mm(bank(2)[:, hp * 256:hp * 256 + 256], mixc("g2", hp * P), rw_lrx)
                m.then_inc(rw_pe, 1)
                pe.wait_ge(rw_dve, 7 * l + 2)
                mm(bank(5), conc("ones"), rw_sq.rearrange("p a b -> p (a b)")).then_inc(rw_pe, 1)
                for k in range(1, 5):
                    fill(l, k)
                pe.wait_ge(rw_dve, 7 * l + 4)
                mm(bank(5), conc("ones"), rw_rk.rearrange("p a b -> p (a b)"))
                for tt in range(TT):
                    for hp in range(2):
                        i = 2 * tt + hp
                        turn(bank(6)[:, i * P:(i + 1) * P], rw_kt[:, hp, tt * P:(tt + 1) * P])
                        turn(bank(7)[:, i * P:(i + 1) * P], rw_bt[:, hp, tt * P:(tt + 1) * P])
                for tt in range(TT):
                    for hp in range(2):
                        kr = rw_kr[:, hp, :, :, tt * P:(tt + 1) * P].rearrange("p a b t -> p (a b) t")
                        m = mm(bank(2 * tt + hp), rw_bt[:, hp, tt * P:(tt + 1) * P], kr)
                m.then_inc(rw_pe, 1)
                fill(l, 5)
                pe.wait_ge(rw_dve, 7 * l + 5)
                for tt in range(TT):
                    for hp in range(2):
                        kr = rw_kr[:, hp, :, :, tt * P:(tt + 1) * P].rearrange("p a b t -> p (a b) t")
                        m = mm(bank(2 * tt + hp), rw_kt[:, hp, tt * P:(tt + 1) * P], kr)
                m.then_inc(rw_pe, 1)
                pe.wait_ge(rw_dve, 7 * l + 6)
                for tt in range(TT):
                    for hp in range(2):
                        m = turn(bank(5)[:, (2 * tt + hp) * P:(2 * tt + hp + 1) * P],
                                 pfm[:, FM_V + hp, tt * P:(tt + 1) * P])
                m.then_inc(rw_pe, 1)

                for j in range(6):
                    for g in range(2):
                        pe.wait_ge(inv_dve, 25 * l + max(1, 4 * j + g))
                        for q in range(4 * g, 4 * g + 4):
                            m = mm(bank(g)[:, (q % 4) * P:(q % 4 + 1) * P],
                                   rw_ab[:, q // 4, (q // 2) % 2, q % 2, 0, :], rw_x[:, q, :])
                        m.then_inc(inv_pe, 1)
                    for g in range(2):
                        pe.wait_ge(inv_dve, 25 * l + 4 * j + 2 + g)
                        for q in range(4 * g, 4 * g + 4):
                            at = slice((q % 4) * P, (q % 4 + 1) * P)
                            mm(bank(2 + g)[:, at], rw_xt[:, q, :], rw_t1[:, q, :])
                            m = mm(bank(6 + g)[:, at], rw_t1[:, q, :], rw_xt[:, q, :])
                        m.then_inc(inv_pe, 1)
                pe.wait_ge(inv_dve, 25 * (l + 1))

                for ch in range(4):
                    tt, par2 = ch // 2, ch % 2
                    rows = slice(64 * par2, 64 * par2 + 64)
                    tok = slice(ch * C_RW, (ch + 1) * C_RW)
                    if ch == 0:
                        pe.wait_ge(rw_act, 8 * l + 6)
                    else:
                        pe.wait_ge(seq_dve, 12 * l + 3 * ch)
                    for h in range(4):
                        o = bank(0)[rows, h * HD:(h + 1) * HD]
                        mm(o, rw_kr[:, h // 2, h % 2, 0, tok], rw_s[:, ch % 2, h // 2, :], True, False)
                        m = mm(o, rw_ak[:, tt, h // 2, h % 2, 0, rows], rw_v[:, tt, h * HD:(h + 1) * HD],
                               False, True)
                    m.then_inc(seq_pe, 1)
                    pe.wait_ge(seq_dve, 12 * l + 3 * ch + 1)
                    for h in range(4):
                        m = mm(bank(1)[rows, h * HD:(h + 1) * HD], rw_xt[:, 4 * tt + h, rows],
                               rw_z[:, h * HD:(h + 1) * HD])
                    m.then_inc(seq_pe, 1)
                    fill(l, 6 + ch)
                    pe.wait_ge(seq_dve, 12 * l + 3 * ch + 2)
                    for hp in range(2):
                        o = bank(3)[:, hp * P:(hp + 1) * P]
                        mm(o, rw_km[:, tt, par2, hp, :], rw_v[:, tt, hp * P:(hp + 1) * P], True, False)
                        m = mm(o, rw_bm[:, tt, par2, hp, :], rw_u[:, hp * P:(hp + 1) * P], False, True)
                    m.then_inc(seq_pe, 1)
                    for h in range(4):
                        o = bank(2)[(h % 2) * HD:(h % 2 + 1) * HD, (h // 2) * 256 + ch * C_RW:
                                    (h // 2) * 256 + (ch + 1) * C_RW]
                        mm(o, rw_s[:, ch % 2, h // 2, :], rw_kr[:, h // 2, h % 2, 1, tok], True, False)
                        mm(o, rw_v[:, tt, h * HD:(h + 1) * HD], rw_ak[:, tt, h // 2, h % 2, 1, rows],
                           False, False)
                        m = mm(o, rw_u[:, h * HD:(h + 1) * HD], rw_ab[:, tt, h // 2, h % 2, 1, rows],
                               False, True)
                    m.then_inc(seq_pe, 1)
                pe.wait_ge(rw_act, 8 * l + 7)
                mm(bank(0), conc("ones"), rw_y.rearrange("p a b -> p (a b)")).then_inc(rw_pe, 1)
                pe.wait_ge(rw_dve, 7 * l + 7)
                mm(bank(1), conc("ones"), rw_y2.rearrange("p a b -> p (a b)")).then_inc(rw_pe, 1)

            def merge(l):
                pe.wait_ge(o_copied, 2 * l + 1)
                pe.wait_ge(pool_o, l + 1)
                pe.wait_ge(gl_dve, 7 * (l + 1))
                pe.wait_ge(rw_out, l + 1)
                for j in range(N_EARLY):
                    if j >= 2:
                        pe.wait_ge(branch_used, N_EARLY * l + j - 1)
                    w = octet(l, O_MERGE + j)
                    for i in range(N_BR):
                        for kc in range(2):
                            m = mm(bank(2 * (j % 2), 2)[:, i * 256:(i + 1) * 256],
                                   w[:, (2 * i + kc) * P:(2 * i + kc + 1) * P], oT[:, 2 * i + kc, :],
                                   kc == 0, kc == 1)
                            if i == 0 and kc == 0:
                                first(m)
                    m.then_inc(branch_done, 1)
                for j in range(KC - N_EARLY):
                    if j == 1:
                        pe.wait_ge(branch_used, N_EARLY * (l + 1))
                    o = O_MERGE + N_EARLY + j * (N_BR + 1)
                    for i in range(N_BR):
                        b = bank(4 * (1 - j) + i)
                        wb = octet(l, o)
                        for kc in range(2):
                            m = mm(b[:, 256:512], wb[:, (2 * i + kc) * P:(2 * i + kc + 1) * P],
                                   oT[:, 2 * i + kc, :], kc == 0, kc == 1)
                            if kc == 0:
                                first(m)
                    for i in range(N_BR):
                        b = bank(4 * (1 - j) + i)
                        wg = octet(l, o + 1 + i)
                        for kc in range(KC):
                            m = mm(b[:, 0:256], wg[:, kc * P:(kc + 1) * P], hT[:, kc, :], kc == 0, kc == KC - 1)
                            if kc == 0:
                                first(m)
                        m.then_inc(gate_done, 1)
                pe.wait_ge(gate_used, 8 * (l + 1))
                for kc in range(KC):
                    w = octet(l, O_OUT + kc)
                    for tt in range(TT):
                        for nb in range(2):
                            m = mm(bank(4 + 2 * tt + nb), merged[:, kc, tt * P:(tt + 1) * P],
                                   w[:, nb * 512:(nb + 1) * 512], kc == 0, kc == KC - 1)
                            if tt == 0 and nb == 0:
                                first(m)
                m.then_inc(merged_out, 1)

            def memory(l):
                for cc in range(2):
                    w = octet(l, O_KV + cc)
                    for kc in range(KC):
                        m = mm(bank(0)[:, cc * 256:cc * 256 + 256], w[:, kc * P:(kc + 1) * P],
                               memT[:, kc, :], kc == 0, kc == KC - 1)
                        if kc == 0:
                            first(m)
                for mt in range(2):
                    for kc in range(KC):
                        w = octet(l, O_KV + 2 + kc // 4)[:, (kc % 4) * 256:(kc % 4 + 1) * 256]
                        m = mm(bank(1 + mt)[:, 0:256], memT[:, kc, mt * P:(mt + 1) * P], w,
                               kc == 0, kc == KC - 1)
                        if kc % 4 == 0 and mt == 0:
                            first(m)
                m.then_inc(mem_done, 1)
                pe.wait_ge(mem_copied, 2 * (l + 1))

            def cross(l):
                pe.wait_ge(h_ready, KC * (3 + 3 * l))
                for cc in range(2):
                    w = octet(l, O_CQ + cc)
                    for kc in range(KC):
                        m = mm(bank(4)[:, cc * 256:cc * 256 + 256], w[:, kc * P:(kc + 1) * P], hT[:, kc, :],
                               kc == 0, kc == KC - 1)
                        if kc == 0:
                            first(m)
                m.then_inc(caq_done, 1)
                pe.wait_ge(caq_padded, l + 1)
                for tt in range(TT):
                    scores(6 * l + 4 + tt, tt, ca_k)
                for tt in range(TT):
                    turn_probs(6 * l + 4 + tt, MEM)
                    if tt:
                        pe.wait_ge(o_added, 6 * l + 5)
                    weigh(6 * l + 4 + tt, lambda h, kb: ca_v[:, kb, h * HD:(h + 1) * HD], MEM)
                turn_out(l, 1)
                pe.wait_ge(o_copied, 2 * l + 2)
                for kc in range(2):
                    w = octet(l, O_CO + kc)
                    for tt in range(TT):
                        for nb in range(2):
                            m = mm(bank(2 * tt + nb), ca_oT[:, kc, tt * P:(tt + 1) * P],
                                   w[:, nb * 512:(nb + 1) * 512], kc == 0, kc == 1)
                            if tt == 0 and nb == 0:
                                first(m)
                m.then_inc(cao_done, 1)

            def gate_up(at, release, h, width):
                b = bank(4 + at % 2)
                w = ring[:, at % RING, :]
                for half in range(2):
                    for kc in range(KC):
                        m = mm(b[:, half * 256:half * 256 + width],
                               w[:, half * OCT + kc * P:half * OCT + (kc + 1) * P], h[:, kc, 0:width],
                               kc == 0, kc == KC - 1)
                        if release and half == 0 and kc == 0:
                            m.then_inc(slab_read, 1)
                m.then_inc(gu_done, 1)

            def down(f, at, width):
                for tt in range((width + P - 1) // P):
                    n = min(width, P)
                    for a, b in ((0, 0), (1, 0), (0, 1)):
                        for nb in range(2):
                            m = mm(bank(2 * tt + nb)[0:n, :], hid[:, at % 2, a, tt * P:tt * P + n],
                                   down_w[:, at % 2, b, nb * 512:(nb + 1) * 512],
                                   f == 0 and (a, b) == (0, 0), f == FC - 1 and b == 1)
                m.then_inc(down_used, 1)

            def expert(c0, e0, slab0, h, width, up=0, ups=0, upe=0):
                for f in range(FC + 1):
                    if f < FC:
                        pe.wait_ge(landed[(slab0 + f) % RING], ups * 16 + 16 * ((slab0 + f) // RING + 1))
                        if c0 + f >= 2:
                            pe.wait_ge(hid_ready, up + (c0 + f - 1))
                        gate_up(slab0 + f, e0 == 0 and f == 0, h, width)
                    if f >= 1:
                        if f == 1 and e0 >= 1:
                            pe.wait_ge(x_added, upe + e0)
                        pe.wait_ge(hid_ready, up + (c0 + f))
                        down(f - 1, slab0 + f - 1, width)

            def ffn(l):
                pe.wait_ge(h_ready, KC * (4 + 3 * l))
                expert(0, 0, LAYER_SLABS, hT, SEQ)
                reading["slab"] = -1

            def moe(l):
                pe.wait_ge(h_ready, KC * (4 + 3 * l))
                for tt in range(TT):
                    for kc in range(KC):
                        m = mm(bank(6)[:, tt * 8:tt * 8 + 8], hT[:, kc, tt * P:(tt + 1) * P],
                               parc(l, "router", 8 * kc, 8), kc == 0, kc == KC - 1)
                        if tt == 0 and kc == 0:
                            m.then_inc(slab_read, 1)
                m.then_inc(routed, 1)
                pe.wait_ge(top_diff, 1)
                mm(bank(7)[:, 0:8], conc("before"), picked[:, 0, :])
                mm(bank(7)[:, 8:16], conc("every"), picked[:, 0, :], True, False)
                mm(bank(7)[:, 8:16], conc("before"), picked[:, 1, :], False, True)
                mm(bank(7)[:, 16:24], conc("every"), picked[:, 0, :], True, False)
                mm(bank(7)[:, 16:24], conc("every"), picked[:, 1, :], False, True).then_inc(placed, 1)
                for e in range(N_EXP):
                    pe.wait_ge(sel_ready, e + 1)
                    if e >= 2:
                        pe.wait_ge(gathered_c, e - 1)
                    for kc in range(KC):
                        for tt in range(TT):
                            mm(bank(2 * (e % 2), 2)[:, kc * P:(kc + 1) * P], xn[:, tt, kc * P:(kc + 1) * P],
                               sel[:, e % 2, tt, :], tt == 0, tt == 1)
                    for tt in range(TT):
                        m = turn(bank(6 + e % 2)[:, tt * P:(tt + 1) * P], sel_w[:, e % 2, tt, :])
                    m.then_inc(gathered, 1)
                pe.wait_ge(gathered_c, N_EXP)
                pe.wait_ge(load_ready, 1)
                s0 = FIRST_SLAB[1] + LAYER_SLABS
                with pe.Fori(0, N_EXP // 2) as i:
                    for half in range(2):
                        ups = (i * (2 * FC), i * (2 * FC // RING), i * 2)
                        tokens = pe.value_load(load_of[0:1, bass.ds(i * 2 + half, 1)], min_val=0, max_val=SEQ)
                        own = h_exp[:, bass.ds(i * 2 + half, 1), :, :].rearrange("p e k t -> p (e k) t")
                        at = (FC * (1 + half), 1 + half, s0 + FC * half)
                        with pe.If(tokens < P + 1):
                            with pe.If(tokens < 3 * P // 4 + 1):
                                with pe.If(tokens < P // 2 + 1):
                                    expert(*at, own, P // 2, *ups)
                                with pe.Else():
                                    expert(*at, own, 3 * P // 4, *ups)
                            with pe.Else():
                                expert(*at, own, P, *ups)
                        with pe.Else():
                            expert(*at, hT, SEQ, *ups)
                pe.wait_ge(x_added, 1 + N_EXP)
                for e in range(N_EXP):
                    for tt in range(TT):
                        for nb in range(2):
                            m = mm(bank(2 * tt + nb), sel_wT[:, e, tt, :], y_exp[:, e, nb * 512:(nb + 1) * 512],
                                   e == 0, e == N_EXP - 1)
                m.then_inc(scattered, 1)

            def final(l):
                pass

            steps = dict(norm=norm, project=project, nsa=nsa, pool=pool, gla=gla, rwkv=rwkv, merge=merge,
                         memory=memory, cross=cross, ffn=ffn, moe=moe, final=final)
            pe.wait_ge(loads, 80)
            for step, l in PLAN:
                steps[step](l)

        @block.scalar
        def _(act):
            n_step = [0]

            def link(ins):
                n_step[0] += 1
                ins.then_inc(act_step, 1)
                act.wait_ge(act_step, n_step[0])

            n_root = [0]

            def root(a):
                n_root[0] += 1
                act.wait_ge(root_ready, n_root[0])
                act.activation(a, a, ACT.Sqrt).then_inc(root_done, 1)

            def norm(k):
                if k > 0:
                    l = (k - 1) // 3
                    if (k - 1) % 3 == 1:
                        act.wait_ge(x_merged, l + 1)
                    elif (k - 1) % 3 == 2:
                        act.wait_ge(x_crossed, l + 1)
                    elif l > 0:
                        act.wait_ge(x_added, 1)
                src = mem_sb if k == 0 else x
                for tt in range(TT):
                    act.activation(xn[:, tt, :], src[:, tt, :], ACT.Square,
                                   accum_out=stat[:, tt:tt + 1]).then_inc(squares, 1)
                root(stat[:, 0:2])
                gain = ("mem_norm", 0) if k == 0 else (("norm_mix", "norm_ca", "norm_ffn")[(k - 1) % 3],
                                                        (k - 1) // 3)
                dst = memT if k == 0 else hT
                for kc in range(KC):
                    act.wait_ge(x_turned, KC // 2 * k + kc // 2 + 1)
                    act.activation(dst[:, kc, :], bank(kc // 2)[:, (kc % 2) * 256:(kc % 2) * 256 + 256],
                                   ACT.Copy, scale=parc(gain[1], gain[0], kc)).then_inc(h_ready, 1)

            def project(l):
                for n, b in enumerate((1, 3, 4, 5)):
                    act.wait_ge(proj_done, 6 * l + b + 1)
                    if b < 4:
                        m = act.copy(pfm[:, 2 * b:2 * b + 2, :].rearrange("p a b -> p (a b)"), bank(b))
                    elif b == 4:
                        m = act.copy(ptm[:, :, TM_END:TM_END + 12],
                                     bank(4)[:, 0:24].rearrange("p (a b) -> p a b", a=2))
                    else:
                        m = act.copy(pfm[:, 8, :], bank(5)[:, 0:256])
                    m.then_inc(proj_act, 1)

            def copy_fill(l, k):
                act.wait_ge(fill_done, 10 * l + k + 1)
                if k < 8:
                    m = act.copy(ptm[:, k % 2, (k // 2) * 384:(k // 2 + 1) * 384], bank(4)[:, 0:384])
                elif k == 8:
                    m = act.copy(pfm[:, 9:11, :].rearrange("p a b -> p (a b)"), bank(4))
                else:
                    m = act.copy(pfm[:, 11, :], bank(4)[:, 0:256])
                m.then_inc(fill_copied, 1)

            def copy_gate(l, g):
                act.wait_ge(early_done, N_BR * N_EARLY * l + g + 1)
                act.activation(early[:, g // N_BR, g % N_BR, :], bank(7)[:, 0:256], ACT.Identity,
                               bias=parc(l, "b_gate", 8 * (g % N_BR) + g // N_BR)).then_inc(early_copied, 1)

            def probs(u, nk):
                act.wait_ge(score_max, u + 1)
                for h in range(4):
                    m = act.activation(prob[:, u % 2, h, 0:nk], prob[:, u % 2, h, 0:nk], ACT.Exp,
                                       bias=stat[:, 8 + 8 * (u % 2) + h:9 + 8 * (u % 2) + h],
                                       accum_out=stat[:, 12 + 8 * (u % 2) + h:13 + 8 * (u % 2) + h])
                m.then_inc(exped, 1)

            def copy_probs(u, nk):
                act.wait_ge(p_turned, u + 1)
                v = bank(4, 2).rearrange("p (h k t) -> p h k t", h=4, k=2)[:, :, 0:nk // P, :]
                o = probT.rearrange("p (h k) t -> p h k t", h=4)[:, :, 0:nk // P, :]
                act.copy(o, v).then_inc(p_copied, 1)

            def nsa(l):
                act.wait_ge(nsa_turned, l + 1)
                act.copy(kT[:, :, :].rearrange("p a b -> p (a b)"), bank(1)).then_inc(kT_copied, 1)
                act.wait_ge(cmp_hidden, l + 1)
                link(act.copy(hid_pe, bank(5)[:, 0:2]))
                for j in range(2):
                    act.activation(hid_c[:, j, :], bank(4)[:, j * 32:j * 32 + 2 * N_CMP], ACT.Gelu_apprx_tanh,
                                   bias=hid_pe[:, j:j + 1]).then_inc(cmp_gelu, 1)
                copy_gate(l, 0)
                act.activation(gates, ptm[:, :, TM_END:TM_END + 12], ACT.Sigmoid).then_inc(gates_on, 1)
                copy_gate(l, 1)
                act.wait_ge(cmp_shifted, l + 1)
                cp = cprob.rearrange("p a b c -> p (a b c)")
                act.activation(cp, cp, ACT.Exp).then_inc(cmp_exp, 1)
                copy_gate(l, 2)
                probs(6 * l, P)
                act.wait_ge(cmp_pturned, l + 1)
                act.copy(cprobT[0:N_CMP, :, :].rearrange("p a b -> p (a b)"),
                         bank(4, 2)[0:N_CMP, :]).then_inc(cmp_pcopied, 1)
                for n in range(4):
                    copy_gate(l, 3 + 3 * n)
                    copy_gate(l, 4 + 3 * n)
                    copy_probs(6 * l + n, P * (n % 2 + 1))
                    if n < 3:
                        probs(6 * l + n + 1, P * ((n + 1) % 2 + 1))
                    copy_gate(l, 5 + 3 * n)
                copy_gate(l, 15)
                act.wait_ge(o_turned, 2 * l + 1)
                act.copy(oT[:, 0:2, :].rearrange("p a b -> p (a b)"), bank(0)).then_inc(o_copied, 1)

            def pool(l):
                copy_gate(l, 16)
                act.wait_ge(pool_y, l + 1)
                for pr in range(2):
                    m = act.activation(oT[:, 2 + pr, :], bank(6)[:, pr * 256:(pr + 1) * 256], ACT.Copy,
                                       scale=parc(l, "pool_scale", pr))
                m.then_inc(pool_o, 1)

            def gla(l):
                act.wait_ge(gl_dve, 7 * l + 1)
                link(act.activation(gl_e, gl_e, ACT.Exp, scale=-1.0))
                act.activation(gl_e, gl_e, ACT.Ln, bias=1.0).then_inc(gl_act, 1)
                copy_gate(l, 17)
                act.wait_ge(gl_dve, 7 * l + 2)
                act.activation(gl_eq, gl_b, ACT.Exp, scale=1.0 / 16)
                act.activation(gl_dl, gl_b[:, C_GL - 1:SEQ:C_GL], ACT.Exp, scale=1.0 / 16)
                act.activation(gl_ek, gl_b, ACT.Exp, scale=-1.0 / 16)
                act.activation(gl_ke, gl_ke, ACT.Exp, scale=1.0 / 16).then_inc(gl_act, 1)
                act.activation(gl_og, pfm[:, FM_OG:FM_OG + 2, :], ACT.Silu).then_inc(gl_act, 1)
                for g in range(18, 23):
                    copy_gate(l, g)
                root(gl_r)
                copy_gate(l, 23)

            def rwkv(l):
                act.wait_ge(rw_dve, 7 * l + 1)
                act.activation(rw_lrx[0:32, :], pfm[0:32, FM_LR, :], ACT.Tanh)
                act.copy(rw_lrx[32:64, :], pfm[32:64, FM_LR, :])
                act.activation(rw_lrx[64:128, :], pfm[64:128, FM_LR, :], ACT.Sigmoid).then_inc(rw_act, 1)
                copy_fill(l, 0)
                act.wait_ge(rw_pe, 7 * l + 1)
                for hp in range(2):
                    at = slice(hp * 256, hp * 256 + 256)
                    act.activation(rw_lw[:, hp, :], bank(0)[:, at], ACT.Sigmoid, bias=parc(l, "w0", hp))
                    act.activation(rw_a[:, hp, :], bank(1)[:, at], ACT.Sigmoid, bias=parc(l, "a0", hp))
                    if l:
                        act.activation(rw_vg[:, hp, :], bank(3)[:, at], ACT.Sigmoid, bias=parc(l, "v0", hp))
                act.copy(rw_g.rearrange("p a b -> p (a b)"), bank(2)).then_inc(rw_act, 1)
                root(rw_bt)
                act.wait_ge(rw_dve, 7 * l + 3)
                act.activation(rw_ep, rw_cl, ACT.Exp)
                act.activation(rw_em, rw_cl, ACT.Exp, scale=-1.0)
                act.activation(rw_clm, rw_clm, ACT.Exp).then_inc(rw_act, 1)
                for k in range(1, 5):
                    copy_fill(l, k)
                act.wait_ge(rw_pe, 7 * l + 3)
                act.copy(rw_bonus.rearrange("p a b -> p (a b)"), bank(5)).then_inc(rw_act, 1)
                for par2 in range(2):
                    r = slice(64 * par2, 64 * par2 + 64)
                    act.mul(rw_bm[r, :, par2, :, :], bank(7)[r, :].rearrange("p (a b c) -> p a b c", a=2, b=2),
                            -1.0)
                    m = act.copy(rw_km[r, :, par2, :, :],
                                 bank(6)[r, :].rearrange("p (a b c) -> p a b c", a=2, b=2))
                m.then_inc(rw_act, 1)
                copy_fill(l, 5)
                act.wait_ge(rw_pe, 7 * l + 5)
                act.wait_ge(inv_dve, 25 * l + 1)
                act.copy(rw_v.rearrange("p a b -> p (a b)"), bank(5)).then_inc(rw_act, 1)
                for k in range(6, 10):
                    copy_fill(l, k)
                act.wait_ge(seq_pe, 16 * (l + 1))
                act.copy(rw_y.rearrange("p a b -> p (a b)"), bank(2)).then_inc(rw_act, 1)
                act.wait_ge(rw_pe, 7 * l + 6)
                act.copy(rw_r.rearrange("p a b -> p (a b)"), bank(0)).then_inc(rw_act, 1)
                root(rw_r)

            def merge(l):
                if l == 0:
                    act.wait_ge(gl_pe, 1)
                    act.dma_start(mw[:, :], mixw[1]).then_inc(mix_loaded, 16)
                act.wait_ge(early_copied, N_BR * N_EARLY * (l + 1))
                for j in range(N_EARLY):
                    act.activation(early[:, j], early[:, j], ACT.Sigmoid).then_inc(early_sig, 1)
                for n in range(N_BR * (KC - N_EARLY)):
                    j, i = n // N_BR, n % N_BR
                    act.wait_ge(gate_done, 8 * l + n + 1)
                    if j:
                        act.wait_ge(gate_used, 8 * l + n - 3)
                    act.activation(sig[:, i, :], bank(4 * (1 - j) + i)[:, 0:256], ACT.Sigmoid,
                                   bias=parc(l, "b_gate", 8 * i + N_EARLY + j)).then_inc(gate_sig, 1)

            def memory(l):
                act.wait_ge(mem_done, l + 1)
                act.copy(ca_k.rearrange("p a b -> p (a b)"), bank(0)).then_inc(mem_copied, 1)
                act.copy(ca_v, bank(1, 2).rearrange("p (a b) -> p a b", a=2)[:, :, 0:256]).then_inc(mem_copied, 1)

            def cross(l):
                for tt in range(TT):
                    probs(6 * l + 4 + tt, MEM)
                for tt in range(TT):
                    copy_probs(6 * l + 4 + tt, MEM)
                act.wait_ge(o_turned, 2 * l + 2)
                act.copy(ca_oT.rearrange("p a b -> p (a b)"), bank(0)).then_inc(o_copied, 1)

            def silus(at, c, up, ups):
                act.wait_ge(landed[at % RING], ups * 16 + 16 * (at // RING + 1))
                if c >= 2:
                    act.wait_ge(down_used, up + (c - 1))
                act.copy(down_w[:, at % 2, 0, :], ring[:, at % RING, 2 * OCT:3 * OCT]).then_inc(down_split, 1)
                act.wait_ge(gu_done, up + (c + 1))
                act.activation(silu[:, at % 2, :], bank(4 + at % 2)[:, 0:256], ACT.Silu).then_inc(silu_done, 1)

            def ffn(l):
                for f in range(FC):
                    silus(LAYER_SLABS + f, f, 0, 0)

            def moe(l):
                act.wait_ge(top_diff, 1)
                act.activation(pick, logit, ACT.Exp).then_inc(top_exp, 1)
                s0 = FIRST_SLAB[1] + LAYER_SLABS
                with act.Fori(0, N_EXP // 2) as i:
                    for f in range(2 * FC):
                        silus(s0 + f, FC + f, i * (2 * FC), i * (2 * FC // RING))

            def final(l):
                act.wait_ge(x_moe, 1)
                act.dma_start(fin_gain, gain_in).then_inc(gain_loaded, 16)
                for tt in range(TT):
                    act.activation(fin_x[:, tt, :], x[:, tt, :], ACT.Square,
                                   accum_out=stat[:, tt:tt + 1]).then_inc(fin_sq, 1)
                root(stat[:, 0:2])

            steps = dict(norm=norm, project=project, nsa=nsa, pool=pool, gla=gla, rwkv=rwkv, merge=merge,
                         memory=memory, cross=cross, ffn=ffn, moe=moe, final=final)
            act.wait_ge(loads, 80)
            act.wait_ge(trig_arg, 1)
            act.activation(trig[:, :, :, :], trig[:, :, :, :], ACT.Sin).then_inc(trig_done, 1)
            for step, l in PLAN:
                steps[step](l)

        @block.vector
        def _(dve):
            n_step = [0]

            def link(ins):
                n_step[0] += 1
                ins.then_inc(dve_step, 1)
                dve.wait_ge(dve_step, n_step[0])

            n_root = [0]

            def rooted(a, ins):
                n_root[0] += 1
                ins.then_inc(root_ready, 1)
                dve.wait_ge(root_done, n_root[0])
                link(dve.reciprocal(a, a))

            def tt_(o, a, b, op):
                return dve.tensor_tensor(o, a, b, op)

            def rope_tables():
                two_pi = 2 * np.pi
                c1 = 6.28125
                c2 = float(np.float32(np.floor((two_pi - c1) * 2.0 ** 20) / 2.0 ** 20))
                c3 = float(np.float32(two_pi - c1 - c2))
                magic = 1.5 * 2.0 ** 23
                ang = gl_z[:, 0:24]
                turns = gl_e[:, 0:48].rearrange("p (a b) -> p a b", a=2)
                posf = stat[:, 40:43]
                link(dve.tensor_copy(posf, pos[:, :]))
                link(tt_(ang.rearrange("p (a b) -> p a b", b=8), spread(posf, 2, 8), spread(conc("freq"), 1, 3),
                         ALU.mult))
                arg = trig[:, :, :, :].rearrange("p a b c -> p a (b c)")
                for s, quarter in ((0, 0.25), (1, 0.0)):
                    link(dve.tensor_scalar(turns[:, s, :], ang, 1.0 / two_pi, quarter, ALU.mult, ALU.add))
                    link(dve.tensor_scalar(turns[:, s, :], turns[:, s, :], magic, magic, ALU.add, ALU.subtract))
                    link(dve.scalar_tensor_tensor(out=arg[:, s, :], in0=turns[:, s, :], scalar=-c1, in1=ang,
                                                  op0=ALU.mult, op1=ALU.add))
                    for cc in (c2, c3):
                        link(dve.scalar_tensor_tensor(out=arg[:, s, :], in0=turns[:, s, :], scalar=-cc,
                                                      in1=arg[:, s, :], op0=ALU.mult, op1=ALU.add))
                link(dve.tensor_scalar(arg[:, 0, :], arg[:, 0, :], float(np.pi / 2), None, ALU.add))
                lim = float(np.nextafter(np.float32(np.pi), np.float32(0)))
                dve.tensor_scalar(arg, arg, lim, -lim, ALU.min, ALU.max).then_inc(trig_arg, 1)

            def rstd_of(s, scale, eps):
                rooted(s, dve.tensor_scalar(s, s, scale, eps, ALU.mult, ALU.add))

            def norm(k):
                dve.wait_ge(squares, TT * (k + 1))
                rstd_of(stat[:, 0:2], 1.0 / D, EPS)
                src = mem_sb if k == 0 else x
                for tt in range(TT):
                    dve.tensor_scalar(xn[:, tt, :], src[:, tt, :], stat[:, tt:tt + 1], None, ALU.mult)\
                       .then_inc(x_scaled, 1)

            def project(l):
                for b in (0, 2):
                    dve.wait_ge(proj_done, 6 * l + b + 1)
                    dve.tensor_copy(pfm[:, 2 * b:2 * b + 2, :].rearrange("p a b -> p (a b)"), bank(b))\
                       .then_inc(proj_dve, 1)
                dve.wait_ge(proj_dve, 2 * (l + 1))

            def rope(t1, t2, cos, sin, ta, tb, tc, td):
                tt_(ta, t1, cos, ALU.mult)
                tt_(tb, t2, sin, ALU.mult)
                tt_(tc, t2, cos, ALU.mult)
                link(tt_(td, t1, sin, ALU.mult))
                tt_(t1, ta, tb, ALU.subtract)
                return tt_(t2, tc, td, ALU.add)

            def shifted(u, tt, nk, mask, scale=0.125):
                dve.wait_ge(scored, u + 1)
                src = bank(2 * (u % 2), 2).rearrange("p (h k) -> p h k", h=4)[:, :, 0:nk]
                dst = prob[:, u % 2, :, 0:nk]
                if mask is None:
                    link(dve.tensor_scalar(dst, src, scale, None, ALU.mult))
                else:
                    link(dve.scalar_tensor_tensor(out=dst, in0=src, scalar=scale, in1=spread(mask, 1, 4),
                                                  op0=ALU.mult, op1=ALU.add))
                nm = stat[:, 8 + 8 * (u % 2):12 + 8 * (u % 2)]
                link(dve.tensor_reduce(nm, dst, AX, ALU.max))
                dve.tensor_scalar(nm, nm, -1.0, None, ALU.mult).then_inc(score_max, 1)

            def output(u, tt, gate):
                dve.wait_ge(att_out, u + 1)
                rs = stat[:, 32 + 4 * (u % 2):36 + 4 * (u % 2)]
                link(dve.reciprocal(rs, stat[:, 12 + 8 * (u % 2):16 + 8 * (u % 2)]))
                src = bank(6)[:, 0:256].rearrange("p (h d) -> p h d", h=4)
                if gate is None:
                    tt_(o_tm[:, tt, :, :], src, spread(rs, 2, HD), ALU.mult).then_inc(o_added, 1)
                    return
                link(tt_(rs, rs, gate, ALU.mult))
                link(tt_(att_tmp, src, spread(rs, 2, HD), ALU.mult))
                tt_(o_tm[:, tt, :, :], o_tm[:, tt, :, :], att_tmp, ALU.add).then_inc(o_added, 1)

            def pad_queries(b, sem_):
                src = bank(b).rearrange("p (a t) -> p a t", a=2)
                dve.tensor_copy(qpad[0:64, :, 0, :], src[0:64])
                dve.tensor_copy(qpad[64:128, :, 1, :], src[64:128]).then_inc(sem_, 1)

            def nsa(l):
                dve.wait_ge(rw_out, l + 1)
                dve.wait_ge(fill_copied, 10 * (l + 1))
                if l == 0:
                    dve.wait_ge(trig_done, 1)
                dve.memset(qpad[64:128, :, 0, :], 0.0)
                dve.memset(qpad[0:64, :, 1, :], 0.0)
                dve.memset(kc2[64:128, :, :, SEQ - 1:SEQ], 0.0)
                for tt in range(TT):
                    dve.tensor_copy(kc_dup[:, tt, :, :, :], spread(
                        ptm[:, tt, TM_KC:TM_KC + 256].rearrange("p (a b) -> p a b", a=4), 2, 2))
                heads = ptm[:, :, 0:512].rearrange("p t (h d) -> p t h d", d=HD)

                def table(s):
                    return spread(trig[:, s, 0:2, :], 2, 8)

                rope(heads[:, :, :, 0:8], heads[:, :, :, 8:16], table(0), table(1),
                     rope_a, rope_b, rope_c, rope_d).then_inc(roped, 1)
                dve.wait_ge(nsa_turned, l + 1)
                for j in range(2):
                    src = bank(2 + j).rearrange("p (g t) -> p g t", g=2)
                    dve.tensor_copy(kc2[0:64, j, :, :], src[0:64])
                    m = dve.tensor_copy(kc2[64:128, j, :, 0:SEQ - 1], src[64:128, :, 1:SEQ])
                m.then_inc(kc_copied, 1)
                pad_queries(0, q_padded)
                dve.wait_ge(cmp_kv, l + 1)
                dve.tensor_copy(v_cmp[0:N_CMP, :, :], bank(6)[0:N_CMP, 128:256].rearrange("p (a b) -> p a b", a=2))
                link(dve.tensor_copy(k_cmp[0:N_CMP, :, :],
                                     bank(6)[0:N_CMP, 0:128].rearrange("p (a b) -> p a b", a=2)))

                def ctable(s):
                    return spread(trig[0:N_CMP, s, 2, :], 1, 2)

                rope(k_cmp[0:N_CMP, :, 0:8], k_cmp[0:N_CMP, :, 8:16], ctable(0), ctable(1),
                     rope_a[0:N_CMP, 0, 0:2, :], rope_b[0:N_CMP, 0, 0:2, :], rope_c[0:N_CMP, 0, 0:2, :],
                     rope_d[0:N_CMP, 0, 0:2, :]).then_inc(cmp_kv_copied, 1)
                dve.wait_ge(cmp_kturned, l + 1)
                dve.tensor_copy(kcT, bank(6)[:, 0:N_CMP]).then_inc(cmp_kcopied, 1)
                dve.wait_ge(cmp_scored, l + 1)
                src = bank(5)[:, 0:8 * N_CMP].rearrange("p (t h n) -> p t h n", t=2, h=4)
                add = spread(conc("cmp_add").rearrange("p (t n) -> p t n", t=2), 2, 4)
                keep = spread(conc("cmp_keep").rearrange("p (t n) -> p t n", t=2), 2, 4)
                for tt in range(TT):
                    m = dve.scalar_tensor_tensor(out=cprob[:, tt], in0=src[:, tt], scalar=0.125, in1=add[:, tt],
                                                 op0=ALU.mult, op1=ALU.add)
                link(m)
                mx = stat[:, 24:32].rearrange("p (t h) -> p t h", t=2)
                link(dve.tensor_reduce(mx, cprob, AX, ALU.max))
                tt_(cprob, cprob, spread(mx, 3, N_CMP), ALU.subtract).then_inc(cmp_shifted, 1)
                shifted(6 * l, 0, P, conc("causal", 0, P))
                dve.wait_ge(cmp_exp, l + 1)
                link(dve.tensor_reduce(mx, cprob, AX, ALU.add))
                tt_(cprob, cprob, keep, ALU.mult).then_inc(cmp_prob, 1)
                dve.wait_ge(gates_on, l + 1)
                gt = gates.rearrange("p t (h a) -> p t h a", a=3)
                link(dve.reciprocal(mx, mx))
                link(tt_(mx, mx, gt[:, :, :, 0], ALU.mult))
                dve.wait_ge(cmp_out, l + 1)
                src = bank(6).rearrange("p (t h d) -> p t h d", t=2, h=4)
                tt_(o_tm, src, spread(mx, 3, HD), ALU.mult).then_inc(cmp_added, 1)
                dve.wait_ge(cmp_added, l + 1)
                for n in range(4):
                    if n < 3:
                        t2 = (n + 1) % 2
                        shifted(6 * l + n + 1, t2, P * (t2 + 1), conc("causal", 256 * t2, P * (t2 + 1)))
                    output(6 * l + n, n % 2, gt[:, n % 2, :, 1 + n // 2])

            def pool(l):
                dve.wait_ge(pool_d, l + 1)
                dve.tensor_copy(poolT.rearrange("p a b -> p (a b)"), bank(5)).then_inc(pool_dc, 1)

            def gla(l):
                dve.wait_ge(gl_pe, 6 * l + 1)
                link(dve.tensor_scalar(gl_z, bank(0)[:, 0:256], parc(l, "ab"), None, ALU.add))
                dve.scalar_tensor_tensor(out=gl_e, in0=gl_z, scalar=-1.0, in1=gl_z,
                                         op0=ALU.mult, op1=ALU.max).then_inc(gl_dve, 1)
                link(dve.tensor_scalar(gl_z, gl_z, 0.0, None, ALU.min))
                dve.wait_ge(gl_act, 3 * l + 1)
                link(tt_(gl_z, gl_z, gl_e, ALU.subtract))
                link(dve.tensor_tensor_scan(gl_b, conc("reset16"), gl_z, 0.0, ALU.mult, ALU.add))
                b = gl_b.rearrange("p (n t) -> p n t", t=C_GL)
                last = b[:, :, C_GL - 1:C_GL].broadcast_to([P, N_GL, C_GL])
                tt_(gl_ke.rearrange("p (n t) -> p n t", t=C_GL), last, b, ALU.subtract).then_inc(gl_dve, 1)
                dve.memset(gl_q, 0.0)
                link(dve.memset(gl_s[:, 0, :], 0.0))
                dve.wait_ge(gl_act, 3 * l + 2)
                for h in range(4):
                    r = slice(32 * h, 32 * h + 32)
                    dve.scalar_tensor_tensor(out=gl_q[r, h, :], in0=pfm[r, FM_GQ, :], scalar=32.0 ** -0.5,
                                             in1=gl_eq[r, :], op0=ALU.mult, op1=ALU.mult)
                tt_(gl_ek, gl_ek, pfm[:, FM_GK, :], ALU.mult)
                tt_(gl_ke, gl_ke, pfm[:, FM_GK, :], ALU.mult).then_inc(gl_dve, 1)
                dve.wait_ge(gl_pe, 6 * l + 3)
                for tt in range(TT):
                    m = tt_(gl_k8[:, tt, :, :], spread(bank(3)[:, tt * P:(tt + 1) * P], 1, 8),
                            spread(conc("chunk16"), 2, P), ALU.mult)
                m.then_inc(gl_dve, 1)
                for tt in range(TT):
                    tt_(gl_att[:, tt, :, :], bank(1 + tt).rearrange("p (h t) -> p h t", h=4),
                        spread(conc("gl_causal"), 1, 4), ALU.mult)
                dve.wait_ge(gl_pe, 6 * l + 4)
                for n in range(N_GL - 1):
                    m = dve.scalar_tensor_tensor(out=gl_s[:, n + 1, :], in0=gl_s[:, n, :], scalar=gl_dl[:, n:n + 1],
                                                 in1=bank(4 + n // 8)[:, (n % 8) * HD:(n % 8 + 1) * HD],
                                                 op0=ALU.mult, op1=ALU.add)
                    if n < N_GL - 2:
                        link(m)
                m.then_inc(gl_dve, 1)
                dve.wait_ge(gl_pe, 6 * l + 5)
                link(dve.tensor_copy(gl_o.rearrange("p a b -> p (a b)"), bank(6)))
                tt_(gl_sq, gl_o, gl_o, ALU.mult).then_inc(gl_dve, 1)
                dve.wait_ge(gl_pe, 6 * l + 6)
                rooted(gl_r, dve.tensor_scalar(gl_r.rearrange("p a b -> p (a b)"), bank(0), EPS, None, ALU.add))
                link(tt_(gl_o, gl_o, gl_r, ALU.mult))
                dve.wait_ge(gl_act, 3 * l + 3)
                dve.scalar_tensor_tensor(out=oT[:, 6:8, :], in0=gl_o, scalar=parc(l, "gnorm"), in1=gl_og,
                                         op0=ALU.mult, op1=ALU.mult).then_inc(gl_dve, 1)

            def rwkv(l):
                dve.wait_ge(proj_act, 4 * l + 2)
                d = rw_kr.rearrange("p a b c t -> p (a b c) t")
                tt_(d[:, 0:7, 1:SEQ], pfm[:, 0:7, 0:SEQ - 1], pfm[:, 0:7, 1:SEQ], ALU.subtract)
                link(dve.tensor_scalar(d[:, 0:7, 0:1], pfm[:, 0:7, 0:1], -1.0, None, ALU.mult))
                for cc in range(7):
                    m = dve.scalar_tensor_tensor(out=pfm[:, cc, :], in0=d[:, cc, :], scalar=parc(l, "mu", cc),
                                                 in1=pfm[:, cc, :], op0=ALU.mult, op1=ALU.add)
                m.then_inc(rw_dve, 1)
                dve.wait_ge(rw_dve, 7 * l + 1)
                r, k, v = (pfm[:, a:a + 2, :] for a in (FM_R, FM_K, FM_V))
                for s, t in ((rw_kr[64:128, :, 0, :, :], 0), (rw_kr[0:64, :, 1, :, :], 0)):
                    dve.memset(s, 0.0)
                for t in (rw_km, rw_bm):
                    dve.memset(t[64:128, :, 0, :, :], 0.0)
                    dve.memset(t[0:64, :, 1, :, :], 0.0)
                link(dve.memset(rw_s[:, 0, :, :], 0.0))
                for hp in range(2):
                    link(dve.tensor_scalar(rw_kk[:, hp, :], k[:, hp, :], parc(l, "k_k", hp), None, ALU.mult))
                tt_(rw_sq, rw_kk, rw_kk, ALU.mult).then_inc(rw_dve, 1)
                dve.wait_ge(rw_pe, 7 * l + 2)
                nrm = rw_bt
                rooted(nrm, dve.tensor_scalar(nrm.rearrange("p a b -> p (a b)"), bank(5), 64.0, 1e-24,
                                              ALU.mult, ALU.max))
                link(tt_(rw_kk, rw_kk, nrm, ALU.mult))
                dve.wait_ge(rw_act, 8 * l + 2)
                link(dve.tensor_scalar(rw_lw, rw_lw, -float(np.exp(-0.5)), None, ALU.mult))
                link(dve.tensor_tensor_scan(rw_cl.rearrange("p a b -> p (a b)"), conc("reset64"),
                                            rw_lw.rearrange("p a b -> p (a b)"), 0.0, ALU.mult, ALU.add))
                tt_(rw_clm, rw_cl, rw_lw, ALU.subtract).then_inc(rw_dve, 1)
                if l == 0:
                    dve.tensor_copy(v_first[:, :, :], v)
                else:
                    link(tt_(rw_bonus, v_first[:, :, :], v, ALU.subtract))
                    link(tt_(rw_bonus, rw_bonus, rw_vg, ALU.mult))
                    link(tt_(v, v, rw_bonus, ALU.add))
                for hp in range(2):
                    link(dve.tensor_scalar(rw_k2[:, hp, :], rw_a[:, hp, :], -1.0, parc(l, "k_a", hp),
                                           ALU.add, ALU.mult))
                link(dve.scalar_tensor_tensor(out=rw_k2, in0=rw_k2, scalar=1.0, in1=k, op0=ALU.add, op1=ALU.mult))
                link(tt_(rw_a, rw_kk, rw_a, ALU.mult))
                dve.wait_ge(rw_act, 8 * l + 3)
                for h2 in range(2):
                    rr = slice(64 * h2, 64 * h2 + 64)
                    tt_(rw_kr[rr, :, h2, 0, :], rw_kk[rr], rw_clm[rr], ALU.mult)
                    tt_(rw_kr[rr, :, h2, 1, :], r[rr], rw_ep[rr], ALU.mult)
                tt_(rw_bt, rw_a, rw_em, ALU.mult)
                tt_(rw_kt, rw_k2, rw_em, ALU.mult)
                for hp in range(2):
                    m = dve.scalar_tensor_tensor(out=rw_rk[:, hp, :], in0=r[:, hp, :], scalar=parc(l, "r_k", hp),
                                                 in1=rw_k2[:, hp, :], op0=ALU.mult, op1=ALU.mult)
                m.then_inc(rw_dve, 1)
                for which, dst in ((0, rw_ab), (1, rw_ak)):
                    dve.wait_ge(rw_pe, 7 * l + 3 + which)
                    if which == 1:
                        dve.wait_ge(rw_act, 8 * l + 5)
                    mask = conc("rw_k" if which else "rw_b").rearrange("p (a t) -> p a t", a=2)
                    for tt in range(TT):
                        for hp in range(2):
                            m = tt_(dst[:, tt, hp], bank(2 * tt + hp).rearrange("p (a b t) -> p a b t", a=2, b=2),
                                    spread(mask, 1, 2), ALU.mult)
                    m.then_inc(rw_dve, 1)
                dve.tensor_copy(rw_x, spread(ident, 1, 8))
                dve.memset(rw_z, 0.0)
                dve.memset(rw_u, 0.0)
                dve.tensor_copy(rw_xt, spread(ident, 1, 8)).then_inc(inv_dve, 1)
                for j in range(6):
                    mask = spread(conc("level", j * P, P), 1, 4)
                    for g in range(2):
                        part = slice(4 * g, 4 * g + 4)
                        dve.wait_ge(inv_pe, 24 * l + 4 * j + 1 + g)
                        tt_(rw_t1[:, part], bank(g).rearrange("p (q t) -> p q t", q=4), mask, ALU.mult)\
                            .then_inc(inv_dve, 1)
                    for g in range(2):
                        part = slice(4 * g, 4 * g + 4)
                        dve.wait_ge(inv_pe, 24 * l + 4 * j + 3 + g)
                        tt_(rw_x[:, part], rw_x[:, part], bank(2 + g).rearrange("p (q t) -> p q t", q=4), ALU.add)
                        tt_(rw_xt[:, part], rw_xt[:, part], bank(6 + g).rearrange("p (q t) -> p q t", q=4),
                            ALU.add).then_inc(inv_dve, 1)
                for ch in range(4):
                    rows = slice(64 * (ch % 2), 64 * (ch % 2) + 64)
                    dve.wait_ge(seq_pe, 16 * l + 4 * ch + 1)
                    dve.tensor_copy(rw_z[rows, :], bank(0)[rows, 0:256]).then_inc(seq_dve, 1)
                    dve.wait_ge(seq_pe, 16 * l + 4 * ch + 2)
                    dve.tensor_copy(rw_u[rows, :], bank(1)[rows, 0:256]).then_inc(seq_dve, 1)
                    dve.wait_ge(seq_pe, 16 * l + 4 * ch + 3)
                    new = rw_s[:, (ch + 1) % 2, :, :]
                    for h2 in range(2):
                        rr = slice(64 * h2, 64 * h2 + 64)
                        src = bank(3)[rr, 0:256].rearrange("p (a b) -> p a b", a=2)[:, :, h2 * HD:(h2 + 1) * HD]
                        m = tt_(new[rr], rw_s[rr, ch % 2, :, :], src, ALU.add)
                    link(m)
                    dec = rw_ep[:, :, ch * C_RW + C_RW - 1:ch * C_RW + C_RW].broadcast_to([P, 2, HD])
                    tt_(new, new, dec, ALU.mult).then_inc(seq_dve, 1)
                dve.wait_ge(rw_act, 8 * l + 8)
                link(tt_(rw_yc, rw_y, rw_r, ALU.subtract))
                tt_(rw_y2, rw_yc, rw_yc, ALU.mult).then_inc(rw_dve, 1)
                dve.wait_ge(rw_pe, 7 * l + 7)
                rooted(rw_r, dve.tensor_scalar(rw_r.rearrange("p a b -> p (a b)"), bank(1), GN_EPS, None, ALU.add))
                link(tt_(rw_yc, rw_yc, rw_r, ALU.mult))
                link(dve.scalar_tensor_tensor(out=rw_bonus, in0=rw_bonus, scalar=64.0, in1=v,
                                              op0=ALU.mult, op1=ALU.mult))
                for hp in range(2):
                    m = dve.scalar_tensor_tensor(out=rw_yc[:, hp, :], in0=rw_yc[:, hp, :],
                                                 scalar=parc(l, "ln", hp), in1=rw_bonus[:, hp, :],
                                                 op0=ALU.mult, op1=ALU.add)
                link(m)
                tt_(oT[:, 4:6, :], rw_yc, rw_g, ALU.mult).then_inc(rw_out, 1)

            def merge(l):
                for j in range(N_EARLY):
                    dve.wait_ge(early_sig, N_EARLY * l + j + 1)
                    dve.wait_ge(branch_done, N_EARLY * l + j + 1)
                    t = mtmp if j % 2 else mtmp2
                    link(tt_(t, early[:, j], bank(2 * (j % 2), 2).rearrange("p (i t) -> p i t", i=N_BR), ALU.mult))
                    dve.tensor_reduce(merged[:, j, :], t.rearrange("p i t -> p t i"), AX, ALU.add)\
                       .then_inc(branch_used, 1)
                for n in range(N_BR * (KC - N_EARLY)):
                    j, i = n // N_BR, n % N_BR
                    dve.wait_ge(gate_sig, 8 * l + n + 1)
                    src = bank(4 * (1 - j) + i)[:, 256:512]
                    if i == 0:
                        tt_(merged[:, N_EARLY + j, :], sig[:, i, :], src, ALU.mult).then_inc(gate_used, 1)
                        continue
                    if i == 1:
                        dve.wait_ge(gate_used, 8 * l + n)
                    link(tt_(mtmp[:, i, :], sig[:, i, :], src, ALU.mult))
                    tt_(merged[:, N_EARLY + j, :], merged[:, N_EARLY + j, :], mtmp[:, i, :], ALU.add)\
                        .then_inc(gate_used, 1)
                add_to_x(4, merged_out, l + 1, x_merged)

            def add_to_x(b, sem_, n, done):
                dve.wait_ge(sem_, n)
                for tt in range(TT):
                    m = tt_(x[:, tt, :], x[:, tt, :], bank(b + 2 * tt, 2), ALU.add)
                m.then_inc(done, 1)

            def memory(l):
                pass

            def cross(l):
                dve.wait_ge(caq_done, l + 1)
                dve.memset(qpad[64:128, :, 0, :], 0.0)
                dve.memset(qpad[0:64, :, 1, :], 0.0)
                pad_queries(4, caq_padded)
                for tt in range(TT):
                    shifted(6 * l + 4 + tt, tt, MEM, None)
                for tt in range(TT):
                    output(6 * l + 4 + tt, tt, None)
                add_to_x(0, cao_done, l + 1, x_crossed)

            def hiddens(at, c, up):
                dve.wait_ge(down_split, up + (c + 1))
                tt_(down_w[:, at % 2, 1, :], ring[:, at % RING, 2 * OCT:3 * OCT], down_w[:, at % 2, 0, :],
                    ALU.subtract)
                dve.wait_ge(silu_done, up + (c + 1))
                t = product[:, at % 2, :]
                b = bank(4 + at % 2)[:, 256:512]
                tt_(t, silu[:, at % 2, :], b, ALU.mult)
                ins = tt_(hid[:, at % 2, 0, :], silu[:, at % 2, :], b, ALU.mult)
                ins.then_inc(slab_read, 1)
                dve.wait_ge(slab_read, up + (at + 1))
                tt_(hid[:, at % 2, 1, :], t, hid[:, at % 2, 0, :], ALU.subtract).then_inc(hid_ready, 1)

            def ffn(l):
                for f in range(FC):
                    hiddens(LAYER_SLABS + f, f, 0)
                add_to_x(0, down_used, FC, x_added)

            def moe(l):
                dve.wait_ge(routed, 1)
                link(dve.tensor_copy(logit, bank(6)[:, 0:16].rearrange("p (t e) -> p t e", t=2)))
                for tt in range(TT):
                    link(dve.max(top[:, tt, :], logit[:, tt, :]))
                    link(dve.max_index(idx[:, :], top[:, tt, :], logit[:, tt, :]))
                    link(dve.tensor_copy(topi[:, tt, :], idx[:, :]))
                    one, two = (topi[:, tt, s:s + 1].broadcast_to([P, 8]) for s in (0, 1))
                    tt_(picked[:, tt, :], conc("iota", 0, 8), one, ALU.is_equal)
                    link(tt_(pick[:, tt, :], conc("iota", 0, 8), two, ALU.is_equal))
                    link(tt_(picked[:, tt, :], picked[:, tt, :], pick[:, tt, :], ALU.add))
                big_ = top[:, :, 0:1].broadcast_to([P, TT, 8])
                tt_(logit, logit, big_, ALU.subtract).then_inc(top_diff, 1)
                dve.wait_ge(top_exp, 1)
                link(tt_(combine, picked, pick, ALU.mult))
                link(dve.tensor_reduce(stat[:, 44:46], combine, AX, ALU.add))
                link(dve.reciprocal(stat[:, 44:46], stat[:, 44:46]))
                link(tt_(combine, combine, stat[:, 44:46].unsqueeze(2).broadcast_to([P, TT, 8]), ALU.mult))
                dve.wait_ge(placed, 1)
                dve.tensor_copy(load_of[:, :], bank(7)[:, 16:24]).then_inc(load_ready, 1)
                dve.tensor_copy(place, bank(7)[:, 0:16].rearrange("p (t e) -> p t e", t=2))
                link(dve.tensor_scalar(few, bank(7)[:, 16:24], float(P), None, ALU.is_le))
                link(tt_(comb_few, combine, spread(few, 1, TT), ALU.mult))
                link(tt_(comb_many, combine, comb_few, ALU.subtract))
                for e in range(N_EXP + 1):
                    if e < N_EXP:
                        for tt in range(TT):
                            pl = place[:, tt, e:e + 1]
                            if e >= 2:
                                dve.wait_ge(gathered, e - 1)
                            dve.tensor_scalar(sel[:, e % 2, tt, :], conc("iota"), pl, picked[:, tt, e:e + 1],
                                              ALU.is_equal, ALU.mult)
                            m = dve.tensor_scalar(sel_w[:, e % 2, tt, :], conc("iota"), pl,
                                                  comb_few[:, tt, e:e + 1], ALU.is_equal, ALU.mult)
                        m.then_inc(sel_ready, 1)
                    if e >= 1:
                        dve.wait_ge(gathered, e)
                        tt_(h_exp[:, e - 1], bank(2 * ((e - 1) % 2), 2).rearrange("p (k t) -> p k t", k=KC),
                            spread(parc(l, "norm_ffn", 0, 8), 2, P), ALU.mult)
                        dve.tensor_copy(sel_wT[:, e - 1], bank(6 + (e - 1) % 2)[:, 0:256]
                                        .rearrange("p (t s) -> p t s", t=2)).then_inc(gathered_c, 1)
                s0 = FIRST_SLAB[1] + LAYER_SLABS
                with dve.Fori(0, N_EXP // 2) as i:
                    for half in range(2):
                        for f in range(FC):
                            hiddens(s0 + FC * half + f, FC * (1 + half) + f, i * (2 * FC))
                        dve.wait_ge(down_used, i * (2 * FC) + FC * (2 + half))
                        dve.wait_ge(x_added, i * 2 + (1 + half))
                        dve.tensor_copy(y_exp[:, bass.ds(i * 2 + half, 1), :].rearrange("p e d -> p (e d)"),
                                        bank(0, 2))
                        for tt in range(TT):
                            w = comb_many[:, tt, bass.ds(i * 2 + half, 1)]
                            m = dve.scalar_tensor_tensor(out=x[:, tt, :], in0=bank(2 * tt, 2), scalar=w,
                                                         in1=x[:, tt, :], op0=ALU.mult, op1=ALU.add)
                        m.then_inc(x_added, 1)
                add_to_x(0, scattered, 1, x_moe)

            def final(l):
                dve.wait_ge(fin_sq, TT)
                rstd_of(stat[:, 0:2], 1.0 / D, EPS)
                dve.wait_ge(gain_loaded, 16)
                for tt in range(TT):
                    m = dve.scalar_tensor_tensor(out=fin_x[:, tt, :], in0=x[:, tt, :], scalar=stat[:, tt:tt + 1],
                                                 in1=fin_gain, op0=ALU.mult, op1=ALU.mult)
                m.then_inc(fin_ready, 1)

            steps = dict(norm=norm, project=project, nsa=nsa, pool=pool, gla=gla, rwkv=rwkv, merge=merge,
                         memory=memory, cross=cross, ffn=ffn, moe=moe, final=final)
            dve.wait_ge(loads, 80)
            rope_tables()
            for step, l in PLAN:
                steps[step](l)


def constants():
    con = np.zeros((P, N_CON), np.float32)

    def put(name, a):
        a = np.asarray(a, np.float64).reshape(P, -1)
        assert a.shape[1] == CON_COLS[name], (name, a.shape)
        con[:, CON[name]:CON[name] + a.shape[1]] = a

    p = np.arange(P)
    t = np.arange(P)
    s256 = np.arange(256)
    put("ident", np.eye(P))
    q = p[:, None] + P * np.arange(2)[None, :]
    put("causal", np.where(s256[None, None, :] <= q[:, :, None], 0.0, NEG))
    end = np.arange(N_CMP) * CMP_STRIDE + CMP_LEN - 1
    ok = end[None, None, :] <= q[:, :, None]
    put("cmp_add", np.where(ok, 0.0, NEG))
    put("cmp_keep", ok)
    levels = []
    for j in range(6):
        b = 1 << j
        row, col = p[:, None], t[None, :]
        levels.append((row // (2 * b) == col // (2 * b)) & (row % (2 * b) >= b) & (col % (2 * b) < b))
    put("level", np.stack(levels, 1))
    s, tc = p[:, None], t[None, :]
    same = s // C_RW == tc // C_RW
    both = np.stack([same & (s < tc), same & (s <= tc)], 1).astype(float)
    put("rw_b", -both)
    put("rw_k", both)
    put("gl_causal", (s // C_GL == tc // C_GL) & (s <= tc))
    tab = []
    for w in (2, 4, 8, 16):
        tq, sq = np.arange(256)[None, :], np.arange(256)[:, None]
        m = ((sq <= tq) & (sq > tq - w)) / np.minimum(tq + 1, w) - (sq == tq)
        tab += [m[0:P, :], m[P:, P:]]
    put("pool", np.concatenate(tab, 1))
    put("reset64", np.tile((np.arange(512) % C_RW != 0)[None], (P, 1)))
    put("reset16", np.tile((np.arange(256) % C_GL != 0)[None], (P, 1)))
    put("ones", (p[:, None] // 64 == t[None, :] // 64) / 64.0)
    put("chunk16", p[:, None] // C_GL == np.arange(8)[None, :])
    inv = (np.float32(500000.0) ** (-np.arange(0, 16, 2, dtype=np.float32) / np.float32(16))).astype(np.float32)
    put("freq", np.tile(inv[None], (P, 1)))
    put("iota", np.tile(np.arange(P)[None], (P, 1)))
    put("before", p[:, None] < t[None, :])
    put("every", np.ones((P, P)))
    return con


def lay_out(a):
    f = np.float32

    def blocks(w):
        return w.reshape(-1, P, w.shape[1]).transpose(1, 0, 2).reshape(P, -1)

    stream = np.zeros((N_SLABS, P, SLAB), f)
    params = np.zeros((DEPTH, P, N_PAR), f)
    mixw = np.zeros((DEPTH, P, N_MIX), f)
    nsa, rw, gl = 0, 1292, 2188
    for l in range(DEPTH):
        w = a["w_in"][l]
        q = w[:, 0:256].reshape(D, 2, 2, HD).transpose(0, 2, 1, 3).reshape(D, 256)
        tm = np.concatenate([q, w[:, 512:640], w[:, 768:896], w[:, 256:512], w[:, 640:768],
                             w[:, 896:1024], w[:, 1036:1292], w[:, gl + 256:gl + 512]], 1)
        s0 = FIRST_SLAB[l]
        for s in range(N_TM):
            stream[s0 + FM_FIRST + s] = blocks(tm[:, s * 384:(s + 1) * 384])
        misc = np.zeros((D, P), f)
        misc[:, 0:16] = w[:, gl + 512:gl + 528]
        if l:
            misc[:, MISC_V1:MISC_V1 + 32] = a["rwkv_v1"][l - 1]
        misc[:, MISC_GATES:MISC_GATES + 12] = w[:, 1024:1036]
        fm = np.concatenate([w[:, rw:rw + 896], misc, w[:, gl:gl + 256], w[:, gl + 528:gl + 784]], 1)
        for ch in range(12):
            stream[s0 + (ch // 3 if ch < 9 else FM_FIRST + N_TM)][:, (ch % 3) * OCT:(ch % 3 + 1) * OCT] = blocks(fm[:, ch * P:(ch + 1) * P])

        def put(o, block):
            stream[s0 + N_TM + N_FM + o // 3][:, (o % 3) * OCT:(o % 3 + 1) * OCT] = block

        for j in range(2):
            w1 = a["nsa_cmp_w1"][l, j].reshape(2 * D, P)
            for half in range(2):
                put(O_CMP + 2 * j + half, blocks(w1[half * D:(half + 1) * D]))
        for j in range(KC):
            o = O_MERGE + j if j < N_EARLY else O_MERGE + N_EARLY + (j - N_EARLY) * (N_BR + 1)
            put(o, blocks(a["w_branch"][l, :, :, j * P:(j + 1) * P].reshape(D, P)))
            for i in range(N_BR):
                put(O_GATE + N_BR * j + i if j < N_EARLY else o + 1 + i,
                    blocks(a["w_gate"][l, i][:, j * P:(j + 1) * P]))
            put(O_OUT + j, a["w_out"][l, j * P:(j + 1) * P])
        kv = a["w_ca_kv"][l]
        for cc in range(2):
            put(O_KV + cc, blocks(kv[:, cc * P:(cc + 1) * P]))
            put(O_KV + 2 + cc, blocks(kv[cc * 512:(cc + 1) * 512, 256:512]))
            put(O_CQ + cc, blocks(a["w_ca_q"][l][:, cc * P:(cc + 1) * P]))
            put(O_CO + cc, a["w_ca_o"][l, cc * P:(cc + 1) * P])

        def small(name, v):
            v = v.reshape(-1, P).T
            params[l][:, PAR[name]:PAR[name] + v.shape[1]] = v

        small("norm_mix", a["norm_mix"][l])
        small("norm_ca", a["norm_ca"][l])
        small("norm_ffn", a["norm_ffn"][l])
        small("mem_norm", a["mem_norm"])
        small("b_gate", a["b_gate"][l])
        small("pool_scale", a["pool_scale"][l])
        small("mu", a["rwkv_mu"][l])
        for name, key in (("w0", "rwkv_w0"), ("a0", "rwkv_a0"), ("k_k", "rwkv_k_k"), ("k_a", "rwkv_k_a"),
                          ("r_k", "rwkv_r_k"), ("ln", "rwkv_ln"), ("ab", "gla_ab")):
            small(name, a[key][l])
        if l:
            small("v0", a["rwkv_v0"][l - 1])
            params[l][:, PAR["router"]:PAR["router"] + 64] = blocks(a["moe_router"][0])
        small("gnorm", np.concatenate([a["gla_norm"][l]] * 2))
        small("pe", a["nsa_cmp_pe"][l])

        def mix(name, rows, v, at=0):
            mixw[l][rows, MIX[name] + at:MIX[name] + at + v.shape[1]] = v

        mix("w2", slice(0, 32), a["rwkv_w2"][l])
        mix("a2", slice(32, 64), a["rwkv_a2"][l])
        mix("g2", slice(64, 128), a["rwkv_g2"][l])
        if l:
            mix("v2", slice(MISC_V1, MISC_V1 + 32), a["rwkv_v2"][l - 1])
        mix("gla_a2", slice(0, 16), a["gla_a2"][l])
        for g in range(4):
            mix("pool", slice(64 * (g % 2), 64 * (g % 2) + 64), a["pool_w"][l, g], P * (g // 2) + 64 * (g % 2))
        for j in range(2):
            mix("cmp", slice(0, P), a["nsa_cmp_w2"][l, j], j * HD)

    def feed(s0, wg, wu, wd):
        dst = stream[s0:s0 + FC].reshape(FC, P, 3, KC, P)
        dst[:, :, 0] = wg.reshape(KC, P, FC, P).transpose(2, 1, 0, 3)
        dst[:, :, 1] = wu.reshape(KC, P, FC, P).transpose(2, 1, 0, 3)
        dst[:, :, 2] = wd.reshape(FC, P, KC, P)

    feed(LAYER_SLABS, a["ffn_w_gate"][0], a["ffn_w_up"][0], a["ffn_w_down"][0])
    for e in range(N_EXP):
        feed(FIRST_SLAB[1] + LAYER_SLABS + FC * e, a["moe_w_gate"][0, e], a["moe_w_up"][0, e],
             a["moe_w_down"][0, e])
    pos = a["positions"].reshape(SEQ)
    positions = np.zeros((P, 3), pos.dtype)
    positions[:, 0:2] = pos.reshape(TT, P).T
    positions[0:N_CMP, 2] = pos[CMP_LEN - 1::CMP_STRIDE]
    return {
        "stream": stream, "params": params, "mixw": mixw, "consts": constants(),
        "x_in": np.ascontiguousarray(a["x"].reshape(TT, P, D).transpose(1, 0, 2)),
        "mem_in": np.ascontiguousarray(a["mem"].reshape(TT, P, D).transpose(1, 0, 2)),
        "pos_in": positions,
        "gain_in": np.ascontiguousarray(np.broadcast_to(a["norm_final"][None], (P, D))),
    }


def kernel(**inputs):
    import concourse.bacc as bacc
    from concourse.bass_utils import run_bass_kernel_spmd as run

    arrays = lay_out({k: np.asarray(v) for k, v in inputs.items()})
    nc = bacc.Bacc("TRN2", target_bir_lowering=False, num_devices=1)
    args = [nc.dram_tensor(n, list(v.shape), mybir.dt.from_np(v.dtype), kind="ExternalInput").ap()
            for n, v in arrays.items()]
    out = nc.dram_tensor("out", [P, TT, D], F32, kind="ExternalOutput").ap()
    trunk(nc, *args, out)
    r = run(nc, [arrays], core_ids=[0])
    return r.results[0]["out"].transpose(1, 0, 2).reshape(1, SEQ, D)
```

```python
from contextlib import ExitStack

import numpy as np

import concourse.bass as bass
from concourse import mybir

F32 = mybir.dt.float32
F32R = mybir.dt.float32r
I32 = mybir.dt.int32
U32 = mybir.dt.uint32
ALU = mybir.AluOpType
ACT = mybir.ActivationFunctionType
AX = mybir.AxisListType.X

P = 128
DEPTH, D, SEQ, MEM = 2, 1024, 256, 256
KC = D // P
TT = SEQ // P
HD = 64
W_BR = 256
N_BR = 4
DFF, N_EXP = 2816, 8
FC = DFF // P
EPS, GN_EPS = 1e-6, 64e-5
NEG = -1e30
CMP_LEN, CMP_STRIDE = 32, 16
N_CMP = (SEQ - CMP_LEN) // CMP_STRIDE + 1
ROPE_HALF = 8
C_RW = 64
C_GL = 16
N_GL = SEQ // C_GL

OCT = 8 * P
SLAB = 3 * OCT
RING = 4
ARENA = 17000
FFN_ARENA = 14952
MOE_FIRST = 4096
FFN_FIRST = 5120
N_TM, N_FM = 4, 4
FM_FIRST = 3
N_EARLY = 6
O_KV = 0
O_CMP = 4
O_GATE = 8
O_MERGE = O_GATE + N_BR * N_EARLY
O_OUT = O_MERGE + N_EARLY + (N_BR + 1) * (KC - N_EARLY)
O_CQ, O_CO = O_OUT + 8, O_OUT + 10
N_OCT = O_CO + 2
LAYER_SLABS = N_TM + N_FM + N_OCT // 3
FIRST_SLAB = [0, LAYER_SLABS + FC]
N_SLABS = 2 * LAYER_SLABS + FC * (1 + N_EXP)

TM_Q, TM_KS, TM_KW, TM_KC, TM_VC, TM_VS, TM_VW, TM_POOL, TM_GV, TM_END = (
    0, 256, 384, 512, 640, 768, 896, 1024, 1280, 1536)
FM_R, FM_K, FM_V, FM_LR, FM_MISC, FM_GQ, FM_GK, FM_OG = 0, 2, 4, 6, 7, 8, 9, 10
MISC_V1, MISC_GATES = 32, 64

PAR_COLS = dict(norm_mix=8, norm_ca=8, norm_ffn=8, mem_norm=8, b_gate=32, pool_scale=2, mu=7, w0=2, a0=2,
                k_k=2, k_a=2, r_k=2, ln=2, v0=2, ab=1, gnorm=1, pe=32, router=64)
PAR = {}
for _n, _c in PAR_COLS.items():
    PAR[_n] = sum(PAR_COLS[m] for m in list(PAR_COLS)[:len(PAR)])
N_PAR = sum(PAR_COLS.values())
MIX_COLS = dict(w2=256, a2=256, g2=256, v2=256, gla_a2=128, pool=256, cmp=128)
MIX = {}
for _n, _c in MIX_COLS.items():
    MIX[_n] = sum(MIX_COLS[m] for m in list(MIX_COLS)[:len(MIX)])
N_MIX = sum(MIX_COLS.values())
CON_COLS = dict(ident=128, causal=512, cmp_add=2 * N_CMP, cmp_keep=2 * N_CMP, level=6 * 128, rw_b=256, rw_k=256,
                gl_causal=128, pool=4 * 384, reset64=512, reset16=256, ones=128, chunk16=8, freq=8,
                iota=128, before=128, every=128)
CON = {}
for _n, _c in CON_COLS.items():
    CON[_n] = sum(CON_COLS[m] for m in list(CON_COLS)[:len(CON)])
N_CON = sum(CON_COLS.values())

PLAN = [("norm", 0)]
for _l in range(DEPTH):
    PLAN += [("norm", 1 + 3 * _l), ("project", _l), ("rwkv", _l), ("nsa", _l), ("pool", _l), ("gla", _l),
             ("merge", _l), ("norm", 2 + 3 * _l), ("cross", _l), ("norm", 3 + 3 * _l),
             ("ffn", _l) if _l == 0 else ("moe", _l)]
PLAN += [("final", 0)]


def slabs_of(plan):
    n = 0
    for step, l in plan:
        f = FIRST_SLAB[min(l, 1)]
        last = {"rwkv": O_KV + 3, "nsa": O_GATE + 15, "pool": O_GATE + 16, "gla": O_GATE + 23, "merge": O_OUT + 7,
                "cross": O_CO + 1}
        n = {"project": f + 3, "ffn": FIRST_SLAB[1], "moe": N_SLABS}.get(step, n)
        if step in last:
            n = f + N_TM + N_FM + last[step] // 3 + 1
    return n


def trunk(nc, stream, params, mixw, consts, x_in, mem_in, pos_in, gain_in, out):
    n_slabs = slabs_of(PLAN)
    with ExitStack() as ctx:
        def sb(name, shape, dt=F32):
            return ctx.enter_context(nc.sbuf_tensor(name, shape, dt))

        def sem(name):
            return ctx.enter_context(nc.semaphore(name))

        ring = sb("ring", [P, RING, SLAB])
        x = sb("x", [P, TT, D])
        hT = sb("hT", [P, KC, SEQ])
        ca_k = sb("ca_k", [P, 2, MEM])[:, :, :]
        ca_v = sb("ca_v", [P, 2, W_BR])[:, :, :]
        v_first = sb("v_first", [P, 2, SEQ])
        par = sb("par", [P, DEPTH, N_PAR])
        mw = sb("mw", [P, N_MIX])
        con = sb("con", [P, N_CON])
        pos = sb("pos", [P, 3], I32)
        trig = sb("trig", [P, 2, 3, ROPE_HALF])
        stat = sb("stat", [P, 64])
        idx = sb("idx", [P, 8], U32)
        load_of = sb("load_of", [P, N_EXP], I32)
        n_ptm, n_pfm = TT * (TM_END + 12), 12 * SEQ
        n_big = KC * MEM + n_ptm + n_pfm
        with ExitStack() as shared:
            def sb_shared(name, shape):
                return shared.enter_context(nc.sbuf_tensor(name, shape, F32))

            big = sb_shared("big", [P, n_big])
            arena = sb_shared("arena", [P, ARENA])
            oT = sb_shared("oT", [P, 2 * N_BR, SEQ])
        memT = big[:, 0:KC * MEM].rearrange("p (k t) -> p k t", k=KC)
        ptm = big[:, KC * MEM:KC * MEM + n_ptm].rearrange("p (t c) -> p t c", t=TT)
        pfm = big[:, KC * MEM + n_ptm:].rearrange("p (c t) -> p c t", c=12)
        with ExitStack() as shared:
            def sb_split(name, shape):
                return shared.enter_context(nc.sbuf_tensor(name, shape, F32R))

            sb_split("memory_kept", [P, KC * MEM])
            h_parts = sb_split("h_parts", [P, 2, KC, SEQ])
            sb_split("scaled_kept", [P, n_big - KC * MEM - 2 * KC * SEQ + FFN_FIRST])
            gu_w = sb_split("gate_up_w", [P, 2, 2, 2 * OCT])
        with ExitStack() as shared:
            y_high = sb_split("y_high", [P, N_EXP, D])
            sb_split("routing_kept", [P, n_big - N_EXP * D + MOE_FIRST])
            y_low = sb_split("y_low", [P, N_EXP, D])
            selT = sb_split("selT", [P, N_EXP, TT, P])
        sb("arena_kept", [P, n_big + FFN_ARENA])
        down_w = sb("down_w", [P, 2, 2, D], F32R)
        hid = sb("hid", [P, 2, 2, SEQ], F32R)
        ps = ctx.enter_context(nc.psum_tensor("ps", [P, 8 * 512], F32))

        def bank(b, n=1):
            return ps[:, b * 512:(b + n) * 512]

        class Carve:

            def __init__(self, at=0):
                self.at = at

            def __call__(self, *shape):
                n = int(np.prod(shape))
                v = arena[:, self.at:self.at + n]
                self.at += n
                assert self.at <= ARENA, self.at
                names = "abcde"[:len(shape)]
                if len(shape) == 1:
                    return v
                return v.rearrange("p (" + " ".join(names) + ") -> p " + " ".join(names),
                                   **dict(zip(names, shape)))

        def parc(l, name, i=0, n=1):
            c = PAR[name] + i
            return par[:, l, c:c + n]

        def conc(name, a=0, n=None):
            c = CON[name] + a
            return con[:, c:c + (CON_COLS[name] - a if n is None else n)]

        def mixc(name, a=0, n=128):
            return mw[:, MIX[name] + a:MIX[name] + a + n]

        def spread(ap, axis, n):
            v = ap.unsqueeze(axis)
            shape = list(v.shape)
            shape[axis] = n
            return v.broadcast_to(shape)

        ident = conc("ident")

        c = Carve()
        xn = c(TT, D)
        mem_sb = c(TT, D)

        c = Carve()
        qpad = c(2, 2, SEQ)
        kT = c(2, SEQ)
        prob = c(2, 4, SEQ)
        probT = c(8, P)
        att_tmp = c(4, HD)
        o_tm = c(TT, 4, HD)
        kc2 = c(2, 2, SEQ)
        hid_c = c(2, 2 * N_CMP)
        hid_pe = c(2)
        k_cmp = c(2, HD)
        v_cmp = c(2, HD)
        kcT = c(N_CMP)
        cprob = c(2, 4, N_CMP)
        cprobT = c(8, P)
        rope_a, rope_b, rope_c, rope_d = (c(2, 8, 8) for _ in range(4))
        gates = c(TT, 12)
        kc_dup = c(TT, 4, 2, HD)
        c = Carve(D)
        ca_oT = c(2, SEQ)

        c = Carve(ARENA - N_BR * N_EARLY * SEQ)
        early = c(N_EARLY, N_BR, SEQ)

        c = Carve()
        poolT = c(2, SEQ)

        c = Carve()
        gl_z, gl_e, gl_b, gl_eq, gl_ek, gl_ke = (c(SEQ) for _ in range(6))
        gl_dl = c(N_GL)
        gl_q = c(4, SEQ)
        gl_att = c(TT, 4, P)
        gl_k8 = c(TT, 8, P)
        gl_s = c(N_GL, HD)
        gl_o = c(2, SEQ)
        gl_sq = c(2, SEQ)
        gl_r = c(2, SEQ)
        gl_og = c(2, SEQ)

        c = Carve()
        rw_kr = c(2, 2, 2, SEQ)
        rw_ab = c(TT, 2, 2, 2, P)
        rw_ak = c(TT, 2, 2, 2, P)
        rw_km = c(TT, 2, 2, P)
        rw_bm = c(TT, 2, 2, P)
        rw_ep, rw_g, rw_bt, rw_kt, rw_rk, rw_bonus = (c(2, SEQ) for _ in range(6))
        rw_s = c(2, 2, HD)
        rw_lrx = c(SEQ)
        work = c.at
        rw_lw, rw_cl, rw_clm, rw_em, rw_kk, rw_sq, rw_a, rw_k2 = (c(2, SEQ) for _ in range(8))
        c = Carve(work)
        rw_x = c(8, P)
        rw_xt = c(8, P)
        rw_t1 = c(8, P)
        rw_v = c(TT, W_BR)
        rw_z = c(W_BR)
        rw_u = c(W_BR)
        c = Carve(work)
        rw_y, rw_yc, rw_y2, rw_r = (c(2, SEQ) for _ in range(4))
        rw_top = work + 8 * 512
        c = Carve(rw_top)
        rw_vg = c(2, SEQ)

        c = Carve()
        merged = c(KC, SEQ)
        sig = c(4, SEQ)
        mtmp = c(4, SEQ)
        mtmp2 = c(4, SEQ)
        c = Carve(TT * D)
        silu = c(2, SEQ)
        product = c(2, SEQ)
        assert c.at <= FFN_FIRST, c.at
        combine = c(TT, N_EXP)
        comb_few = c(TT, N_EXP)
        comb_many = c(TT, N_EXP)
        few = c(N_EXP)
        picked = c(TT, N_EXP)
        place = c(TT, N_EXP)
        logit = c(TT, N_EXP)
        top = c(TT, 8)
        topi = c(TT, 8)
        pick = c(TT, N_EXP)
        sel = c(2, TT, P)
        w_slot = c(N_EXP)
        assert c.at <= MOE_FIRST, c.at
        c = Carve(MOE_FIRST)
        h_exp = c(N_EXP, KC, P)
        assert c.at + N_EXP * TT * P <= FFN_ARENA, c.at
        c = Carve()
        fin_gain = c(D)
        fin_x = c(TT, D)

        def merge_octet(l, n):
            j, i = n // N_BR, n % N_BR
            o = O_MERGE + N_EARLY + j * (N_BR + 1) + 1 + i if n < 8 else O_OUT + n - 8
            return FIRST_SLAB[l] + N_TM + N_FM + o // 3, (o % 3) * OCT

        def octet_part(n, part):
            return gu_w[:, (n % 4) // 2, part, (n % 2) * OCT:(n % 2 + 1) * OCT]

        landed = [sem(f"slab_landed_{i}") for i in range(RING)]
        slab_read = sem("slab_read")
        mem_loaded = sem("memory_loaded")
        par_loaded = sem("parameters_loaded")
        x_loaded = sem("x_loaded")
        con_loaded = sem("constants_loaded")
        mix_loaded = sem("mix_loaded")
        gain_loaded = sem("gain_loaded")
        stored = sem("stored")
        dve_step = sem("dve_step")
        act_step = sem("act_step")
        root_ready = sem("root_ready")
        root_done = sem("root_done")
        trig_arg = sem("trig_arg")
        trig_done = sem("trig_done")
        squares = sem("squares")
        x_scaled = sem("x_scaled")
        x_turned = sem("x_turned")
        h_ready = sem("h_ready")
        proj_done = sem("proj_done")
        proj_dve = sem("proj_copied_dve")
        proj_act = sem("proj_copied_act")
        roped = sem("roped")
        nsa_turned = sem("nsa_turned")
        q_padded = sem("q_padded")
        kT_copied = sem("kT_copied")
        kc_copied = sem("kc_copied")
        cmp_hidden = sem("cmp_hidden")
        cmp_gelu = sem("cmp_gelu")
        cmp_kv = sem("cmp_kv")
        cmp_kv_copied = sem("cmp_kv_copied")
        cmp_kturned = sem("cmp_kturned")
        cmp_kcopied = sem("cmp_kcopied")
        cmp_scored = sem("cmp_scored")
        cmp_shifted = sem("cmp_shifted")
        cmp_exp = sem("cmp_exp")
        cmp_prob = sem("cmp_prob")
        cmp_pturned = sem("cmp_pturned")
        cmp_pcopied = sem("cmp_pcopied")
        cmp_out = sem("cmp_out")
        cmp_added = sem("cmp_added")
        gates_on = sem("gates_on")
        scored = sem("scored")
        score_max = sem("score_max")
        exped = sem("exped")
        p_turned = sem("p_turned")
        p_copied = sem("p_copied")
        att_out = sem("att_out")
        o_added = sem("o_added")
        o_turned = sem("o_turned")
        o_copied = sem("o_copied")
        pool_d = sem("pool_d")
        pool_dc = sem("pool_dcopied")
        pool_y = sem("pool_y")
        pool_o = sem("pool_o")
        gl_pe = sem("gla_products")
        gl_dve = sem("gla_dve")
        gl_act = sem("gla_act")
        rw_pe = sem("rwkv_products")
        rw_dve = sem("rwkv_dve")
        rw_act = sem("rwkv_act")
        rw_out = sem("rwkv_out")
        inv_pe = sem("inverse_products")
        inv_dve = sem("inverse_dve")
        seq_pe = sem("chunk_products")
        seq_dve = sem("chunk_dve")
        fill_done = sem("late_projections")
        fill_copied = sem("late_projections_copied")
        early_done = sem("early_gate_products")
        early_copied = sem("early_gates_copied")
        early_sig = sem("early_sigmoids")
        branch_done = sem("branch_products")
        branch_used = sem("branches_added")
        gate_done = sem("gate_products")
        gate_sig = sem("gate_sigmoids")
        gate_used = sem("gate_used")
        hm_high = sem("gate_input_high")
        hm_split = sem("gate_input_split")
        oct_high = sem("octets_high")
        oct_split = sem("octets_split")
        merged_high = sem("merged_high")
        merged_split = sem("merged_split")
        out_used = sem("out_products")
        merged_out = sem("merged_out")
        x_tile = sem("x_tile_added")
        mem_done = sem("mem_products")
        mem_copied = sem("mem_copied")
        caq_done = sem("caq_done")
        caq_padded = sem("caq_padded")
        cao_done = sem("cao_done")
        routed = sem("router_logits")
        top_diff = sem("top_differences")
        top_exp = sem("top_exp")
        placed = sem("places_counted")
        sel_ready = sem("selections_ready")
        gathered = sem("tokens_gathered")
        gathered_c = sem("tokens_copied")
        load_ready = sem("expert_loads_ready")
        scattered = sem("outputs_scattered")
        x_moe = sem("x_moe")
        gu_done = sem("gate_up_done")
        silu_done = sem("silu_done")
        hid_ready = sem("hidden_ready")
        h_high = sem("input_high")
        h_split = sem("input_split")
        gu_high = sem("gate_up_weights_high")
        gu_split = sem("gate_up_weights_split")
        down_split = sem("down_weights_high")
        down_used = sem("down_products")
        x_added = sem("x_added")
        y_ready = sem("output_high")
        fin_ready = sem("fin_ready")
        fin_sq = sem("fin_squares")

        block = ctx.enter_context(nc.Block())

        @block.sync
        def _(sp):
            sp.dma_start(mem_sb, mem_in).then_inc(mem_loaded, 16)
            sp.dma_start(con[:, 0:P], consts[:, 0:P]).then_inc(par_loaded, 16)
            sp.dma_start(par[:, :, :], params.rearrange("l p c -> p l c")).then_inc(par_loaded, 16)
            sp.dma_start(x[:, :, :], x_in).then_inc(x_loaded, 16)
            for n in range(min(RING, n_slabs)):
                sp.dma_start(ring[:, n, :], stream[n]).then_inc(landed[n], 16)
                if n == 0:
                    sp.dma_start(pos[:, :], pos_in).then_inc(con_loaded, 16)
                    sp.dma_start(mw[:, :], mixw[0]).then_inc(mix_loaded, 16)
                if n == 2:
                    sp.dma_start(con[:, P:N_CON], consts[:, P:N_CON]).then_inc(con_loaded, 16)
            rounds = (n_slabs - RING) // RING
            if rounds > 0:
                with sp.Fori(0, rounds) as i:
                    for k in range(RING):
                        sp.wait_ge(slab_read, i * RING + (k + 1))
                        sp.dma_start(ring[:, k, :], stream[i * RING + (RING + k)]).then_inc(landed[k], 16)
            for n in range(RING + rounds * RING, n_slabs):
                sp.wait_ge(slab_read, n - RING + 1)
                sp.dma_start(ring[:, n % RING, :], stream[n]).then_inc(landed[n % RING], 16)
            if PLAN[-1][0] == "final":
                for tt in range(TT):
                    sp.wait_ge(fin_ready, tt + 1)
                    sp.dma_start(out[:, tt, :], fin_x[:, tt, :]).then_inc(stored, 16)
                sp.wait_ge(stored, 16 * TT)

        @block.tensor
        def _(pe):
            reading = {"slab": -1}

            def mm(o, a, b, start=True, stop=True):
                return pe.matmul(o, a, b, start=start, stop=stop, skip_group_check=True)

            def slab(n):
                if reading["slab"] != n:
                    pe.wait_ge(landed[n % RING], 16 * (n // RING + 1))
                    reading["release"] = reading["slab"] >= 0
                    reading["slab"] = n
                return ring[:, n % RING, :]

            def octet(l, o):
                s = slab(FIRST_SLAB[l] + N_TM + N_FM + o // 3)
                return s[:, (o % 3) * OCT:(o % 3 + 1) * OCT]

            def first(ins):
                if reading.get("release"):
                    ins.then_inc(slab_read, 1)
                    reading["release"] = False

            def turn(o, i, n=P):
                return pe.transpose(o, i, conc("ident")[0:n, 0:n])

            def norm(k):
                for tt in range(TT):
                    pe.wait_ge(x_scaled, TT * k + tt + 1)
                    for kc in range(KC):
                        t = turn(bank(kc // 2)[:, (kc % 2) * 256 + tt * P:(kc % 2) * 256 + (tt + 1) * P],
                                 xn[:, tt, kc * P:(kc + 1) * P])
                        if tt == TT - 1 and kc % 2:
                            t.then_inc(x_turned, 1)

            def project(l):
                for b in range(6):
                    if b == 4:
                        w = slab(FIRST_SLAB[l] + 2)[:, OCT:2 * OCT]
                        for tt in range(TT):
                            for kc in range(KC):
                                m = mm(bank(4)[:, tt * 12:(tt + 1) * 12], hT[:, kc, tt * P:(tt + 1) * P],
                                       w[:, kc * P + MISC_GATES:kc * P + MISC_GATES + 12],
                                       kc == 0, kc == KC - 1)
                        m.then_inc(proj_done, 1)
                        continue
                    for ch in ((2 * b, 2 * b + 1) if b < 4 else (8,)):
                        m = fm_chunk(l, ch, bank(b or 6)[:, (ch % 2) * 256:(ch % 2) * 256 + 256])
                    m.then_inc(proj_done, 1)

            def fm_chunk(l, ch, o):
                w = slab(FIRST_SLAB[l] + (ch // 3 if ch < 9 else FM_FIRST + N_TM))
                w = w[:, (ch % 3) * OCT:(ch % 3 + 1) * OCT]
                for kc in range(KC):
                    if ch == 0:
                        pe.wait_ge(h_ready, KC * (1 + 3 * l) + kc + 1)
                    m = mm(o, w[:, kc * P:(kc + 1) * P], hT[:, kc, :], kc == 0, kc == KC - 1)
                    if kc == 0:
                        first(m)
                return m

            def fill(l, k):
                if k == 0:
                    pe.wait_ge(proj_act, 4 * l + 3)
                else:
                    pe.wait_ge(fill_copied, 10 * l + k)
                if k < 8:
                    w = slab(FIRST_SLAB[l] + FM_FIRST + k // 2).rearrange("p (k c) -> p k c", k=KC)
                    for kc in range(KC):
                        m = mm(bank(4)[:, 0:384], hT[:, kc, (k % 2) * P:(k % 2 + 1) * P], w[:, kc, :],
                               kc == 0, kc == KC - 1)
                        if kc == 0:
                            first(m)
                elif k == 8:
                    fm_chunk(l, 9, bank(4)[:, 0:256])
                    m = fm_chunk(l, 10, bank(4)[:, 256:512])
                else:
                    m = fm_chunk(l, 11, bank(4)[:, 0:256])
                m.then_inc(fill_done, 1)

            def gate(l, g, half=0):
                if g and half == 0:
                    pe.wait_ge(early_copied, N_BR * N_EARLY * l + g)
                w = octet(l, O_GATE + g)
                for kc in range(KC):
                    m = mm(bank(7)[:, half * 256:half * 256 + 256], w[:, kc * P:(kc + 1) * P], hT[:, kc, :],
                           kc == 0, kc == KC - 1)
                    if kc == 0:
                        first(m)
                m.then_inc(early_done, 1)

            def scores(u, tt, keys):
                nk = keys.shape[2]
                for hp in range(2):
                    for h2 in range(2):
                        h = 2 * h2 + hp if u % 6 < 4 else 2 * hp + h2
                        m = mm(bank(2 * (u % 2) + h // 2)[:, (h % 2) * 256:(h % 2) * 256 + nk],
                               qpad[:, hp, h2, tt * P:(tt + 1) * P], keys[:, hp, :])
                m.then_inc(scored, 1)

            def turn_probs(u, nk):
                pe.wait_ge(exped, u + 1)
                for h in range(4):
                    for kb in range(nk // P):
                        m = turn(bank(4, 2)[:, (2 * h + kb) * P:(2 * h + kb + 1) * P],
                                 prob[:, u % 2, h, kb * P:(kb + 1) * P])
                m.then_inc(p_turned, 1)

            def weigh(u, values, nk):
                pe.wait_ge(p_copied, u + 1)
                for h in range(4):
                    for kb in range(nk // P):
                        m = mm(bank(6)[:, h * HD:(h + 1) * HD], probT[:, 2 * h + kb, :],
                               values(h, kb), kb == 0, kb == nk // P - 1)
                m.then_inc(att_out, 1)

            def turn_out(l, which):
                pe.wait_ge(o_added, 6 * l + (4 if which == 0 else 6))
                for cc in range(2):
                    for tt in range(TT):
                        m = turn(bank(0)[:, cc * 256 + tt * P:cc * 256 + (tt + 1) * P],
                                 o_tm[:, tt, 2 * cc:2 * cc + 2, :].rearrange("p a b -> p (a b)"))
                m.then_inc(o_turned, 1)

            def nsa(l):
                pe.wait_ge(roped, l + 1)
                for r in range(2):
                    for tt in range(TT):
                        turn(bank(0)[:, (2 * r + tt) * P:(2 * r + tt + 1) * P],
                             ptm[:, tt, TM_Q + r * P:TM_Q + (r + 1) * P])
                for a, at in enumerate((TM_KS, TM_KW)):
                    for tt in range(TT):
                        turn(bank(1)[:, (2 * a + tt) * P:(2 * a + tt + 1) * P], ptm[:, tt, at:at + P])
                for j in range(2):
                    for g in range(2):
                        for tt in range(TT):
                            m = turn(bank(2 + j)[:, (2 * g + tt) * P:(2 * g + tt + 1) * P],
                                     kc_dup[:, tt, 2 * j + g, :, :].rearrange("p a b -> p (a b)"))
                m.then_inc(nsa_turned, 1)
                pe.wait_ge(mem_copied, 2 * (l + 1))
                pe.wait_ge(kc_copied, l + 1)
                for j in range(2):
                    for lp in range(16):
                        w = octet(l, O_CMP + 2 * j + lp // 8)[:, (lp % 8) * P:(lp % 8 + 1) * P]
                        t = kc2[:, j, :, :].rearrange("p g (m a b) -> p g m a b", a=8, b=2)
                        t = t[:, :, lp // 8:lp // 8 + N_CMP, lp % 8, 0]
                        o = bank(4)[:, j * 32:j * 32 + 2 * N_CMP].rearrange("p (g n) -> p g n", g=2)
                        first(mm(o, w, t, lp == 0, lp == 15))
                        m = mm(bank(5)[:, j:j + 1], w, parc(l, "pe", j * 16 + lp), lp == 0, lp == 15)
                m.then_inc(cmp_hidden, 1)
                gate(l, 0)
                pe.wait_ge(cmp_gelu, 2 * (l + 1))
                for j in range(2):
                    for g in range(2):
                        m = mm(bank(6)[0:N_CMP, (2 * j + g) * HD:(2 * j + g + 1) * HD],
                               hid_c[:, j, g * N_CMP:(g + 1) * N_CMP], mixc("cmp", j * HD, HD))
                m.then_inc(cmp_kv, 1)
                gate(l, 1)
                pe.wait_ge(cmp_kv_copied, l + 1)
                turn(bank(6)[:, 0:N_CMP], k_cmp[0:N_CMP, :, :].rearrange("p a b -> p (a b)"),
                     N_CMP).then_inc(cmp_kturned, 1)
                pe.wait_ge(cmp_kcopied, l + 1)
                pe.wait_ge(q_padded, l + 1)
                for tt in range(TT):
                    for h in range(4):
                        m = mm(bank(5)[:, (4 * tt + h) * N_CMP:(4 * tt + h + 1) * N_CMP],
                               qpad[:, h % 2, h // 2, tt * P:(tt + 1) * P], kcT)
                m.then_inc(cmp_scored, 1)
                pe.wait_ge(kT_copied, l + 1)
                units = [(6 * l, 0, 0), (6 * l + 1, 0, 1), (6 * l + 2, 1, 0), (6 * l + 3, 1, 1)]

                def keys(a, tt):
                    return spread(kT[:, a, 0:P * (tt + 1)], 1, 2)

                def values(a):
                    at = TM_VS if a == 0 else TM_VW
                    return lambda h, kb: ptm[:, kb, at + (h // 2) * HD:at + (h // 2 + 1) * HD]

                scores(units[0][0], units[0][2], keys(units[0][1], units[0][2]))
                gate(l, 2)
                pe.wait_ge(cmp_prob, l + 1)
                for h in range(8):
                    m = turn(bank(4, 2)[0:N_CMP, h * P:(h + 1) * P], cprob[:, h // 4, h % 4, :])
                m.then_inc(cmp_pturned, 1)
                pe.wait_ge(cmp_pcopied, l + 1)
                for h in range(8):
                    m = mm(bank(6)[:, h * HD:(h + 1) * HD], cprobT[0:N_CMP, h, :],
                           v_cmp[0:N_CMP, (h % 4) // 2, :])
                m.then_inc(cmp_out, 1)
                for n, (u, a, tt) in enumerate(units):
                    if n < 3:
                        u2, a2, t2 = units[n + 1]
                        if n >= 1:
                            pe.wait_ge(score_max, u)
                        scores(u2, t2, keys(a2, t2))
                    gate(l, 3 + 3 * n)
                    gate(l, 4 + 3 * n, 1)
                    turn_probs(u, P * (tt + 1))
                    gate(l, 5 + 3 * n)
                    if n == 0:
                        pe.wait_ge(cmp_added, l + 1)
                    else:
                        pe.wait_ge(o_added, u)
                    weigh(u, values(a), P * (tt + 1))
                gate(l, 15)
                turn_out(l, 0)

            def pool(l):
                pe.wait_ge(o_copied, 2 * l + 1)
                for pr in range(2):
                    for g2 in range(2):
                        g = 2 * pr + g2
                        o = bank(5)[g2 * HD:(g2 + 1) * HD, pr * 256:(pr + 1) * 256]
                        for tt in range(TT):
                            u = ptm[:, tt, TM_POOL + g * HD:TM_POOL + (g + 1) * HD]
                            if tt == 0:
                                m = mm(o, u, conc("pool", 384 * g, 256), True, False)
                            else:
                                m = mm(o[:, P:2 * P], u, conc("pool", 384 * g + 256, P), False, True)
                m.then_inc(pool_d, 1)
                gate(l, 16)
                pe.wait_ge(pool_dc, l + 1)
                for pr in range(2):
                    m = mm(bank(6)[:, pr * 256:(pr + 1) * 256], mixc("pool", pr * P), poolT[:, pr, :])
                m.then_inc(pool_y, 1)

            def gla(l):
                pe.wait_ge(pool_o, l + 1)
                mm(bank(0)[:, 0:256], mixc("gla_a2"), pfm[:, FM_MISC, :]).then_inc(gl_pe, 1)
                gate(l, 17)
                gate(l, 18)
                pe.wait_ge(gl_dve, 7 * l + 3)
                for tt in range(TT):
                    m = mm(bank(1 + tt), gl_ek[:, tt * P:(tt + 1) * P], gl_q[:, :, tt * P:(tt + 1) * P])
                m.then_inc(gl_pe, 1)
                for tt in range(TT):
                    m = turn(bank(3)[:, tt * P:(tt + 1) * P], gl_ke[:, tt * P:(tt + 1) * P])
                m.then_inc(gl_pe, 1)
                gate(l, 19)
                pe.wait_ge(gl_dve, 7 * l + 4)
                for tt in range(TT):
                    for h in range(4):
                        for n in range(8):
                            m = mm(bank(4 + tt)[32 * h:32 * h + 32, n * HD:(n + 1) * HD],
                                   gl_k8[:, tt, n, 32 * h:32 * h + 32],
                                   ptm[:, tt, TM_GV + h * HD:TM_GV + (h + 1) * HD])
                m.then_inc(gl_pe, 1)
                gate(l, 20)
                gate(l, 21, 1)
                pe.wait_ge(gl_dve, 7 * l + 5)
                for hp in range(2):
                    for tt in range(TT):
                        for h2 in range(2):
                            h = 2 * hp + h2
                            o = bank(6)[h2 * HD:(h2 + 1) * HD, hp * 256 + tt * P:hp * 256 + (tt + 1) * P]
                            mm(o, ptm[:, tt, TM_GV + h * HD:TM_GV + (h + 1) * HD], gl_att[:, tt, h, :],
                               True, False)
                            for n in range(8):
                                m = mm(o[:, n * C_GL:(n + 1) * C_GL], gl_s[:, 8 * tt + n, :],
                                       gl_q[:, h, tt * P + n * C_GL:tt * P + (n + 1) * C_GL], False, n == 7)
                m.then_inc(gl_pe, 1)
                gate(l, 22)
                pe.wait_ge(gl_dve, 7 * l + 6)
                mm(bank(0), conc("ones"), gl_sq.rearrange("p a b -> p (a b)")).then_inc(gl_pe, 1)
                gate(l, 23)

            def memory_keys(l, cc):
                if cc == 0:
                    pe.wait_ge(fill_copied, 10 * (l + 1))
                w = octet(l, O_KV + cc)
                for kc in range(KC):
                    m = mm(bank(4)[:, cc * 256:cc * 256 + 256], w[:, kc * P:(kc + 1) * P], memT[:, kc, :],
                           kc == 0, kc == KC - 1)
                    if kc == 0:
                        first(m)
                if cc == 1:
                    m.then_inc(mem_done, 1)

            def memory_values(l):
                for kc in range(KC):
                    w = octet(l, O_KV + 2 + kc // 4)[:, (kc % 4) * 256:(kc % 4 + 1) * 256]
                    for mt in range(2):
                        m = mm(bank(5 + mt)[:, 0:256], memT[:, kc, mt * P:(mt + 1) * P], w,
                               kc == 0, kc == KC - 1)
                        if kc % 4 == 0 and mt == 0:
                            first(m)
                m.then_inc(mem_done, 1)

            def rwkv(l):
                fill(l, 0)
                fill(l, 1)
                if l == 0:
                    pe.wait_ge(con_loaded, 32)
                pe.wait_ge(mix_loaded, 16 * (l + 1))
                pe.wait_ge(rw_act, 8 * l + 1)
                for hp in range(2):
                    mm(bank(0)[:, hp * 256:hp * 256 + 256], mixc("w2", hp * P), rw_lrx)
                    mm(bank(1)[:, hp * 256:hp * 256 + 256], mixc("a2", hp * P), rw_lrx)
                    if l:
                        mm(bank(3)[:, hp * 256:hp * 256 + 256], mixc("v2", hp * P), pfm[:, FM_MISC, :])
                    m = mm(bank(2)[:, hp * 256:hp * 256 + 256], mixc("g2", hp * P), rw_lrx)
                m.then_inc(rw_pe, 1)
                pe.wait_ge(rw_dve, 7 * l + 2)
                mm(bank(5), conc("ones"), rw_sq.rearrange("p a b -> p (a b)")).then_inc(rw_pe, 1)
                for k in range(2, 5):
                    fill(l, k)
                pe.wait_ge(rw_dve, 7 * l + 4)
                mm(bank(5), conc("ones"), rw_rk.rearrange("p a b -> p (a b)"))
                for tt in range(TT):
                    for hp in range(2):
                        i = 2 * tt + hp
                        turn(bank(6)[:, i * P:(i + 1) * P], rw_kt[:, hp, tt * P:(tt + 1) * P])
                        turn(bank(7)[:, i * P:(i + 1) * P], rw_bt[:, hp, tt * P:(tt + 1) * P])
                for tt in range(TT):
                    for hp in range(2):
                        kr = rw_kr[:, hp, :, :, tt * P:(tt + 1) * P].rearrange("p a b t -> p (a b) t")
                        m = mm(bank(2 * tt + hp), rw_bt[:, hp, tt * P:(tt + 1) * P], kr)
                m.then_inc(rw_pe, 1)
                fill(l, 5)
                pe.wait_ge(rw_dve, 7 * l + 5)
                for tt in range(TT):
                    for hp in range(2):
                        kr = rw_kr[:, hp, :, :, tt * P:(tt + 1) * P].rearrange("p a b t -> p (a b) t")
                        m = mm(bank(2 * tt + hp), rw_kt[:, hp, tt * P:(tt + 1) * P], kr)
                m.then_inc(rw_pe, 1)
                pe.wait_ge(rw_dve, 7 * l + 6)
                for tt in range(TT):
                    for hp in range(2):
                        m = turn(bank(5)[:, (2 * tt + hp) * P:(2 * tt + hp + 1) * P],
                                 pfm[:, FM_V + hp, tt * P:(tt + 1) * P])
                m.then_inc(rw_pe, 1)

                for j in range(6):
                    for g in range(2):
                        pe.wait_ge(inv_dve, 25 * l + max(1, 4 * j + g))
                        for q in range(4 * g, 4 * g + 4):
                            m = mm(bank(g)[:, (q % 4) * P:(q % 4 + 1) * P],
                                   rw_ab[:, q // 4, (q // 2) % 2, q % 2, 0, :], rw_x[:, q, :])
                        m.then_inc(inv_pe, 1)
                    for g in range(2):
                        pe.wait_ge(inv_dve, 25 * l + 4 * j + 2 + g)
                        for q in range(4 * g, 4 * g + 4):
                            at = slice((q % 4) * P, (q % 4 + 1) * P)
                            mm(bank(2 + g)[:, at], rw_xt[:, q, :], rw_t1[:, q, :])
                            m = mm(bank(6 + g)[:, at], rw_t1[:, q, :], rw_xt[:, q, :])
                        m.then_inc(inv_pe, 1)
                pe.wait_ge(inv_dve, 25 * (l + 1))

                for ch in range(4):
                    tt, par2 = ch // 2, ch % 2
                    rows = slice(64 * par2, 64 * par2 + 64)
                    tok = slice(ch * C_RW, (ch + 1) * C_RW)
                    if ch == 0:
                        pe.wait_ge(rw_act, 8 * l + 6)
                    else:
                        pe.wait_ge(seq_dve, 12 * l + 3 * ch)
                    for h in range(4):
                        o = bank(0)[rows, h * HD:(h + 1) * HD]
                        mm(o, rw_kr[:, h // 2, h % 2, 0, tok], rw_s[:, ch % 2, h // 2, :], True, False)
                        m = mm(o, rw_ak[:, tt, h // 2, h % 2, 0, rows], rw_v[:, tt, h * HD:(h + 1) * HD],
                               False, True)
                    m.then_inc(seq_pe, 1)
                    pe.wait_ge(seq_dve, 12 * l + 3 * ch + 1)
                    for h in range(4):
                        m = mm(bank(1)[rows, h * HD:(h + 1) * HD], rw_xt[:, 4 * tt + h, rows],
                               rw_z[:, h * HD:(h + 1) * HD])
                    m.then_inc(seq_pe, 1)
                    fill(l, 6 + ch)
                    pe.wait_ge(seq_dve, 12 * l + 3 * ch + 2)
                    for hp in range(2):
                        o = bank(3)[:, hp * P:(hp + 1) * P]
                        mm(o, rw_km[:, tt, par2, hp, :], rw_v[:, tt, hp * P:(hp + 1) * P], True, False)
                        m = mm(o, rw_bm[:, tt, par2, hp, :], rw_u[:, hp * P:(hp + 1) * P], False, True)
                    m.then_inc(seq_pe, 1)
                    for h in range(4):
                        o = bank(2)[(h % 2) * HD:(h % 2 + 1) * HD, (h // 2) * 256 + ch * C_RW:
                                    (h // 2) * 256 + (ch + 1) * C_RW]
                        mm(o, rw_s[:, ch % 2, h // 2, :], rw_kr[:, h // 2, h % 2, 1, tok], True, False)
                        mm(o, rw_v[:, tt, h * HD:(h + 1) * HD], rw_ak[:, tt, h // 2, h % 2, 1, rows],
                           False, False)
                        m = mm(o, rw_u[:, h * HD:(h + 1) * HD], rw_ab[:, tt, h // 2, h % 2, 1, rows],
                               False, True)
                    m.then_inc(seq_pe, 1)
                pe.wait_ge(rw_act, 8 * l + 7)
                mm(bank(0), conc("ones"), rw_y.rearrange("p a b -> p (a b)")).then_inc(rw_pe, 1)
                memory_keys(l, 0)
                pe.wait_ge(rw_dve, 7 * l + 7)
                mm(bank(1), conc("ones"), rw_y2.rearrange("p a b -> p (a b)")).then_inc(rw_pe, 1)
                memory_keys(l, 1)
                memory_values(l)

            def merge(l):
                pe.wait_ge(o_copied, 2 * l + 1)
                pe.wait_ge(pool_o, l + 1)
                pe.wait_ge(rw_out, l + 1)
                for j in range(N_EARLY):
                    if j >= 2:
                        pe.wait_ge(branch_used, N_EARLY * l + j - 1)
                    w = octet(l, O_MERGE + j)
                    for i in range(N_BR):
                        if j == 0 and i == N_BR - 1:
                            pe.wait_ge(gl_dve, 7 * (l + 1))
                        for kc in range(2):
                            m = mm(bank(2 * (1 - j % 2), 2)[:, i * 256:(i + 1) * 256],
                                   w[:, (2 * i + kc) * P:(2 * i + kc + 1) * P], oT[:, 2 * i + kc, :],
                                   kc == 0, kc == 1)
                            if i == 0 and kc == 0:
                                first(m)
                    m.then_inc(branch_done, 1)
                for j in range(KC - N_EARLY):
                    if j == 1:
                        pe.wait_ge(branch_used, N_EARLY * (l + 1))
                    o = O_MERGE + N_EARLY + j * (N_BR + 1)
                    for i in range(N_BR):
                        b = bank(4 * (1 - j) + i)
                        wb = octet(l, o)
                        for kc in range(2):
                            m = mm(b[:, 256:512], wb[:, (2 * i + kc) * P:(2 * i + kc + 1) * P],
                                   oT[:, 2 * i + kc, :], kc == 0, kc == 1)
                            if kc == 0:
                                first(m)
                    if j == 0:
                        pe.wait_ge(hm_split, l + 1)
                    for i in range(N_BR):
                        b = bank(4 * (1 - j) + i)
                        n = N_BR * j + i
                        octet(l, o + 1 + i)
                        pe.wait_ge(oct_split, 16 * l + n + 1)
                        for kc in range(KC):
                            for a, c in ((0, 0), (0, 1), (1, 0)):
                                m = mm(b[:, 0:256], octet_part(n, a)[:, kc * P:(kc + 1) * P], h_parts[:, c, kc, :],
                                       kc == 0 and (a, c) == (0, 0), kc == KC - 1 and a == 1)
                                if kc == 0:
                                    first(m)
                        m.then_inc(gate_done, 1)
                pe.wait_ge(gate_used, 8 * l + 4)
                for kc in range(KC):
                    octet(l, O_OUT + kc)
                    pe.wait_ge(oct_split, 16 * l + 8 + kc + 1)
                    pe.wait_ge(merged_split, KC * l + kc + 1)
                    for tt in range(TT):
                        for a, c in ((0, 0), (0, 1), (1, 0)):
                            for nb in range(2):
                                w = octet_part(kc, c)[:, nb * 512:(nb + 1) * 512]
                                m = mm(bank(4 + 2 * tt + nb), h_parts[:, a, kc, tt * P:(tt + 1) * P], w,
                                       kc == 0 and (a, c) == (0, 0), kc == KC - 1 and a == 1)
                                if tt == 0 and nb == 0:
                                    first(m)
                        if kc == KC - 1:
                            m.then_inc(merged_out, 1)
                    if kc < 4:
                        m.then_inc(out_used, 1)

            def cross(l):
                for cc in range(2):
                    w = octet(l, O_CQ + cc)
                    for kc in range(KC):
                        if cc == 0:
                            pe.wait_ge(h_ready, KC * (2 + 3 * l) + kc + 1)
                        m = mm(bank(4)[:, cc * 256:cc * 256 + 256], w[:, kc * P:(kc + 1) * P], hT[:, kc, :],
                               kc == 0, kc == KC - 1)
                        if kc == 0:
                            first(m)
                m.then_inc(caq_done, 1)
                pe.wait_ge(caq_padded, l + 1)
                for tt in range(TT):
                    scores(6 * l + 4 + tt, tt, ca_k)
                for tt in range(TT):
                    turn_probs(6 * l + 4 + tt, MEM)
                    if tt:
                        pe.wait_ge(o_added, 6 * l + 5)
                    weigh(6 * l + 4 + tt, lambda h, kb: ca_v[:, kb, h * HD:(h + 1) * HD], MEM)
                turn_out(l, 1)
                pe.wait_ge(o_copied, 2 * l + 2)
                for kc in range(2):
                    w = octet(l, O_CO + kc)
                    for tt in range(TT):
                        for nb in range(2):
                            m = mm(bank(2 * tt + nb), ca_oT[:, kc, tt * P:(tt + 1) * P],
                                   w[:, nb * 512:(nb + 1) * 512], kc == 0, kc == 1)
                            if tt == 0 and nb == 0:
                                first(m)
                        if kc == 1:
                            m.then_inc(cao_done, 1)

            def gate_up(at, h, width):
                b = bank(4 + at % 2)
                w = ring[:, at % RING, :]
                for half in range(2):
                    for kc in range(KC):
                        m = mm(b[:, half * 256:half * 256 + width],
                               w[:, half * OCT + kc * P:half * OCT + (kc + 1) * P], h[:, kc, 0:width],
                               kc == 0, kc == KC - 1)
                m.then_inc(gu_done, 1)

            def gate_up_split(at, f):
                b = bank(4 + at % 2)
                for half in range(2):
                    for kc in range(KC):
                        for n, (a, c) in enumerate(((0, 0), (0, 1), (1, 0))):
                            if f == 0 and half == 0 and n == 0:
                                pe.wait_ge(h_split, kc + 1)
                            w = gu_w[:, at % 2, a, half * OCT + kc * P:half * OCT + (kc + 1) * P]
                            m = mm(b[:, half * 256:half * 256 + SEQ], w, h_parts[:, c, kc, :],
                                   kc == 0 and n == 0, kc == KC - 1 and n == 2)
                            if f == 0 and half == 0 and kc == 0 and n == 0:
                                m.then_inc(slab_read, 1)
                m.then_inc(gu_done, 1)

            def down(f, at, width):
                for tt in range((width + P - 1) // P):
                    n = min(width, P)
                    for a, b in ((0, 0), (1, 0), (0, 1)):
                        for nb in range(2):
                            m = mm(bank(2 * tt + nb)[0:n, :], hid[:, at % 2, a, tt * P:tt * P + n],
                                   down_w[:, at % 2, b, nb * 512:(nb + 1) * 512],
                                   f == 0 and (a, b) == (0, 0), f == FC - 1 and b == 1)
                m.then_inc(down_used, 1)

            def expert(c0, e0, slab0, h, width, up=0, ups=0, upe=0):
                for f in range(FC + 1):
                    if f < FC:
                        if c0 + f >= 2:
                            pe.wait_ge(hid_ready, up + (c0 + f - 1))
                        if h is None:
                            pe.wait_ge(gu_split, f + 1)
                            gate_up_split(slab0 + f, f)
                        else:
                            pe.wait_ge(landed[(slab0 + f) % RING], ups * 16 + 16 * ((slab0 + f) // RING + 1))
                            gate_up(slab0 + f, h, width)
                    if f >= 1:
                        if f == 1 and e0 >= 1:
                            pe.wait_ge(gathered_c, N_EXP)
                            pe.wait_ge(x_added, upe + e0)
                        pe.wait_ge(hid_ready, up + (c0 + f))
                        down(f - 1, slab0 + f - 1, width)

            def ffn(l):
                expert(0, 0, LAYER_SLABS, None, SEQ)
                reading["slab"] = -1

            def moe(l):
                for tt in range(TT):
                    for kc in range(KC):
                        if tt == 0:
                            pe.wait_ge(h_ready, KC * (3 + 3 * l) + kc + 1)
                        m = mm(bank(6)[:, tt * 8:tt * 8 + 8], hT[:, kc, tt * P:(tt + 1) * P],
                               parc(l, "router", 8 * kc, 8), kc == 0, kc == KC - 1)
                        if tt == 0 and kc == 0:
                            m.then_inc(slab_read, 1)
                m.then_inc(routed, 1)
                pe.wait_ge(top_diff, 1)
                mm(bank(7)[:, 0:8], conc("before"), picked[:, 0, :])
                mm(bank(7)[:, 8:16], conc("every"), picked[:, 0, :], True, False)
                mm(bank(7)[:, 8:16], conc("before"), picked[:, 1, :], False, True)
                mm(bank(7)[:, 16:24], conc("every"), picked[:, 0, :], True, False)
                mm(bank(7)[:, 16:24], conc("every"), picked[:, 1, :], False, True).then_inc(placed, 1)
                for e in range(N_EXP):
                    pe.wait_ge(sel_ready, e + 1)
                    if e >= 2:
                        pe.wait_ge(gathered_c, e - 1)
                    for kc in range(KC):
                        for tt in range(TT):
                            mm(bank(2 * (e % 2), 2)[:, kc * P:(kc + 1) * P], xn[:, tt, kc * P:(kc + 1) * P],
                               sel[:, e % 2, tt, :], tt == 0, tt == 1)
                    for tt in range(TT):
                        turn(bank(6 + e % 2)[:, tt * P:(tt + 1) * P], sel[:, e % 2, tt, :])
                    for tt in range(TT):
                        m = mm(bank(6 + e % 2)[:, 256:257], sel[:, e % 2, tt, :], comb_few[:, tt, e:e + 1],
                               tt == 0, tt == 1)
                    m.then_inc(gathered, 1)
                pe.wait_ge(gathered_c, 1)
                pe.wait_ge(load_ready, 1)
                s0 = FIRST_SLAB[1] + LAYER_SLABS
                with pe.Fori(0, N_EXP // 2) as i:
                    for half in range(2):
                        ups = (i * (2 * FC), i * (2 * FC // RING), i * 2)
                        tokens = pe.value_load(load_of[0:1, bass.ds(i * 2 + half, 1)], min_val=0, max_val=SEQ)
                        own = h_exp[:, bass.ds(i * 2 + half, 1), :, :].rearrange("p e k t -> p (e k) t")
                        at = (FC * (1 + half), 1 + half, s0 + FC * half)
                        with pe.If(tokens < P + 1):
                            with pe.If(tokens < 3 * P // 4 + 1):
                                with pe.If(tokens < P // 2 + 1):
                                    expert(*at, own, P // 2, *ups)
                                with pe.Else():
                                    expert(*at, own, 3 * P // 4, *ups)
                            with pe.Else():
                                expert(*at, own, P, *ups)
                        with pe.Else():
                            expert(*at, hT, SEQ, *ups)
                for tt in range(TT):
                    for e in range(N_EXP):
                        if tt == 0 and e == N_EXP - 1:
                            pe.wait_ge(x_added, 1 + N_EXP)
                        for part, y in enumerate((y_high, y_low)):
                            for nb in range(2):
                                m = mm(bank(4 + 2 * tt + nb), selT[:, e, tt, :], y[:, e, nb * 512:(nb + 1) * 512],
                                       e == 0 and part == 0, e == N_EXP - 1 and part == 1)
                    m.then_inc(scattered, 1)

            def final(l):
                pass

            steps = dict(norm=norm, project=project, nsa=nsa, pool=pool, gla=gla, rwkv=rwkv, merge=merge,
                         cross=cross, ffn=ffn, moe=moe, final=final)
            pe.wait_ge(par_loaded, 32)
            for step, l in PLAN:
                steps[step](l)

        @block.scalar
        def _(act):
            n_step = [0]

            def link(ins):
                n_step[0] += 1
                ins.then_inc(act_step, 1)
                act.wait_ge(act_step, n_step[0])

            def warm(function):
                link(act.activation(stat[:, 60:61], conc("ident", 0, 1), function))

            n_root = [0]

            def root(a):
                n_root[0] += 1
                act.wait_ge(root_ready, n_root[0])
                act.activation(a, a, ACT.Sqrt).then_inc(root_done, 1)

            def high(f):
                at = LAYER_SLABS + f
                act.wait_ge(landed[at % RING], 16 * (at // RING + 1))
                if f >= 2:
                    act.wait_ge(gu_done, f - 1)
                act.copy(gu_w[:, at % 2, 0, :], ring[:, at % RING, 0:2 * OCT]).then_inc(gu_high, 1)

            def norm(k):
                warm(ACT.Sqrt)
                src = mem_sb if k == 0 else x
                for tt in range(TT):
                    if k == 0:
                        act.wait_ge(mem_loaded, 16)
                    elif k == 1:
                        act.wait_ge(x_loaded, 16)
                    elif k == 4 and tt == 1:
                        act.wait_ge(x_added, 1)
                    else:
                        act.wait_ge(x_tile, TT * (k - 2) + tt + (k < 5))
                    act.activation(xn[:, tt, :], src[:, tt, :], ACT.Square,
                                   accum_out=stat[:, tt:tt + 1]).then_inc(squares, 1)
                for tt in range(TT):
                    root(stat[:, tt:tt + 1])
                gain = ("mem_norm", 0) if k == 0 else (("norm_mix", "norm_ca", "norm_ffn")[(k - 1) % 3],
                                                        (k - 1) // 3)
                dst = memT if k == 0 else hT
                for kc in range(KC):
                    act.wait_ge(x_turned, KC // 2 * k + kc // 2 + 1)
                    act.activation(dst[:, kc, :], bank(kc // 2)[:, (kc % 2) * 256:(kc % 2) * 256 + 256],
                                   ACT.Copy, scale=parc(gain[1], gain[0], kc)).then_inc(h_ready, 1)
                    if k == 3:
                        act.activation(h_parts[:, 0, kc, :],
                                       bank(kc // 2)[:, (kc % 2) * 256:(kc % 2) * 256 + 256],
                                       ACT.Copy, scale=parc(gain[1], gain[0], kc)).then_inc(h_high, 1)

            def project(l):
                for n, b in enumerate((1, 3, 4, 5)):
                    act.wait_ge(proj_done, 6 * l + b + 1)
                    if b < 4:
                        m = act.copy(pfm[:, 2 * b:2 * b + 2, :].rearrange("p a b -> p (a b)"), bank(b))
                    elif b == 4:
                        m = act.copy(ptm[:, :, TM_END:TM_END + 12],
                                     bank(4)[:, 0:24].rearrange("p (a b) -> p a b", a=2))
                    else:
                        m = act.copy(pfm[:, 8, :], bank(5)[:, 0:256])
                    m.then_inc(proj_act, 1)
                if l == 0:
                    act.wait_ge(trig_arg, 1)
                    act.activation(trig[:, :, :, :], trig[:, :, :, :], ACT.Sin).then_inc(trig_done, 1)

            def copy_fill(l, k):
                act.wait_ge(fill_done, 10 * l + k + 1)
                if k < 8:
                    m = act.copy(ptm[:, k % 2, (k // 2) * 384:(k // 2 + 1) * 384], bank(4)[:, 0:384])
                elif k == 8:
                    m = act.copy(pfm[:, 9:11, :].rearrange("p a b -> p (a b)"), bank(4))
                else:
                    m = act.copy(pfm[:, 11, :], bank(4)[:, 0:256])
                m.then_inc(fill_copied, 1)

            def copy_gate(l, g, n=1):
                act.wait_ge(early_done, N_BR * N_EARLY * l + g + n)
                for half in range(n):
                    act.activation(early[:, (g + half) // N_BR, (g + half) % N_BR, :],
                                   bank(7)[:, half * 256:half * 256 + 256], ACT.Identity,
                                   bias=parc(l, "b_gate", 8 * ((g + half) % N_BR) + (g + half) // N_BR))\
                        .then_inc(early_copied, 1)

            def cross_probs(u):
                act.wait_ge(score_max, u + 1)
                for h in range(4):
                    m = act.activation(prob[:, u % 2, h, 0:MEM],
                                       bank(2 * (u % 2) + h // 2)[:, (h % 2) * 256:(h % 2) * 256 + MEM], ACT.Exp,
                                       scale=0.125, bias=stat[:, 8 + 8 * (u % 2) + h:9 + 8 * (u % 2) + h],
                                       accum_out=stat[:, 12 + 8 * (u % 2) + h:13 + 8 * (u % 2) + h])
                m.then_inc(exped, 1)

            def probs(u, nk):
                act.wait_ge(score_max, u + 1)
                for h in range(4):
                    m = act.activation(prob[:, u % 2, h, 0:nk], prob[:, u % 2, h, 0:nk], ACT.Exp,
                                       bias=stat[:, 8 + 8 * (u % 2) + h:9 + 8 * (u % 2) + h],
                                       accum_out=stat[:, 12 + 8 * (u % 2) + h:13 + 8 * (u % 2) + h])
                m.then_inc(exped, 1)

            def copy_probs(u, nk):
                act.wait_ge(p_turned, u + 1)
                v = bank(4, 2).rearrange("p (h k t) -> p h k t", h=4, k=2)[:, :, 0:nk // P, :]
                o = probT.rearrange("p (h k) t -> p h k t", h=4)[:, :, 0:nk // P, :]
                act.copy(o, v).then_inc(p_copied, 1)

            def nsa(l):
                act.wait_ge(nsa_turned, l + 1)
                act.copy(kT[:, :, :].rearrange("p a b -> p (a b)"), bank(1)).then_inc(kT_copied, 1)
                act.wait_ge(cmp_hidden, l + 1)
                link(act.copy(hid_pe, bank(5)[:, 0:2]))
                for j in range(2):
                    act.activation(hid_c[:, j, :], bank(4)[:, j * 32:j * 32 + 2 * N_CMP], ACT.Gelu_apprx_tanh,
                                   bias=hid_pe[:, j:j + 1]).then_inc(cmp_gelu, 1)
                copy_gate(l, 0)
                act.activation(gates, ptm[:, :, TM_END:TM_END + 12], ACT.Sigmoid).then_inc(gates_on, 1)
                copy_gate(l, 1)
                act.wait_ge(cmp_shifted, l + 1)
                cp = cprob.rearrange("p a b c -> p (a b c)")
                act.activation(cp, cp, ACT.Exp).then_inc(cmp_exp, 1)
                copy_gate(l, 2)
                probs(6 * l, P)
                act.wait_ge(cmp_pturned, l + 1)
                act.copy(cprobT[0:N_CMP, :, :].rearrange("p a b -> p (a b)"),
                         bank(4, 2)[0:N_CMP, :]).then_inc(cmp_pcopied, 1)
                for n in range(4):
                    copy_gate(l, 3 + 3 * n, 2)
                    copy_probs(6 * l + n, P * (n % 2 + 1))
                    if n < 3:
                        probs(6 * l + n + 1, P * ((n + 1) % 2 + 1))
                    copy_gate(l, 5 + 3 * n)
                copy_gate(l, 15)
                act.wait_ge(o_turned, 2 * l + 1)
                act.copy(oT[:, 0:2, :].rearrange("p a b -> p (a b)"), bank(0)).then_inc(o_copied, 1)

            def pool(l):
                copy_gate(l, 16)
                act.wait_ge(pool_y, l + 1)
                for pr in range(2):
                    m = act.activation(oT[:, 2 + pr, :], bank(6)[:, pr * 256:(pr + 1) * 256], ACT.Copy,
                                       scale=parc(l, "pool_scale", pr))
                m.then_inc(pool_o, 1)

            def gla(l):
                act.wait_ge(gl_dve, 7 * l + 1)
                link(act.activation(gl_e, gl_e, ACT.Exp, scale=-1.0))
                act.activation(gl_e, gl_e, ACT.Ln, bias=1.0).then_inc(gl_act, 1)
                copy_gate(l, 17)
                act.wait_ge(gl_dve, 7 * l + 2)
                act.activation(gl_eq, gl_b, ACT.Exp, scale=1.0 / 16)
                act.activation(gl_dl, gl_b[:, C_GL - 1:SEQ:C_GL], ACT.Exp, scale=1.0 / 16)
                act.activation(gl_ek, gl_b, ACT.Exp, scale=-1.0 / 16)
                act.activation(gl_ke, gl_ke, ACT.Exp, scale=1.0 / 16).then_inc(gl_act, 1)
                act.activation(gl_og, pfm[:, FM_OG:FM_OG + 2, :], ACT.Silu).then_inc(gl_act, 1)
                copy_gate(l, 18)
                copy_gate(l, 19)
                copy_gate(l, 20, 2)
                copy_gate(l, 22)
                warm(ACT.Sqrt)
                root(gl_r)
                copy_gate(l, 23)

            def rwkv(l):
                copy_fill(l, 0)
                act.wait_ge(rw_dve, 7 * l + 1)
                act.activation(rw_lrx[0:32, :], pfm[0:32, FM_LR, :], ACT.Tanh)
                act.copy(rw_lrx[32:64, :], pfm[32:64, FM_LR, :])
                act.activation(rw_lrx[64:128, :], pfm[64:128, FM_LR, :], ACT.Sigmoid).then_inc(rw_act, 1)
                copy_fill(l, 1)
                act.wait_ge(rw_pe, 7 * l + 1)
                for hp in range(2):
                    at = slice(hp * 256, hp * 256 + 256)
                    act.activation(rw_lw[:, hp, :], bank(0)[:, at], ACT.Sigmoid, bias=parc(l, "w0", hp))
                    act.activation(rw_a[:, hp, :], bank(1)[:, at], ACT.Sigmoid, bias=parc(l, "a0", hp))
                    if l:
                        act.activation(rw_vg[:, hp, :], bank(3)[:, at], ACT.Sigmoid, bias=parc(l, "v0", hp))
                act.copy(rw_g.rearrange("p a b -> p (a b)"), bank(2)).then_inc(rw_act, 1)
                root(rw_bt)
                copy_fill(l, 2)
                act.wait_ge(rw_dve, 7 * l + 3)
                act.activation(rw_ep, rw_cl, ACT.Exp)
                act.activation(rw_em, rw_cl, ACT.Exp, scale=-1.0)
                act.activation(rw_clm, rw_clm, ACT.Exp).then_inc(rw_act, 1)
                for k in range(3, 5):
                    copy_fill(l, k)
                act.wait_ge(rw_pe, 7 * l + 3)
                act.copy(rw_bonus.rearrange("p a b -> p (a b)"), bank(5)).then_inc(rw_act, 1)
                for par2 in range(2):
                    r = slice(64 * par2, 64 * par2 + 64)
                    act.mul(rw_bm[r, :, par2, :, :], bank(7)[r, :].rearrange("p (a b c) -> p a b c", a=2, b=2),
                            -1.0)
                    m = act.copy(rw_km[r, :, par2, :, :],
                                 bank(6)[r, :].rearrange("p (a b c) -> p a b c", a=2, b=2))
                m.then_inc(rw_act, 1)
                copy_fill(l, 5)
                act.wait_ge(rw_pe, 7 * l + 5)
                act.wait_ge(inv_dve, 25 * l + 1)
                act.copy(rw_v.rearrange("p a b -> p (a b)"), bank(5)).then_inc(rw_act, 1)
                for k in range(6, 10):
                    copy_fill(l, k)
                act.wait_ge(seq_pe, 16 * (l + 1))
                act.copy(rw_y.rearrange("p a b -> p (a b)"), bank(2)).then_inc(rw_act, 1)
                act.wait_ge(rw_pe, 7 * l + 6)
                act.copy(rw_r.rearrange("p a b -> p (a b)"), bank(0)).then_inc(rw_act, 1)
                warm(ACT.Sqrt)
                root(rw_r)
                act.wait_ge(mem_done, 2 * l + 1)
                act.copy(ca_k.rearrange("p a b -> p (a b)"), bank(4)).then_inc(mem_copied, 1)
                act.wait_ge(mem_done, 2 * (l + 1))
                act.copy(ca_v, bank(5, 2).rearrange("p (a b) -> p a b", a=2)[:, :, 0:256]).then_inc(mem_copied, 1)

            def merge(l):
                if l == 0:
                    act.wait_ge(gl_pe, 1)
                    act.dma_start(mw[:, :], mixw[1]).then_inc(mix_loaded, 16)
                act.wait_ge(early_copied, N_BR * N_EARLY * (l + 1))
                for j in range(N_EARLY):
                    act.activation(early[:, j], early[:, j], ACT.Sigmoid).then_inc(early_sig, 1)
                act.wait_ge(gl_dve, 7 * (l + 1))
                act.wait_ge(fill_copied, 10 * (l + 1))
                act.copy(h_parts[:, 0, :, :], hT[:, :, :]).then_inc(hm_high, 1)

                def octet_high(n):
                    at, col = merge_octet(l, n)
                    act.wait_ge(landed[at % RING], 16 * (at // RING + 1))
                    if n < 4:
                        act.wait_ge(branch_used, N_EARLY * l + (1 if n < 2 else 3))
                    elif n < 12:
                        act.wait_ge(gate_done, 8 * l + n - 3)
                    else:
                        act.wait_ge(out_used, 4 * l + n - 11)
                    act.copy(octet_part(n, 0), ring[:, at % RING, col:col + OCT]).then_inc(oct_high, 1)

                for n in range(4):
                    octet_high(n)
                for n in range(N_BR * (KC - N_EARLY)):
                    j, i = n // N_BR, n % N_BR
                    act.wait_ge(gate_done, 8 * l + n + 1)
                    if j:
                        act.wait_ge(gate_used, 8 * l + n - 3)
                    act.activation(sig[:, i, :], bank(4 * (1 - j) + i)[:, 0:256], ACT.Sigmoid,
                                   bias=parc(l, "b_gate", 8 * i + N_EARLY + j)).then_inc(gate_sig, 1)
                    if n < 6:
                        octet_high(n + 4)
                for kc in range(KC):
                    if kc < N_EARLY:
                        act.wait_ge(branch_used, N_EARLY * l + kc + 1)
                    else:
                        act.wait_ge(gate_used, 8 * l + N_BR * (kc - N_EARLY + 1))
                    act.copy(h_parts[:, 0, kc, :], merged[:, kc, :]).then_inc(merged_high, 1)
                for n in range(10, 16):
                    octet_high(n)

            def cross(l):
                warm(ACT.Exp)
                for tt in range(TT):
                    cross_probs(6 * l + 4 + tt)
                for tt in range(TT):
                    copy_probs(6 * l + 4 + tt, MEM)
                act.wait_ge(o_turned, 2 * l + 2)
                act.copy(ca_oT.rearrange("p a b -> p (a b)"), bank(0)).then_inc(o_copied, 1)
                if l == 0:
                    high(0)

            def silus(at, c, up, ups):
                if c >= FC:
                    act.wait_ge(landed[at % RING], ups * 16 + 16 * (at // RING + 1))
                if c >= 2:
                    act.wait_ge(down_used, up + (c - 1))
                act.copy(down_w[:, at % 2, 0, :], ring[:, at % RING, 2 * OCT:3 * OCT]).then_inc(down_split, 1)
                act.wait_ge(gu_done, up + (c + 1))
                act.activation(silu[:, at % 2, :], bank(4 + at % 2)[:, 0:256], ACT.Silu).then_inc(silu_done, 1)

            def ffn(l):
                for f in range(FC):
                    if f + 1 < FC:
                        high(f + 1)
                    silus(LAYER_SLABS + f, f, 0, 0)

            def moe(l):
                act.wait_ge(top_diff, 1)
                act.activation(pick, logit, ACT.Exp).then_inc(top_exp, 1)
                s0 = FIRST_SLAB[1] + LAYER_SLABS
                with act.Fori(0, N_EXP // 2) as i:
                    for f in range(2 * FC):
                        silus(s0 + f, FC + f, i * (2 * FC), i * (2 * FC // RING))

            def final(l):
                act.wait_ge(gathered, N_EXP)
                act.dma_start(fin_gain, gain_in).then_inc(gain_loaded, 16)
                warm(ACT.Sqrt)
                for tt in range(TT):
                    act.wait_ge(x_moe, tt + 1)
                    act.activation(fin_x[:, tt, :], x[:, tt, :], ACT.Square,
                                   accum_out=stat[:, tt:tt + 1]).then_inc(fin_sq, 1)
                    root(stat[:, tt:tt + 1])

            steps = dict(norm=norm, project=project, nsa=nsa, pool=pool, gla=gla, rwkv=rwkv, merge=merge,
                         cross=cross, ffn=ffn, moe=moe, final=final)
            act.wait_ge(par_loaded, 32)
            for step, l in PLAN:
                steps[step](l)

        @block.vector
        def _(dve):
            n_step = [0]

            def link(ins):
                n_step[0] += 1
                ins.then_inc(dve_step, 1)
                dve.wait_ge(dve_step, n_step[0])

            n_root = [0]

            def rooted(a, ins):
                n_root[0] += 1
                ins.then_inc(root_ready, 1)
                dve.wait_ge(root_done, n_root[0])
                link(dve.reciprocal(a, a))

            def tt_(o, a, b, op):
                return dve.tensor_tensor(o, a, b, op)

            def rope_tables():
                two_pi = 2 * np.pi
                c1 = 6.28125
                c2 = float(np.float32(np.floor((two_pi - c1) * 2.0 ** 20) / 2.0 ** 20))
                c3 = float(np.float32(two_pi - c1 - c2))
                magic = 1.5 * 2.0 ** 23
                ang = gl_z[:, 0:24]
                turns = gl_e[:, 0:48].rearrange("p (a b) -> p a b", a=2)
                posf = stat[:, 40:43]
                link(dve.tensor_copy(posf, pos[:, :]))
                link(tt_(ang.rearrange("p (a b) -> p a b", b=8), spread(posf, 2, 8), spread(conc("freq"), 1, 3),
                         ALU.mult))
                arg = trig[:, :, :, :].rearrange("p a b c -> p a (b c)")
                for s, quarter in ((0, 0.25), (1, 0.0)):
                    link(dve.tensor_scalar(turns[:, s, :], ang, 1.0 / two_pi, quarter, ALU.mult, ALU.add))
                    link(dve.tensor_scalar(turns[:, s, :], turns[:, s, :], magic, magic, ALU.add, ALU.subtract))
                    link(dve.scalar_tensor_tensor(out=arg[:, s, :], in0=turns[:, s, :], scalar=-c1, in1=ang,
                                                  op0=ALU.mult, op1=ALU.add))
                    for cc in (c2, c3):
                        link(dve.scalar_tensor_tensor(out=arg[:, s, :], in0=turns[:, s, :], scalar=-cc,
                                                      in1=arg[:, s, :], op0=ALU.mult, op1=ALU.add))
                link(dve.tensor_scalar(arg[:, 0, :], arg[:, 0, :], float(np.pi / 2), None, ALU.add))
                lim = float(np.nextafter(np.float32(np.pi), np.float32(0)))
                dve.tensor_scalar(arg, arg, lim, -lim, ALU.min, ALU.max).then_inc(trig_arg, 1)

            def rstd_of(s, scale, eps):
                rooted(s, dve.tensor_scalar(s, s, scale, eps, ALU.mult, ALU.add))

            def split(f):
                at = LAYER_SLABS + f
                dve.wait_ge(gu_high, f + 1)
                tt_(gu_w[:, at % 2, 1, :], ring[:, at % RING, 0:2 * OCT], gu_w[:, at % 2, 0, :],
                    ALU.subtract).then_inc(gu_split, 1)

            def norm(k):
                src = mem_sb if k == 0 else x
                for tt in range(TT):
                    dve.wait_ge(squares, TT * k + tt + 1)
                    rstd_of(stat[:, tt:tt + 1], 1.0 / D, EPS)
                    dve.tensor_scalar(xn[:, tt, :], src[:, tt, :], stat[:, tt:tt + 1], None, ALU.mult)\
                       .then_inc(x_scaled, 1)

            def project(l):
                if l == 0:
                    dve.wait_ge(h_ready, 2 * KC)
                    dve.wait_ge(con_loaded, 32)
                    rope_tables()
                for b in (0, 2):
                    dve.wait_ge(proj_done, 6 * l + b + 1)
                    dve.tensor_copy(pfm[:, 2 * b:2 * b + 2, :].rearrange("p a b -> p (a b)"), bank(b or 6))\
                       .then_inc(proj_dve, 1)
                dve.wait_ge(proj_dve, 2 * (l + 1))

            def rope(t1, t2, cos, sin, ta, tb, tc, td):
                tt_(ta, t1, cos, ALU.mult)
                tt_(tb, t2, sin, ALU.mult)
                tt_(tc, t2, cos, ALU.mult)
                link(tt_(td, t1, sin, ALU.mult))
                tt_(t1, ta, tb, ALU.subtract)
                return tt_(t2, tc, td, ALU.add)

            def shifted(u, tt, nk, mask, scale=0.125):
                dve.wait_ge(scored, u + 1)
                src = bank(2 * (u % 2), 2).rearrange("p (h k) -> p h k", h=4)[:, :, 0:nk]
                dst = prob[:, u % 2, :, 0:nk]
                link(dve.scalar_tensor_tensor(out=dst, in0=src, scalar=scale, in1=spread(mask, 1, 4),
                                              op0=ALU.mult, op1=ALU.add))
                nm = stat[:, 8 + 8 * (u % 2):12 + 8 * (u % 2)]
                link(dve.tensor_reduce(nm, dst, AX, ALU.max))
                dve.tensor_scalar(nm, nm, -1.0, None, ALU.mult).then_inc(score_max, 1)

            def output(u, tt, gate):
                dve.wait_ge(att_out, u + 1)
                rs = stat[:, 32 + 4 * (u % 2):36 + 4 * (u % 2)]
                link(dve.reciprocal(rs, stat[:, 12 + 8 * (u % 2):16 + 8 * (u % 2)]))
                src = bank(6)[:, 0:256].rearrange("p (h d) -> p h d", h=4)
                if gate is None:
                    tt_(o_tm[:, tt, :, :], src, spread(rs, 2, HD), ALU.mult).then_inc(o_added, 1)
                    return
                link(tt_(rs, rs, gate, ALU.mult))
                link(tt_(att_tmp, src, spread(rs, 2, HD), ALU.mult))
                tt_(o_tm[:, tt, :, :], o_tm[:, tt, :, :], att_tmp, ALU.add).then_inc(o_added, 1)

            def pad_queries(b, sem_):
                src = bank(b).rearrange("p (a t) -> p a t", a=2)
                dve.tensor_copy(qpad[0:64, :, 0, :], src[0:64])
                dve.tensor_copy(qpad[64:128, :, 1, :], src[64:128]).then_inc(sem_, 1)

            def nsa(l):
                dve.wait_ge(rw_out, l + 1)
                dve.wait_ge(fill_copied, 10 * (l + 1))
                if l == 0:
                    dve.wait_ge(trig_done, 1)
                for tt in range(TT):
                    dve.tensor_copy(kc_dup[:, tt, :, :, :], spread(
                        ptm[:, tt, TM_KC:TM_KC + 256].rearrange("p (a b) -> p a b", a=4), 2, 2))
                heads = ptm[:, :, 0:512].rearrange("p t (h d) -> p t h d", d=HD)

                def table(s):
                    return spread(trig[:, s, 0:2, :], 2, 8)

                rope(heads[:, :, :, 0:8], heads[:, :, :, 8:16], table(0), table(1),
                     rope_a, rope_b, rope_c, rope_d).then_inc(roped, 1)
                dve.memset(qpad[64:128, :, 0, :], 0.0)
                dve.memset(qpad[0:64, :, 1, :], 0.0)
                dve.memset(kc2[64:128, :, :, SEQ - 1:SEQ], 0.0)
                dve.wait_ge(nsa_turned, l + 1)
                for j in range(2):
                    src = bank(2 + j).rearrange("p (g t) -> p g t", g=2)
                    dve.tensor_copy(kc2[0:64, j, :, :], src[0:64])
                    m = dve.tensor_copy(kc2[64:128, j, :, 0:SEQ - 1], src[64:128, :, 1:SEQ])
                m.then_inc(kc_copied, 1)
                pad_queries(0, q_padded)
                dve.wait_ge(cmp_kv, l + 1)
                dve.tensor_copy(v_cmp[0:N_CMP, :, :], bank(6)[0:N_CMP, 128:256].rearrange("p (a b) -> p a b", a=2))
                link(dve.tensor_copy(k_cmp[0:N_CMP, :, :],
                                     bank(6)[0:N_CMP, 0:128].rearrange("p (a b) -> p a b", a=2)))

                def ctable(s):
                    return spread(trig[0:N_CMP, s, 2, :], 1, 2)

                rope(k_cmp[0:N_CMP, :, 0:8], k_cmp[0:N_CMP, :, 8:16], ctable(0), ctable(1),
                     rope_a[0:N_CMP, 0, 0:2, :], rope_b[0:N_CMP, 0, 0:2, :], rope_c[0:N_CMP, 0, 0:2, :],
                     rope_d[0:N_CMP, 0, 0:2, :]).then_inc(cmp_kv_copied, 1)
                dve.wait_ge(cmp_kturned, l + 1)
                dve.tensor_copy(kcT, bank(6)[:, 0:N_CMP]).then_inc(cmp_kcopied, 1)
                dve.wait_ge(cmp_scored, l + 1)
                src = bank(5)[:, 0:8 * N_CMP].rearrange("p (t h n) -> p t h n", t=2, h=4)
                add = spread(conc("cmp_add").rearrange("p (t n) -> p t n", t=2), 2, 4)
                keep = spread(conc("cmp_keep").rearrange("p (t n) -> p t n", t=2), 2, 4)
                for tt in range(TT):
                    m = dve.scalar_tensor_tensor(out=cprob[:, tt], in0=src[:, tt], scalar=0.125, in1=add[:, tt],
                                                 op0=ALU.mult, op1=ALU.add)
                link(m)
                mx = stat[:, 24:32].rearrange("p (t h) -> p t h", t=2)
                link(dve.tensor_reduce(mx, cprob, AX, ALU.max))
                tt_(cprob, cprob, spread(mx, 3, N_CMP), ALU.subtract).then_inc(cmp_shifted, 1)
                shifted(6 * l, 0, P, conc("causal", 0, P))
                dve.wait_ge(cmp_exp, l + 1)
                link(dve.tensor_reduce(mx, cprob, AX, ALU.add))
                tt_(cprob, cprob, keep, ALU.mult).then_inc(cmp_prob, 1)
                dve.wait_ge(gates_on, l + 1)
                gt = gates.rearrange("p t (h a) -> p t h a", a=3)
                link(dve.reciprocal(mx, mx))
                link(tt_(mx, mx, gt[:, :, :, 0], ALU.mult))
                dve.wait_ge(cmp_out, l + 1)
                src = bank(6).rearrange("p (t h d) -> p t h d", t=2, h=4)
                tt_(o_tm, src, spread(mx, 3, HD), ALU.mult).then_inc(cmp_added, 1)
                dve.wait_ge(cmp_added, l + 1)
                for n in range(4):
                    if n < 3:
                        t2 = (n + 1) % 2
                        shifted(6 * l + n + 1, t2, P * (t2 + 1), conc("causal", 256 * t2, P * (t2 + 1)))
                    output(6 * l + n, n % 2, gt[:, n % 2, :, 1 + n // 2])

            def pool(l):
                dve.wait_ge(pool_d, l + 1)
                dve.tensor_copy(poolT.rearrange("p a b -> p (a b)"), bank(5)).then_inc(pool_dc, 1)

            def gla(l):
                dve.wait_ge(gl_pe, 6 * l + 1)
                link(dve.tensor_scalar(gl_z, bank(0)[:, 0:256], parc(l, "ab"), None, ALU.add))
                dve.scalar_tensor_tensor(out=gl_e, in0=gl_z, scalar=-1.0, in1=gl_z,
                                         op0=ALU.mult, op1=ALU.max).then_inc(gl_dve, 1)
                link(dve.tensor_scalar(gl_z, gl_z, 0.0, None, ALU.min))
                dve.wait_ge(gl_act, 3 * l + 1)
                link(tt_(gl_z, gl_z, gl_e, ALU.subtract))
                link(dve.tensor_tensor_scan(gl_b, conc("reset16"), gl_z, 0.0, ALU.mult, ALU.add))
                b = gl_b.rearrange("p (n t) -> p n t", t=C_GL)
                last = b[:, :, C_GL - 1:C_GL].broadcast_to([P, N_GL, C_GL])
                tt_(gl_ke.rearrange("p (n t) -> p n t", t=C_GL), last, b, ALU.subtract).then_inc(gl_dve, 1)
                dve.memset(gl_q, 0.0)
                link(dve.memset(gl_s[:, 0, :], 0.0))
                dve.wait_ge(gl_act, 3 * l + 2)
                for h in range(4):
                    r = slice(32 * h, 32 * h + 32)
                    dve.scalar_tensor_tensor(out=gl_q[r, h, :], in0=pfm[r, FM_GQ, :], scalar=32.0 ** -0.5,
                                             in1=gl_eq[r, :], op0=ALU.mult, op1=ALU.mult)
                tt_(gl_ek, gl_ek, pfm[:, FM_GK, :], ALU.mult)
                tt_(gl_ke, gl_ke, pfm[:, FM_GK, :], ALU.mult).then_inc(gl_dve, 1)
                dve.wait_ge(gl_pe, 6 * l + 3)
                for tt in range(TT):
                    m = tt_(gl_k8[:, tt, :, :], spread(bank(3)[:, tt * P:(tt + 1) * P], 1, 8),
                            spread(conc("chunk16"), 2, P), ALU.mult)
                m.then_inc(gl_dve, 1)
                for tt in range(TT):
                    tt_(gl_att[:, tt, :, :], bank(1 + tt).rearrange("p (h t) -> p h t", h=4),
                        spread(conc("gl_causal"), 1, 4), ALU.mult)
                dve.wait_ge(gl_pe, 6 * l + 4)
                for n in range(N_GL - 1):
                    m = dve.scalar_tensor_tensor(out=gl_s[:, n + 1, :], in0=gl_s[:, n, :], scalar=gl_dl[:, n:n + 1],
                                                 in1=bank(4 + n // 8)[:, (n % 8) * HD:(n % 8 + 1) * HD],
                                                 op0=ALU.mult, op1=ALU.add)
                    if n < N_GL - 2:
                        link(m)
                m.then_inc(gl_dve, 1)
                dve.wait_ge(gl_pe, 6 * l + 5)
                link(dve.tensor_copy(gl_o.rearrange("p a b -> p (a b)"), bank(6)))
                tt_(gl_sq, gl_o, gl_o, ALU.mult).then_inc(gl_dve, 1)
                dve.wait_ge(gl_pe, 6 * l + 6)
                rooted(gl_r, dve.tensor_scalar(gl_r.rearrange("p a b -> p (a b)"), bank(0), EPS, None, ALU.add))
                link(tt_(gl_o, gl_o, gl_r, ALU.mult))
                dve.wait_ge(gl_act, 3 * l + 3)
                dve.scalar_tensor_tensor(out=oT[:, 6:8, :], in0=gl_o, scalar=parc(l, "gnorm"), in1=gl_og,
                                         op0=ALU.mult, op1=ALU.mult).then_inc(gl_dve, 1)

            def rwkv(l):
                dve.wait_ge(proj_act, 4 * l + 2)
                d = rw_kr.rearrange("p a b c t -> p (a b c) t")
                for part in (slice(FM_LR, FM_LR + 1), slice(0, FM_LR)):
                    tt_(d[:, part, 1:SEQ], pfm[:, part, 0:SEQ - 1], pfm[:, part, 1:SEQ], ALU.subtract)
                    link(dve.tensor_scalar(d[:, part, 0:1], pfm[:, part, 0:1], -1.0, None, ALU.mult))
                    for cc in range(part.start, part.stop):
                        m = dve.scalar_tensor_tensor(out=pfm[:, cc, :], in0=d[:, cc, :],
                                                     scalar=parc(l, "mu", cc), in1=pfm[:, cc, :],
                                                     op0=ALU.mult, op1=ALU.add)
                    if part.start:
                        m.then_inc(rw_dve, 1)
                    else:
                        link(m)
                r, k, v = (pfm[:, a:a + 2, :] for a in (FM_R, FM_K, FM_V))
                for s, t in ((rw_kr[64:128, :, 0, :, :], 0), (rw_kr[0:64, :, 1, :, :], 0)):
                    dve.memset(s, 0.0)
                for t in (rw_km, rw_bm):
                    dve.memset(t[64:128, :, 0, :, :], 0.0)
                    dve.memset(t[0:64, :, 1, :, :], 0.0)
                link(dve.memset(rw_s[:, 0, :, :], 0.0))
                for hp in range(2):
                    link(dve.tensor_scalar(rw_kk[:, hp, :], k[:, hp, :], parc(l, "k_k", hp), None, ALU.mult))
                tt_(rw_sq, rw_kk, rw_kk, ALU.mult).then_inc(rw_dve, 1)
                dve.wait_ge(rw_pe, 7 * l + 2)
                nrm = rw_bt
                rooted(nrm, dve.tensor_scalar(nrm.rearrange("p a b -> p (a b)"), bank(5), 64.0, 1e-24,
                                              ALU.mult, ALU.max))
                link(tt_(rw_kk, rw_kk, nrm, ALU.mult))
                dve.wait_ge(rw_act, 8 * l + 2)
                link(dve.tensor_scalar(rw_lw, rw_lw, -float(np.exp(-0.5)), None, ALU.mult))
                link(dve.tensor_tensor_scan(rw_cl.rearrange("p a b -> p (a b)"), conc("reset64"),
                                            rw_lw.rearrange("p a b -> p (a b)"), 0.0, ALU.mult, ALU.add))
                tt_(rw_clm, rw_cl, rw_lw, ALU.subtract).then_inc(rw_dve, 1)
                if l == 0:
                    dve.tensor_copy(v_first[:, :, :], v)
                else:
                    link(tt_(rw_bonus, v_first[:, :, :], v, ALU.subtract))
                    link(tt_(rw_bonus, rw_bonus, rw_vg, ALU.mult))
                    link(tt_(v, v, rw_bonus, ALU.add))
                for hp in range(2):
                    link(dve.tensor_scalar(rw_k2[:, hp, :], rw_a[:, hp, :], -1.0, parc(l, "k_a", hp),
                                           ALU.add, ALU.mult))
                link(dve.scalar_tensor_tensor(out=rw_k2, in0=rw_k2, scalar=1.0, in1=k, op0=ALU.add, op1=ALU.mult))
                link(tt_(rw_a, rw_kk, rw_a, ALU.mult))
                dve.wait_ge(rw_act, 8 * l + 3)
                for h2 in range(2):
                    rr = slice(64 * h2, 64 * h2 + 64)
                    tt_(rw_kr[rr, :, h2, 0, :], rw_kk[rr], rw_clm[rr], ALU.mult)
                    tt_(rw_kr[rr, :, h2, 1, :], r[rr], rw_ep[rr], ALU.mult)
                tt_(rw_bt, rw_a, rw_em, ALU.mult)
                tt_(rw_kt, rw_k2, rw_em, ALU.mult)
                for hp in range(2):
                    m = dve.scalar_tensor_tensor(out=rw_rk[:, hp, :], in0=r[:, hp, :], scalar=parc(l, "r_k", hp),
                                                 in1=rw_k2[:, hp, :], op0=ALU.mult, op1=ALU.mult)
                m.then_inc(rw_dve, 1)
                for which, dst in ((0, rw_ab), (1, rw_ak)):
                    dve.wait_ge(rw_pe, 7 * l + 3 + which)
                    if which == 1:
                        dve.wait_ge(rw_act, 8 * l + 5)
                    mask = conc("rw_k" if which else "rw_b").rearrange("p (a t) -> p a t", a=2)
                    for tt in range(TT):
                        for hp in range(2):
                            m = tt_(dst[:, tt, hp], bank(2 * tt + hp).rearrange("p (a b t) -> p a b t", a=2, b=2),
                                    spread(mask, 1, 2), ALU.mult)
                    m.then_inc(rw_dve, 1)
                dve.tensor_copy(rw_x, spread(ident, 1, 8))
                dve.memset(rw_z, 0.0)
                dve.memset(rw_u, 0.0)
                dve.tensor_copy(rw_xt, spread(ident, 1, 8)).then_inc(inv_dve, 1)
                for j in range(6):
                    mask = spread(conc("level", j * P, P), 1, 4)
                    for g in range(2):
                        part = slice(4 * g, 4 * g + 4)
                        dve.wait_ge(inv_pe, 24 * l + 4 * j + 1 + g)
                        tt_(rw_t1[:, part], bank(g).rearrange("p (q t) -> p q t", q=4), mask, ALU.mult)\
                            .then_inc(inv_dve, 1)
                    for g in range(2):
                        part = slice(4 * g, 4 * g + 4)
                        dve.wait_ge(inv_pe, 24 * l + 4 * j + 3 + g)
                        tt_(rw_x[:, part], rw_x[:, part], bank(2 + g).rearrange("p (q t) -> p q t", q=4), ALU.add)
                        tt_(rw_xt[:, part], rw_xt[:, part], bank(6 + g).rearrange("p (q t) -> p q t", q=4),
                            ALU.add).then_inc(inv_dve, 1)
                for ch in range(4):
                    rows = slice(64 * (ch % 2), 64 * (ch % 2) + 64)
                    dve.wait_ge(seq_pe, 16 * l + 4 * ch + 1)
                    dve.tensor_copy(rw_z[rows, :], bank(0)[rows, 0:256]).then_inc(seq_dve, 1)
                    dve.wait_ge(seq_pe, 16 * l + 4 * ch + 2)
                    dve.tensor_copy(rw_u[rows, :], bank(1)[rows, 0:256]).then_inc(seq_dve, 1)
                    dve.wait_ge(seq_pe, 16 * l + 4 * ch + 3)
                    new = rw_s[:, (ch + 1) % 2, :, :]
                    for h2 in range(2):
                        rr = slice(64 * h2, 64 * h2 + 64)
                        src = bank(3)[rr, 0:256].rearrange("p (a b) -> p a b", a=2)[:, :, h2 * HD:(h2 + 1) * HD]
                        m = tt_(new[rr], rw_s[rr, ch % 2, :, :], src, ALU.add)
                    link(m)
                    dec = rw_ep[:, :, ch * C_RW + C_RW - 1:ch * C_RW + C_RW].broadcast_to([P, 2, HD])
                    tt_(new, new, dec, ALU.mult).then_inc(seq_dve, 1)
                dve.wait_ge(rw_act, 8 * l + 8)
                link(tt_(rw_yc, rw_y, rw_r, ALU.subtract))
                tt_(rw_y2, rw_yc, rw_yc, ALU.mult).then_inc(rw_dve, 1)
                dve.wait_ge(rw_pe, 7 * l + 7)
                rooted(rw_r, dve.tensor_scalar(rw_r.rearrange("p a b -> p (a b)"), bank(1), GN_EPS, None, ALU.add))
                link(tt_(rw_yc, rw_yc, rw_r, ALU.mult))
                link(dve.scalar_tensor_tensor(out=rw_bonus, in0=rw_bonus, scalar=64.0, in1=v,
                                              op0=ALU.mult, op1=ALU.mult))
                for hp in range(2):
                    m = dve.scalar_tensor_tensor(out=rw_yc[:, hp, :], in0=rw_yc[:, hp, :],
                                                 scalar=parc(l, "ln", hp), in1=rw_bonus[:, hp, :],
                                                 op0=ALU.mult, op1=ALU.add)
                link(m)
                tt_(oT[:, 4:6, :], rw_yc, rw_g, ALU.mult).then_inc(rw_out, 1)

            def merge(l):
                def octet_low(n):
                    at, col = merge_octet(l, n)
                    dve.wait_ge(oct_high, 16 * l + n + 1)
                    tt_(octet_part(n, 1), ring[:, at % RING, col:col + OCT], octet_part(n, 0),
                        ALU.subtract).then_inc(oct_split, 1)

                for j in range(N_EARLY):
                    dve.wait_ge(early_sig, N_EARLY * l + j + 1)
                    dve.wait_ge(branch_done, N_EARLY * l + j + 1)
                    t = mtmp if j % 2 else mtmp2
                    link(tt_(t, early[:, j], bank(2 * (1 - j % 2), 2).rearrange("p (i t) -> p i t", i=N_BR), ALU.mult))
                    dve.tensor_reduce(merged[:, j, :], t.rearrange("p i t -> p t i"), AX, ALU.add)\
                       .then_inc(branch_used, 1)
                    if j == 3:
                        dve.wait_ge(hm_high, l + 1)
                        tt_(h_parts[:, 1, :, :], hT[:, :, :], h_parts[:, 0, :, :], ALU.subtract).then_inc(hm_split, 1)
                for n in range(4):
                    octet_low(n)
                for n in range(N_BR * (KC - N_EARLY)):
                    j, i = n // N_BR, n % N_BR
                    dve.wait_ge(gate_sig, 8 * l + n + 1)
                    src = bank(4 * (1 - j) + i)[:, 256:512]
                    if i == 0:
                        tt_(merged[:, N_EARLY + j, :], sig[:, i, :], src, ALU.mult).then_inc(gate_used, 1)
                    else:
                        if i == 1:
                            dve.wait_ge(gate_used, 8 * l + n)
                        link(tt_(mtmp[:, i, :], sig[:, i, :], src, ALU.mult))
                        tt_(merged[:, N_EARLY + j, :], merged[:, N_EARLY + j, :], mtmp[:, i, :], ALU.add)\
                            .then_inc(gate_used, 1)
                    if n < 6:
                        octet_low(n + 4)
                for kc in range(KC):
                    dve.wait_ge(merged_high, KC * l + kc + 1)
                    tt_(h_parts[:, 1, kc, :], merged[:, kc, :], h_parts[:, 0, kc, :],
                        ALU.subtract).then_inc(merged_split, 1)
                for n in range(10, 16):
                    octet_low(n)
                add_to_x(4, merged_out, 2 * l, (x_tile, x_tile))

            def add_to_x(b, sem_, n, done, step=1):
                for tt in range(TT):
                    dve.wait_ge(sem_, n + step * (tt + 1))
                    tt_(x[:, tt, :], x[:, tt, :], bank(b + 2 * tt, 2), ALU.add).then_inc(done[tt], 1)

            def cross(l):
                dve.wait_ge(x_turned, KC // 2 * (3 + 3 * l))
                dve.memset(qpad[64:128, :, 0, :], 0.0)
                dve.memset(qpad[0:64, :, 1, :], 0.0)
                dve.wait_ge(caq_done, l + 1)
                pad_queries(4, caq_padded)
                for tt in range(TT):
                    u = 6 * l + 4 + tt
                    dve.wait_ge(scored, u + 1)
                    nm = stat[:, 8 + 8 * (u % 2):12 + 8 * (u % 2)]
                    link(dve.tensor_reduce(nm, bank(2 * (u % 2), 2).rearrange("p (h k) -> p h k", h=4), AX, ALU.max))
                    dve.tensor_scalar(nm, nm, -0.125, None, ALU.mult).then_inc(score_max, 1)
                for tt in range(TT):
                    output(6 * l + 4 + tt, tt, None)
                if l == 0:
                    split(0)
                add_to_x(0, cao_done, 2 * l, (x_tile, x_tile))

            def hiddens(at, c, up):
                dve.wait_ge(down_split, up + (c + 1))
                tt_(down_w[:, at % 2, 1, :], ring[:, at % RING, 2 * OCT:3 * OCT], down_w[:, at % 2, 0, :],
                    ALU.subtract)
                dve.wait_ge(silu_done, up + (c + 1))
                t = product[:, at % 2, :]
                b = bank(4 + at % 2)[:, 256:512]
                tt_(t, silu[:, at % 2, :], b, ALU.mult)
                ins = tt_(hid[:, at % 2, 0, :], silu[:, at % 2, :], b, ALU.mult)
                ins.then_inc(slab_read, 1)
                dve.wait_ge(slab_read, up + (at + 1))
                tt_(hid[:, at % 2, 1, :], t, hid[:, at % 2, 0, :], ALU.subtract).then_inc(hid_ready, 1)

            def ffn(l):
                for kc in range(KC):
                    dve.wait_ge(h_ready, KC * (3 + 3 * l) + kc + 1)
                    dve.wait_ge(h_high, kc + 1)
                    tt_(h_parts[:, 1, kc, :], hT[:, kc, :], h_parts[:, 0, kc, :], ALU.subtract)\
                        .then_inc(h_split, 1)
                for f in range(FC):
                    if f + 1 < FC:
                        split(f + 1)
                    hiddens(LAYER_SLABS + f, f, 0)
                add_to_x(0, down_used, FC, (x_tile, x_added), 0)

            def moe(l):
                dve.wait_ge(routed, 1)
                link(dve.tensor_copy(logit, bank(6)[:, 0:16].rearrange("p (t e) -> p t e", t=2)))
                for tt in range(TT):
                    link(dve.max(top[:, tt, :], logit[:, tt, :]))
                    link(dve.max_index(idx[:, :], top[:, tt, :], logit[:, tt, :]))
                    link(dve.tensor_copy(topi[:, tt, :], idx[:, :]))
                    one, two = (topi[:, tt, s:s + 1].broadcast_to([P, 8]) for s in (0, 1))
                    tt_(picked[:, tt, :], conc("iota", 0, 8), one, ALU.is_equal)
                    link(tt_(pick[:, tt, :], conc("iota", 0, 8), two, ALU.is_equal))
                    link(tt_(picked[:, tt, :], picked[:, tt, :], pick[:, tt, :], ALU.add))
                big_ = top[:, :, 0:1].broadcast_to([P, TT, 8])
                tt_(logit, logit, big_, ALU.subtract).then_inc(top_diff, 1)
                dve.wait_ge(top_exp, 1)
                link(tt_(combine, picked, pick, ALU.mult))
                link(dve.tensor_reduce(stat[:, 44:46], combine, AX, ALU.add))
                link(dve.reciprocal(stat[:, 44:46], stat[:, 44:46]))
                link(tt_(combine, combine, stat[:, 44:46].unsqueeze(2).broadcast_to([P, TT, 8]), ALU.mult))
                dve.wait_ge(placed, 1)
                dve.tensor_copy(load_of[:, :], bank(7)[:, 16:24]).then_inc(load_ready, 1)
                dve.tensor_copy(place, bank(7)[:, 0:16].rearrange("p (t e) -> p t e", t=2))
                link(dve.tensor_scalar(few, bank(7)[:, 16:24], float(P), None, ALU.is_le))
                link(tt_(comb_few, combine, spread(few, 1, TT), ALU.mult))
                link(tt_(comb_many, combine, comb_few, ALU.subtract))
                for e in range(N_EXP + 1):
                    if e < N_EXP:
                        for tt in range(TT):
                            pl = place[:, tt, e:e + 1]
                            if e >= 2:
                                dve.wait_ge(gathered, e - 1)
                            m = dve.tensor_scalar(sel[:, e % 2, tt, :], conc("iota"), pl,
                                                  picked[:, tt, e:e + 1], ALU.is_equal, ALU.mult)
                        m.then_inc(sel_ready, 1)
                    if e >= 1:
                        dve.wait_ge(gathered, e)
                        tt_(h_exp[:, e - 1], bank(2 * ((e - 1) % 2), 2).rearrange("p (k t) -> p k t", k=KC),
                            spread(parc(l, "norm_ffn", 0, 8), 2, P), ALU.mult)
                        dve.tensor_copy(w_slot[:, e - 1:e], bank(6 + (e - 1) % 2)[:, 256:257])
                        dve.tensor_copy(selT[:, e - 1], bank(6 + (e - 1) % 2)[:, 0:256]
                                        .rearrange("p (t s) -> p t s", t=2)).then_inc(gathered_c, 1)
                s0 = FIRST_SLAB[1] + LAYER_SLABS
                with dve.Fori(0, N_EXP // 2) as i:
                    for half in range(2):
                        for f in range(FC):
                            hiddens(s0 + FC * half + f, FC * (1 + half) + f, i * (2 * FC))
                        dve.wait_ge(down_used, i * (2 * FC) + FC * (2 + half))
                        dve.wait_ge(x_added, i * 2 + (1 + half))
                        mine = bass.ds(i * 2 + half, 1)
                        high = y_high[:, mine, :].rearrange("p e d -> p (e d)")
                        dve.tensor_scalar(high, bank(0, 2), w_slot[:, mine], None, ALU.mult).then_inc(y_ready, 1)
                        dve.wait_ge(y_ready, i * 2 + (1 + half))
                        dve.scalar_tensor_tensor(out=y_low[:, mine, :].rearrange("p e d -> p (e d)"),
                                                 in0=bank(0, 2), scalar=w_slot[:, mine], in1=high,
                                                 op0=ALU.mult, op1=ALU.subtract)
                        for tt in range(TT):
                            w = comb_many[:, tt, bass.ds(i * 2 + half, 1)]
                            m = dve.scalar_tensor_tensor(out=x[:, tt, :], in0=bank(2 * tt, 2), scalar=w,
                                                         in1=x[:, tt, :], op0=ALU.mult, op1=ALU.add)
                        m.then_inc(x_added, 1)
                add_to_x(4, scattered, 0, (x_moe, x_moe))

            def final(l):
                for tt in range(TT):
                    dve.wait_ge(fin_sq, tt + 1)
                    rstd_of(stat[:, tt:tt + 1], 1.0 / D, EPS)
                    dve.wait_ge(gain_loaded, 16)
                    dve.scalar_tensor_tensor(out=fin_x[:, tt, :], in0=x[:, tt, :], scalar=stat[:, tt:tt + 1],
                                             in1=fin_gain, op0=ALU.mult, op1=ALU.mult).then_inc(fin_ready, 1)

            steps = dict(norm=norm, project=project, nsa=nsa, pool=pool, gla=gla, rwkv=rwkv, merge=merge,
                         cross=cross, ffn=ffn, moe=moe, final=final)
            dve.wait_ge(par_loaded, 32)
            dve.wait_ge(mem_loaded, 16)
            for step, l in PLAN:
                steps[step](l)


def constants():
    con = np.zeros((P, N_CON), np.float32)

    def put(name, a):
        a = np.asarray(a, np.float64).reshape(P, -1)
        assert a.shape[1] == CON_COLS[name], (name, a.shape)
        con[:, CON[name]:CON[name] + a.shape[1]] = a

    p = np.arange(P)
    t = np.arange(P)
    s256 = np.arange(256)
    put("ident", np.eye(P))
    q = p[:, None] + P * np.arange(2)[None, :]
    put("causal", np.where(s256[None, None, :] <= q[:, :, None], 0.0, NEG))
    end = np.arange(N_CMP) * CMP_STRIDE + CMP_LEN - 1
    ok = end[None, None, :] <= q[:, :, None]
    put("cmp_add", np.where(ok, 0.0, NEG))
    put("cmp_keep", ok)
    levels = []
    for j in range(6):
        b = 1 << j
        row, col = p[:, None], t[None, :]
        levels.append((row // (2 * b) == col // (2 * b)) & (row % (2 * b) >= b) & (col % (2 * b) < b))
    put("level", np.stack(levels, 1))
    s, tc = p[:, None], t[None, :]
    same = s // C_RW == tc // C_RW
    both = np.stack([same & (s < tc), same & (s <= tc)], 1).astype(float)
    put("rw_b", -both)
    put("rw_k", both)
    put("gl_causal", (s // C_GL == tc // C_GL) & (s <= tc))
    tab = []
    for w in (2, 4, 8, 16):
        tq, sq = np.arange(256)[None, :], np.arange(256)[:, None]
        m = ((sq <= tq) & (sq > tq - w)) / np.minimum(tq + 1, w) - (sq == tq)
        tab += [m[0:P, :], m[P:, P:]]
    put("pool", np.concatenate(tab, 1))
    put("reset64", np.tile((np.arange(512) % C_RW != 0)[None], (P, 1)))
    put("reset16", np.tile((np.arange(256) % C_GL != 0)[None], (P, 1)))
    put("ones", (p[:, None] // 64 == t[None, :] // 64) / 64.0)
    put("chunk16", p[:, None] // C_GL == np.arange(8)[None, :])
    inv = (np.float32(500000.0) ** (-np.arange(0, 16, 2, dtype=np.float32) / np.float32(16))).astype(np.float32)
    put("freq", np.tile(inv[None], (P, 1)))
    put("iota", np.tile(np.arange(P)[None], (P, 1)))
    put("before", p[:, None] < t[None, :])
    put("every", np.ones((P, P)))
    return con


def lay_out(a):
    f = np.float32

    def blocks(w):
        return w.reshape(-1, P, w.shape[1]).transpose(1, 0, 2).reshape(P, -1)

    stream = np.zeros((N_SLABS, P, SLAB), f)
    params = np.zeros((DEPTH, P, N_PAR), f)
    mixw = np.zeros((DEPTH, P, N_MIX), f)
    nsa, rw, gl = 0, 1292, 2188
    for l in range(DEPTH):
        w = a["w_in"][l]
        q = w[:, 0:256].reshape(D, 2, 2, HD).transpose(0, 2, 1, 3).reshape(D, 256)
        tm = np.concatenate([q, w[:, 512:640], w[:, 768:896], w[:, 256:512], w[:, 640:768],
                             w[:, 896:1024], w[:, 1036:1292], w[:, gl + 256:gl + 512]], 1)
        s0 = FIRST_SLAB[l]
        for s in range(N_TM):
            stream[s0 + FM_FIRST + s] = blocks(tm[:, s * 384:(s + 1) * 384])
        misc = np.zeros((D, P), f)
        misc[:, 0:16] = w[:, gl + 512:gl + 528]
        if l:
            misc[:, MISC_V1:MISC_V1 + 32] = a["rwkv_v1"][l - 1]
        misc[:, MISC_GATES:MISC_GATES + 12] = w[:, 1024:1036]
        fm = np.concatenate([w[:, rw:rw + 896], misc, w[:, gl:gl + 256], w[:, gl + 528:gl + 784]], 1)
        for ch in range(12):
            slab = stream[s0 + (ch // 3 if ch < 9 else FM_FIRST + N_TM)]
            slab[:, (ch % 3) * OCT:(ch % 3 + 1) * OCT] = blocks(fm[:, ch * P:(ch + 1) * P])

        def put(o, block):
            stream[s0 + N_TM + N_FM + o // 3][:, (o % 3) * OCT:(o % 3 + 1) * OCT] = block

        for j in range(2):
            w1 = a["nsa_cmp_w1"][l, j].reshape(2 * D, P)
            for half in range(2):
                put(O_CMP + 2 * j + half, blocks(w1[half * D:(half + 1) * D]))
        for j in range(KC):
            o = O_MERGE + j if j < N_EARLY else O_MERGE + N_EARLY + (j - N_EARLY) * (N_BR + 1)
            put(o, blocks(a["w_branch"][l, :, :, j * P:(j + 1) * P].reshape(D, P)))
            for i in range(N_BR):
                put(O_GATE + N_BR * j + i if j < N_EARLY else o + 1 + i,
                    blocks(a["w_gate"][l, i][:, j * P:(j + 1) * P]))
            put(O_OUT + j, a["w_out"][l, j * P:(j + 1) * P])
        kv = a["w_ca_kv"][l]
        for cc in range(2):
            put(O_KV + cc, blocks(kv[:, cc * P:(cc + 1) * P]))
            put(O_KV + 2 + cc, blocks(kv[cc * 512:(cc + 1) * 512, 256:512]))
            put(O_CQ + cc, blocks(a["w_ca_q"][l][:, cc * P:(cc + 1) * P]))
            put(O_CO + cc, a["w_ca_o"][l, cc * P:(cc + 1) * P])

        def small(name, v):
            v = v.reshape(-1, P).T
            params[l][:, PAR[name]:PAR[name] + v.shape[1]] = v

        small("norm_mix", a["norm_mix"][l])
        small("norm_ca", a["norm_ca"][l])
        small("norm_ffn", a["norm_ffn"][l])
        small("mem_norm", a["mem_norm"])
        small("b_gate", a["b_gate"][l])
        small("pool_scale", a["pool_scale"][l])
        small("mu", a["rwkv_mu"][l])
        for name, key in (("w0", "rwkv_w0"), ("a0", "rwkv_a0"), ("k_k", "rwkv_k_k"), ("k_a", "rwkv_k_a"),
                          ("r_k", "rwkv_r_k"), ("ln", "rwkv_ln"), ("ab", "gla_ab")):
            small(name, a[key][l])
        if l:
            small("v0", a["rwkv_v0"][l - 1])
            params[l][:, PAR["router"]:PAR["router"] + 64] = blocks(a["moe_router"][0])
        small("gnorm", np.concatenate([a["gla_norm"][l]] * 2))
        small("pe", a["nsa_cmp_pe"][l])

        def mix(name, rows, v, at=0):
            mixw[l][rows, MIX[name] + at:MIX[name] + at + v.shape[1]] = v

        mix("w2", slice(0, 32), a["rwkv_w2"][l])
        mix("a2", slice(32, 64), a["rwkv_a2"][l])
        mix("g2", slice(64, 128), a["rwkv_g2"][l])
        if l:
            mix("v2", slice(MISC_V1, MISC_V1 + 32), a["rwkv_v2"][l - 1])
        mix("gla_a2", slice(0, 16), a["gla_a2"][l])
        for g in range(4):
            mix("pool", slice(64 * (g % 2), 64 * (g % 2) + 64), a["pool_w"][l, g], P * (g // 2) + 64 * (g % 2))
        for j in range(2):
            mix("cmp", slice(0, P), a["nsa_cmp_w2"][l, j], j * HD)

    def feed(s0, wg, wu, wd):
        dst = stream[s0:s0 + FC].reshape(FC, P, 3, KC, P)
        dst[:, :, 0] = wg.reshape(KC, P, FC, P).transpose(2, 1, 0, 3)
        dst[:, :, 1] = wu.reshape(KC, P, FC, P).transpose(2, 1, 0, 3)
        dst[:, :, 2] = wd.reshape(FC, P, KC, P)

    feed(LAYER_SLABS, a["ffn_w_gate"][0], a["ffn_w_up"][0], a["ffn_w_down"][0])
    for e in range(N_EXP):
        feed(FIRST_SLAB[1] + LAYER_SLABS + FC * e, a["moe_w_gate"][0, e], a["moe_w_up"][0, e],
             a["moe_w_down"][0, e])
    pos = a["positions"].reshape(SEQ)
    positions = np.zeros((P, 3), pos.dtype)
    positions[:, 0:2] = pos.reshape(TT, P).T
    positions[0:N_CMP, 2] = pos[CMP_LEN - 1::CMP_STRIDE]
    return {
        "stream": stream, "params": params, "mixw": mixw, "consts": constants(),
        "x_in": np.ascontiguousarray(a["x"].reshape(TT, P, D).transpose(1, 0, 2)),
        "mem_in": np.ascontiguousarray(a["mem"].reshape(TT, P, D).transpose(1, 0, 2)),
        "pos_in": positions,
        "gain_in": np.ascontiguousarray(np.broadcast_to(a["norm_final"][None], (P, D))),
    }


def kernel(**inputs):
    import concourse.bacc as bacc
    from concourse.bass_utils import run_bass_kernel_spmd as run

    arrays = lay_out({k: np.asarray(v) for k, v in inputs.items()})
    nc = bacc.Bacc("TRN2", target_bir_lowering=False, num_devices=1)
    args = [nc.dram_tensor(n, list(v.shape), mybir.dt.from_np(v.dtype), kind="ExternalInput").ap()
            for n, v in arrays.items()]
    out = nc.dram_tensor("out", [P, TT, D], F32, kind="ExternalOutput").ap()
    trunk(nc, *args, out)
    r = run(nc, [arrays], core_ids=[0])
    return r.results[0]["out"].transpose(1, 0, 2).reshape(1, SEQ, D)
```
